# Optimizing a Trainium2 kernel written in Bass

```python
import math
import jax
import jax.numpy as jnp
from jax import lax
import numpy as np

D_MODEL = 1024
BATCH = 1
SEQ = 256
DEPTH = 2

CHUNK = 64
Q_BLOCK = 128
N_A_LAYERS = DEPTH // 2
N_B_LAYERS = DEPTH - N_A_LAYERS
DIFF_HEAD_DIM = 64
DIFF_V_DIM = 2 * DIFF_HEAD_DIM
DIFF_HEADS = D_MODEL // DIFF_V_DIM
DIFF_WIDTH = DIFF_HEADS * DIFF_V_DIM
MLA_NOPE_DIM = 128
MLA_ROPE_DIM = 64
MLA_V_DIM = 128
MLA_HEADS = D_MODEL // MLA_V_DIM
MLA_Q_RANK = 384
MLA_KV_RANK = 256
ROPE_BASE = 10000.0
N_EXPERTS = 32
N_GROUPS = 8
TOP_K = 2
EXPERT_FF = 256
NORM_EPS = 1e-5
DEEPNORM_ALPHA = (2 * DEPTH) ** 0.25
DEEPNORM_BETA = (8 * DEPTH) ** -0.25

kernel_name = 'hybrid_diffattn_mla_moe_deepnorm'

def _layernorm(x, g, b):
    xf = x.astype(jnp.float32)
    mu = jnp.mean(xf, axis=-1, keepdims=True)
    var = jnp.mean(jnp.square(xf - mu), axis=-1, keepdims=True)
    return ((xf - mu) * lax.rsqrt(var + NORM_EPS) * g.astype(jnp.float32) + b.astype(jnp.float32)).astype(x.dtype)

def _rmsnorm(x, g):
    xf = x.astype(jnp.float32)
    inv = lax.rsqrt(jnp.mean(jnp.square(xf), axis=-1, keepdims=True) + NORM_EPS)
    return (xf * inv * g.astype(jnp.float32)).astype(x.dtype)

def _rope_tables(seq):
    inv_freq = ROPE_BASE ** (-jnp.arange(0, MLA_ROPE_DIM, 2, dtype=jnp.float32) / MLA_ROPE_DIM)
    ang = jnp.arange(seq, dtype=jnp.float32)[:, None] * inv_freq[None, :]
    return jnp.cos(ang), jnp.sin(ang)

def _rope(x, cos, sin):
    xf = x.astype(jnp.float32)
    x1, x2 = jnp.split(xf, 2, axis=-1)
    return jnp.concatenate([x1 * cos - x2 * sin, x2 * cos + x1 * sin], axis=-1).astype(x.dtype)

def _alibi_slopes(n_heads):
    return 2.0 ** (-8.0 * jnp.arange(1, n_heads + 1, dtype=jnp.float32) / n_heads)

def _chunk_causal_mask(q0, q1):
    q_chunk = jnp.arange(q0, q1) // CHUNK
    k_chunk = jnp.arange(q1) // CHUNK
    return k_chunk[None, :] <= q_chunk[:, None]

def _sweep_query_blocks(seq, block_fn):
    return jnp.concatenate([block_fn(q0, q0 + Q_BLOCK) for q0 in range(0, seq, Q_BLOCK)], axis=1)

def _lambda_init(layer):
    return 0.8 - 0.6 * math.exp(-0.3 * layer)

def _diff_attention(x, w_qkv, lam, subln_g, w_o, lambda_init):
    b, s, _ = x.shape
    q, k, v = jnp.split(x @ w_qkv, 3, axis=-1)
    q = q.reshape(b, s, DIFF_HEADS, 2, DIFF_HEAD_DIM) * (DIFF_HEAD_DIM ** -0.5)
    k = k.reshape(b, s, DIFF_HEADS, 2, DIFF_HEAD_DIM)
    v = v.reshape(b, s, DIFF_HEADS, DIFF_V_DIM)
    lf = lam.astype(jnp.float32)
    lam_full = jnp.exp(jnp.sum(lf[0] * lf[1])) - jnp.exp(jnp.sum(lf[2] * lf[3])) + lambda_init
    slopes = _alibi_slopes(DIFF_HEADS)[:, None, None, None]

    def block(q0, q1):
        logits = jnp.einsum('bqhcd,bkhcd->bhcqk', q[:, q0:q1], k[:, :q1]).astype(jnp.float32)
        dist = jnp.abs(jnp.arange(q0, q1)[:, None] - jnp.arange(q1)[None, :]).astype(jnp.float32)
        logits = jnp.where(_chunk_causal_mask(q0, q1), logits - slopes * dist, -jnp.inf)
        p = jax.nn.softmax(logits, axis=-1)
        a = (p[:, :, 0] - lam_full * p[:, :, 1]).astype(v.dtype)
        return jnp.einsum('bhqk,bkhd->bqhd', a, v[:, :q1])

    o = _sweep_query_blocks(s, block)
    o = _rmsnorm(o, subln_g) * (1.0 - lambda_init)
    return o.reshape(b, s, DIFF_WIDTH) @ w_o

def _mla_shared_kv(x, w_kv_a, kv_norm_g, w_kv_b, cos, sin):
    b, s, _ = x.shape
    kv_a = x @ w_kv_a
    c_kv = _rmsnorm(kv_a[..., :MLA_KV_RANK], kv_norm_g)
    k_rope = _rope(kv_a[..., MLA_KV_RANK:], cos, sin)
    kv = (c_kv @ w_kv_b).reshape(b, s, MLA_HEADS, MLA_NOPE_DIM + MLA_V_DIM)
    return kv[..., :MLA_NOPE_DIM], kv[..., MLA_NOPE_DIM:], k_rope

def _mla_attention(x, w_q_a, q_norm_g, w_q_b, w_o, k_nope, v, k_rope, cos, sin):
    b, s, _ = x.shape
    q = (_rmsnorm(x @ w_q_a, q_norm_g) @ w_q_b).reshape(b, s, MLA_HEADS, MLA_NOPE_DIM + MLA_ROPE_DIM)
    scale = (MLA_NOPE_DIM + MLA_ROPE_DIM) ** -0.5
    q_nope = q[..., :MLA_NOPE_DIM] * scale
    q_rope = _rope(q[..., MLA_NOPE_DIM:], cos[:, None], sin[:, None]) * scale

    def block(q0, q1):
        logits = (jnp.einsum('bqhd,bkhd->bhqk', q_nope[:, q0:q1], k_nope[:, :q1]).astype(jnp.float32)
                  + jnp.einsum('bqhr,bkr->bhqk', q_rope[:, q0:q1], k_rope[:, :q1]).astype(jnp.float32))
        logits = jnp.where(_chunk_causal_mask(q0, q1), logits, -jnp.inf)
        p = jax.nn.softmax(logits, axis=-1).astype(v.dtype)
        return jnp.einsum('bhqk,bkhd->bqhd', p, v[:, :q1])

    o = _sweep_query_blocks(s, block)
    return o.reshape(b, s, MLA_HEADS * MLA_V_DIM) @ w_o

def _grouped_moe(x, router_w, router_b, w_gate, w_up, w_down):
    b, s, d = x.shape
    t = x.reshape(b * s, d)
    scores = jax.nn.sigmoid((t @ router_w).astype(jnp.float32))
    sel = scores + router_b.astype(jnp.float32)
    grouped = sel.reshape(-1, N_GROUPS, N_EXPERTS // N_GROUPS)
    group_score = jnp.sum(lax.top_k(grouped, 2)[0], axis=-1)
    group_mask = jnp.argmax(group_score, axis=-1)[:, None] == jnp.arange(N_GROUPS)[None, :]
    in_group = jnp.where(group_mask[:, :, None], grouped, -jnp.inf).reshape(-1, N_EXPERTS)
    _, idx = lax.top_k(in_group, TOP_K)
    gate = jnp.take_along_axis(scores, idx, axis=-1)
    gate = gate / jnp.sum(gate, axis=-1, keepdims=True)
    combine = jnp.sum(jax.nn.one_hot(idx, N_EXPERTS, dtype=jnp.float32) * gate[..., None], axis=1).astype(t.dtype)
    y = jnp.zeros_like(t)
    for e in range(N_EXPERTS):
        h = jax.nn.silu(t @ w_gate[e]) * (t @ w_up[e])
        y = y + combine[:, e:e + 1] * (h @ w_down[e])
    return y.reshape(b, s, d)

def setup_inputs(seed: int = 0) -> dict:
    key = jax.random.key(seed)
    ks = jax.random.split(key, 19)
    d = D_MODEL

    def nrm(k, shape, scale):
        return jax.random.normal(k, shape, dtype=jnp.float32) * scale

    return {
        'x': nrm(ks[0], (BATCH, SEQ, d), 1.0),
        'diff_w_qkv': nrm(ks[1], (N_A_LAYERS, d, 3 * DIFF_WIDTH), d ** -0.5),
        'diff_lambda': nrm(ks[2], (N_A_LAYERS, 4, DIFF_HEAD_DIM), 0.1),
        'diff_subln_g': 1.0 + nrm(ks[3], (N_A_LAYERS, DIFF_V_DIM), 0.01),
        'diff_w_o': nrm(ks[4], (N_A_LAYERS, DIFF_WIDTH, d), DEEPNORM_BETA * DIFF_WIDTH ** -0.5),
        'mla_w_kv_a': nrm(ks[5], (d, MLA_KV_RANK + MLA_ROPE_DIM), d ** -0.5),
        'mla_kv_norm_g': 1.0 + nrm(ks[6], (MLA_KV_RANK,), 0.01),
        'mla_w_kv_b': nrm(ks[7], (MLA_KV_RANK, MLA_HEADS * (MLA_NOPE_DIM + MLA_V_DIM)), MLA_KV_RANK ** -0.5),
        'mla_w_q_a': nrm(ks[8], (N_B_LAYERS, d, MLA_Q_RANK), d ** -0.5),
        'mla_q_norm_g': 1.0 + nrm(ks[9], (N_B_LAYERS, MLA_Q_RANK), 0.01),
        'mla_w_q_b': nrm(ks[10], (N_B_LAYERS, MLA_Q_RANK, MLA_HEADS * (MLA_NOPE_DIM + MLA_ROPE_DIM)), MLA_Q_RANK ** -0.5),
        'mla_w_o': nrm(ks[11], (N_B_LAYERS, MLA_HEADS * MLA_V_DIM, d), DEEPNORM_BETA * (MLA_HEADS * MLA_V_DIM) ** -0.5),
        'router_w': nrm(ks[12], (d, N_EXPERTS), d ** -0.5),
        'router_b': nrm(ks[13], (N_EXPERTS,), 0.01),
        'moe_w_gate': nrm(ks[14], (DEPTH, N_EXPERTS, d, EXPERT_FF), d ** -0.5),
        'moe_w_up': nrm(ks[15], (DEPTH, N_EXPERTS, d, EXPERT_FF), d ** -0.5),
        'moe_w_down': nrm(ks[16], (DEPTH, N_EXPERTS, EXPERT_FF, d), DEEPNORM_BETA * EXPERT_FF ** -0.5),
        'ln_g': 1.0 + nrm(ks[17], (DEPTH, 2, d), 0.01),
        'ln_b': nrm(ks[18], (DEPTH, 2, d), 0.01),
    }

def reference(x, diff_w_qkv, diff_lambda, diff_subln_g, diff_w_o, mla_w_kv_a, mla_kv_norm_g, mla_w_kv_b,
              mla_w_q_a, mla_q_norm_g, mla_w_q_b, mla_w_o, router_w, router_b, moe_w_gate, moe_w_up,
              moe_w_down, ln_g, ln_b):
    cos, sin = _rope_tables(x.shape[1])
    for layer in range(DEPTH):
        if layer < N_A_LAYERS:
            h = _diff_attention(x, diff_w_qkv[layer], diff_lambda[layer], diff_subln_g[layer],
                                diff_w_o[layer], _lambda_init(layer))
        else:
            if layer == N_A_LAYERS:
                k_nope, v_shared, k_rope = _mla_shared_kv(x, mla_w_kv_a, mla_kv_norm_g, mla_w_kv_b, cos, sin)
            j = layer - N_A_LAYERS
            h = _mla_attention(x, mla_w_q_a[j], mla_q_norm_g[j], mla_w_q_b[j], mla_w_o[j],
                               k_nope, v_shared, k_rope, cos, sin)
        x = _layernorm(DEEPNORM_ALPHA * x + h, ln_g[layer, 0], ln_b[layer, 0])
        f = _grouped_moe(x, router_w, router_b, moe_w_gate[layer], moe_w_up[layer], moe_w_down[layer])
        x = _layernorm(DEEPNORM_ALPHA * x + f, ln_g[layer, 1], ln_b[layer, 1])
    return x


_drawn_inputs = setup_inputs


def setup_inputs(seed=0):
    import zlib

    import numpy as np

    out = dict(_drawn_inputs(seed))
    spreads = {}
    factors = {'diff_subln_g': 8.0, 'mla_kv_norm_g': 8.0, 'mla_q_norm_g': 8.0}
    for name, (base, spread) in spreads.items():
        noise = np.random.default_rng([zlib.crc32(name.encode()), seed]).standard_normal(out[name].shape)
        drawn = base * np.exp(spread * noise) if base else spread * noise
        out[name] = jnp.asarray(drawn.astype(out[name].dtype))
    for name, factor in factors.items():
        out[name] = (out[name] * factor).astype(out[name].dtype)
    return out
```

```python
import math
from contextlib import ExitStack

import numpy as np

import concourse.bass as bass
from concourse import mybir

F32 = mybir.dt.float32
F32R = mybir.dt.float32r
BF16 = mybir.dt.bfloat16
I32 = mybir.dt.int32
ALU = mybir.AluOpType
ACT = mybir.ActivationFunctionType
AX = mybir.AxisListType

P = 128
SEQ = 256
TT = SEQ // P
D = 1024
KD = D // P
CHUNK = 64
EPS = 1e-5
ALPHA = 4.0 ** 0.25
HEADS = 8
DH = 64
NOPE, ROPE, KVR, QR = 128, 64, 256, 384
LAMBDA_INIT = 0.8 - 0.6 * math.exp(-0.3 * 0)
MLA_SCALE = (NOPE + ROPE) ** -0.5
EXPERTS, GROUPS, FF = 32, 8, 256
PER_GROUP = EXPERTS // GROUPS
WIN = 64
ROUNDS = SEQ // WIN
PAIRS = EXPERTS // 2
SLOTS = 3
KEY = 1024
NSLOT = 2 * SEQ
BIG = 1e30

GU = KD * FF
DN = (FF // P) * D
SLOT = 4 * GU + 2 * DN

CONST = {}
_at = 0
for _name, _n in (("ident", P), ("ones", P), ("dist", 3 * P), ("mask", 3 * P), ("cos", TT * 32), ("sin", TT * 32),
                  ("ecol", ROUNDS * PAIRS), ("rowc", 1), ("w8", GROUPS), ("w32", EXPERTS), ("key", EXPERTS)):
    CONST[_name] = (_at, _at + _n)
    _at += _n
CONSTS = _at


def shape_constants():
    c = np.zeros((P, CONSTS + P), np.float32)

    def put(name, a):
        lo, hi = CONST[name]
        c[:, lo:hi] = a

    p = np.arange(P)
    put("ident", np.eye(P))
    put("ones", 1.0)
    q0, q1, k = p, p + P, np.arange(SEQ)

    def blocked(f):
        return np.concatenate([f(q0[:, None], k[None, :P]), f(q1[:, None], k[None, :])], axis=1)

    seen = blocked(lambda q, k: (k // CHUNK) <= (q // CHUNK))
    put("dist", np.where(seen, blocked(lambda q, k: np.abs(q - k)), BIG))
    put("mask", np.where(seen, 0.0, -BIG))
    inv = (np.float32(10000.0) ** (-np.arange(0, ROPE, 2, dtype=np.float32) / np.float32(ROPE))).astype(np.float32)
    ang = (np.arange(SEQ, dtype=np.float32)[:, None] * inv[None, :]).astype(np.float32).astype(np.float64)
    put("cos", np.cos(ang).reshape(TT, P, 32).transpose(1, 0, 2).reshape(P, -1))
    put("sin", np.sin(ang).reshape(TT, P, 32).transpose(1, 0, 2).reshape(P, -1))
    put("ecol", (2 * KEY * np.arange(PAIRS)[None, :] + WIN * np.arange(ROUNDS)[:, None]).reshape(1, -1))
    put("rowc", (p % WIN + KEY * (p // WIN))[:, None])
    put("w8", GROUPS - np.arange(GROUPS))
    put("w32", EXPERTS - np.arange(EXPERTS))
    put("key", KEY * np.arange(EXPERTS))
    c[:, CONSTS:] = p[:, None] < p[None, :]
    return c


class Chain:

    def __init__(self, eng, sem):
        self.eng, self.sem, self.n = eng, sem, 0

    def __call__(self, ins):
        ins.then_inc(self.sem, 1)
        self.n += 1
        self.eng.wait_ge(self.sem, self.n)


class Phase:

    def __init__(self, sems, totals, layer):
        self.sems, self.totals, self.layer = sems, totals, layer

    def __getitem__(self, name):
        return self.sems[name]

    def __call__(self, name, n):
        return self.sems[name], n + self.layer * self.totals[name]


def build(nc, consts, x, diff_w_qkv, diff_lambda, diff_subln_g, diff_w_o, mla_w_kv_a, mla_kv_norm_g, mla_w_kv_b,
          mla_w_q_a, mla_q_norm_g, mla_w_q_b, mla_w_o, router_w, router_b, moe_w_gate, moe_w_up, moe_w_down,
          ln_g, ln_b, out):
    with ExitStack() as ctx:
        def sb(name, shape, dt=F32):
            return ctx.enter_context(nc.sbuf_tensor(name, shape, dt))

        def sb_and_rounded(name, shape):
            t = sb(name, shape)
            size = 4 * int(np.prod(shape[1:]))
            return t, nc.alloc_sbuf_tensor_at(name + "_rounded", shape, F32R, offset=nc.sbuf_base - size)

        def sem(name):
            return ctx.enter_context(nc.semaphore(name))

        ring = sb("ring", [P, SLOTS * SLOT])
        xs = sb("x_res", [P, TT, D])
        xT, xT_r = sb_and_rounded("x_T", [P, KD, SEQ])
        work, work_r = sb_and_rounded("work", [P, 8192])
        scratch = sb("scratch", [P, 1920])
        cst = sb("cst", [P, CONSTS])
        tri_b = sb("tri_b", [P, P], BF16)
        ones_b = sb("ones_b", [P, P], BF16)
        zeros_b = sb("zeros_b", [P, 512], BF16)
        rb = sb("router_b_sb", [P, EXPERTS])
        eps = sb("eps", [P, 1])
        subg = sb("subln_g_sb", [P, 1])
        qg = sb("q_norm_g_sb", [P, QR // P])
        kvg = sb("kv_norm_g_sb", [P, KVR // P])
        gcol = sb("ln_g_cols", [P, 3, KD])
        bcol = sb("ln_b_cols", [P, 3, KD])
        nlam = sb("neg_lambda", [P, 1])
        ln_stats = sb("ln_stats", [P, TT, 2, 6])
        ln_mv = sb("ln_mean_var", [P, TT, 2])
        ln_sd = sb("ln_sd", [P, TT])
        ln_rstd = sb("ln_rstd", [P, TT])
        ln_nb = sb("ln_neg_mean_rstd", [P, TT])
        small = sb("small", [P, 64])
        offs = sb("window_offsets", [P, ROUNDS * EXPERTS + 2], I32)

        ident, ones = (cst[:, slice(*CONST[n])] for n in ("ident", "ones"))
        dist, mask = (cst[:, slice(*CONST[n])] for n in ("dist", "mask"))
        cos, sin = (cst[:, slice(*CONST[n])].rearrange("p (t f) -> p t f", t=TT) for n in ("cos", "sin"))
        ecol, rowc = (cst[:, slice(*CONST[n])] for n in ("ecol", "rowc"))
        w8, w32, ekey = (cst[:, slice(*CONST[n])] for n in ("w8", "w32", "key"))
        tri_f = work[:, 8064:8192]

        psum = ctx.enter_context(nc.psum_tensor("psum", [P, 8, 512], F32))

        wqkv = ring[:, 0:6 * 4096].rearrange("p (c k n) -> p c k n", c=6, k=KD)
        wo_a = ring[:, 2 * SLOT:2 * SLOT + 8192].rearrange("p (h n) -> p h n", h=HEADS)
        qz = work[:, 0:4096].rearrange("p (h c t) -> p h c t", h=HEADS, c=2)
        kT = work[:, 4096:6144].rearrange("p (h t) -> p h t", h=HEADS)
        v = work[:, 6144:8192].rearrange("p (t n) -> p t n", t=TT)
        o_sb = qz[:, :, 0, :]
        o_sq = qz[:, :, 1, :]
        oT = xT
        lg = scratch[:, 0:1536].rearrange("p (b c n) -> p b c n", b=2, c=2)
        aT = scratch[:, 1536:1920]
        lam_in = scratch[:, 0:256].rearrange("p (i d) -> p i d", i=4)
        lam_prod = scratch[:, 256:384].rearrange("p (i d) -> p i d", i=2)
        lam_dot = small[:, 28:30]
        kva = ring[:, SLOT:SLOT + 2560].rearrange("p (k n) -> p k n", k=KD)
        qa = ring[:, SLOT + 2560:SLOT + 5632].rearrange("p (k n) -> p k n", k=KD)
        qb = ring[:, SLOT + 5632:SLOT + 10240].rearrange("p (k n) -> p k n", k=QR // P)
        kvb = ring[:, 2 * SLOT:2 * SLOT + 4096].rearrange("p (k n) -> p k n", k=KVR // P)
        wo_b = ring[:, 2 * SLOT + 4096:3 * SLOT].rearrange("p (h n) -> p h n", h=HEADS)
        qnT = work[:, 0:2048].rearrange("p (h t) -> p h t", h=HEADS)
        qrz = work[:, 2048:4096].rearrange("p (h t) -> p h t", h=HEADS)
        knT = kT
        c_q = work[:, 6144:6912].rearrange("p (t n) -> p t n", t=TT)
        c_kv = work[:, 6912:7424].rearrange("p (t n) -> p t n", t=TT)
        kr_raw = work[:, 7424:7552].rearrange("p (t n) -> p t n", t=TT)
        kr2 = work[:, 7552:7808].rearrange("p (t n) -> p t n", t=TT)
        sq_junk = work[:, 7808:8192]
        qr_raw = xT[:, 0:4, :].rearrange("p a b -> p (a b)").rearrange("p (t h d) -> p t h d", t=TT, h=HEADS)
        qr_rot = xT[:, 4:8, :].rearrange("p a b -> p (a b)").rearrange("p (t h d) -> p t h d", t=TT, h=HEADS)
        cqT = scratch[:, 0:768].rearrange("p (k t) -> p k t", k=QR // P)
        ckvT = scratch[:, 768:1280].rearrange("p (k t) -> p k t", k=KVR // P)
        krT2 = scratch[:, 1280:1536]
        rope_tmp = scratch[:, 1536:1792].rearrange("p (h d) -> p h d", h=HEADS)
        rope_tmp2 = sq_junk[:, 0:256].rearrange("p (h d) -> p h d", h=HEADS)
        mlg = scratch[:, 0:768].rearrange("p (b n) -> p b n", b=2)
        pT = scratch[:, 768:1152]
        gb = [a.rearrange("p (s n) -> p s n", s=2) for a in (
            work[:, 4096:6144], ring[:, SLOT + 10240:2 * SLOT], work[:, 4096:6144], work[:, 0:2048])]
        XW = NSLOT + WIN
        xsT = work[:, 0:KD * XW].rearrange("p (k s) -> p k s", k=KD)
        xg = work[:, KD * XW:KD * XW + SLOTS * KD * P].rearrange("p (b k c) -> p b k c", b=SLOTS, k=KD)
        top = work[:, KD * XW + 2 * KD * P:KD * XW + 3 * KD * P]
        rw = work[:, 7680:7936].rearrange("p (k e) -> p k e", k=KD)
        hi_parts = [xT_r[:, 4:8, :].rearrange("p a b -> p (a b)").rearrange("p (k n) -> p k n", k=KD),
                    work_r[:, 7680:8192].rearrange("p (k n) -> p k n", k=4),
                    work_r[:, 7 * XW:7 * XW + NSLOT].rearrange("p (k n) -> p k n", k=4)]
        hi_of = [(0, 0, KD), (1, 0, 4), (1, 4, KD)]
        xs_lo = work_r[:, KD * XW:KD * XW + TT * D].rearrange("p (t k n) -> p t k n", t=TT, k=KD)

        def xs_tiles(t, k0, k1):
            return xs[:, t, :].rearrange("p (n k) -> p k n", k=KD)[:, k0:k1, :]

        def xs_hi(t, k):
            part, first = (0, 0) if t == 0 else (1 + k // 4, 4 * (k // 4))
            return hi_parts[part][:, k - first, :]

        onehot_r = xT_r[:, 0:4, :].rearrange("p a b -> p (a b)").rearrange("p (t s) -> p t s", t=TT)
        y_sb = xT[:, 0:4, :].rearrange("p a b -> p (a b)")
        key_row = xT[:, 4:6, :]
        gate_row = xT[:, 6:8, :]
        diag = scratch[:, 768:1792].rearrange("p (t q n) -> p t q n", t=TT, q=4)
        logit_T = scratch[0:EXPERTS, 0:256]
        iota = scratch[:, 256:768]
        comb = scratch[:, 0:768].rearrange("p (b t) -> p b t", b=SLOTS)
        act_s = scratch[:, 768:1024]
        h_sb = scratch[:, 1024:1280]
        hT = scratch[:, 1280:1536].rearrange("p (k c) -> p k c", k=FF // P)
        g_tmp = scratch[:, 1536:1792]

        def slot_gu(s, j):
            a = s * SLOT + j * 2 * GU
            return ring[:, a:a + 2 * GU].rearrange("p (u k f) -> p u k f", u=2, k=KD)

        def slot_dn(s, j):
            a = s * SLOT + 4 * GU + j * DN
            return ring[:, a:a + DN].rearrange("p (k n) -> p k n", k=FF // P)

        ld_x = [sem(f"ld_x{t}") for t in range(TT)]
        MISC = 7
        ld_cst, ld_misc, ld_lam = sem("ld_cst"), sem("ld_misc"), sem("ld_lam")
        ld_rw = [sem(f"ld_router{l}") for l in range(2)]
        ld_qkv = [sem(f"ld_qkv{c}") for c in range(6)]
        ld_wo_a = sem("ld_wo_a")
        ld_kva, ld_qa, ld_qb, ld_kvb, ld_wo_b = (sem(n) for n in ("ld_kva", "ld_qa", "ld_qb", "ld_kvb", "ld_wo_b"))
        sems = {"gb": sem("ld_ln")}
        ld_gb = [Phase(sems, {"gb": 32}, n) for n in range(4)]
        cast_ready, zeroed, lam_ready, lam_exp = (sem(n) for n in ("cast_ready", "zeroed", "lam_ready", "lam_exp"))
        totals = {"ps": 4, "sb": KD}
        sems = {n: sem("xt_" + n) for n in totals}
        xt = [Phase(sems, totals, n) for n in range(4)]
        qkv_ps, qkv_act, qkv_dve = sem("qkv_ps"), sem("qkv_act"), sem("qkv_dve")
        totals = {"sc_ps": 2 * HEADS, "sc_read": 2 * HEADS, "mx_ready": 2 * HEADS, "e_ready": 4 * HEADS,
                  "r_ready": HEADS, "e1_scaled": 2 * HEADS, "p_ready": 2 * HEADS, "pt_ps": HEADS, "pt_sb": HEADS,
                  "o_ps": HEADS, "o_sb": HEADS}
        sems = {n: sem(n) for n in totals}
        at = [Phase(sems, totals, l) for l in range(2)]
        sq_ready, ss_ready, sd_ready, rs_ready = sem("sq_ready"), sem("ss_ready"), sem("sd_ready"), sem("rs_ready")
        on_dve, on_pool, ot_ps, ot_sb = sem("on_dve"), sem("on_pool"), sem("ot_ps"), sem("ot_sb")
        wo_ps = [sem(f"wo_ps{l}") for l in range(2)]
        totals = {"var": TT, "sd": TT, "rstd": TT, "norm": TT + 1, "x_dve": 1, "x_pool": 1}
        sems = {n: sem("ln_" + n) for n in totals}
        ln = [Phase(sems, totals, n) for n in range(4)]
        mq = {n: sem("mla_" + n) for n in (
            "a_ps", "sq", "sd", "rstd", "c_ready", "kr_raw", "kr_rot", "ct_ps", "ct_sb", "qr_ps", "qr_raw", "qr_rot_dve",
            "qr_rot_pool", "b_ps", "b_sb", "b_act", "b_dve", "qt_ps", "qt_sb", "krt_ps", "krt_sb", "zeroed")}
        totals = {"lgt_ps": 1, "lgt_sb": 1, "lg_ps": 1, "score": 1, "m_ready": 1, "rank_ps": 1, "offs_ready": 1,
                  "iota_ready": 1, "hi_ready": 3, "lo_ready": 3, "hot_ready": TT, "pad_zero": 1, "key_ready": 1, "sort_ps": KD, "sort_act": KD // 2,
                  "sort_dve": KD // 2, "diag_ready": 4 * TT, "row_ps": 1, "row_sb_a": TT, "row_sb_d": TT,
                  "xg_ready": 2 * PAIRS, "gu_ps": PAIRS, "s_ready": PAIRS, "h_ready": PAIRS, "ht_ps": PAIRS,
                  "ht_sb": PAIRS, "y_ps": PAIRS, "y_act": PAIRS, "y_dve": PAIRS, "g_part": 2 * PAIRS,
                  "g_ready": PAIRS, "c_ps": PAIRS, "sum_ps": 1}
        sems = {n: sem("moe_" + n) for n in totals}
        mo = [Phase(sems, totals, l) for l in range(2)]
        uses = [len(range(s, PAIRS, SLOTS)) for s in range(SLOTS)]
        sems = [{n: sem(f"ring_{n}{s}") for n in ("gu", "dn")} for s in range(SLOTS)]
        rings = [[Phase(sems[s], {"gu": 64 * uses[s], "dn": 32 * uses[s]}, l) for s in range(SLOTS)]
                 for l in range(2)]
        names = ("w", "xg", "gu", "s", "h", "ht_ps", "ht_sb", "y_ps", "y_act", "y_dve", "g_part", "g", "free")
        ov = [{n: sem(f"ov_{n}{l}") for n in names} for l in range(2)]
        out_done = sem("out_done")
        dve_chain, act_chain, pool_chain = sem("dve_chain"), sem("act_chain"), sem("pool_chain")

        def for_pairs_4_up(eng, body):
            with eng.Fori(0, (PAIRS - 4) // SLOTS) as it:
                for j in range(SLOTS):
                    body(it * SLOTS + (4 + j), (4 + j) % SLOTS)

        def for_pairs_1_up(eng, body):
            with eng.Fori(0, (PAIRS - 1) // SLOTS) as it:
                for j in range(SLOTS):
                    body(it * SLOTS + (1 + j), (1 + j) % SLOTS)

        def overflow_steps(eng, body):
            with eng.Fori(1, ROUNDS) as r:
                with eng.Fori(0, PAIRS) as i:
                    body(i, r, (r - 1) * PAIRS + i)

        def overflows(eng, l):
            eng.wait_ge(*mo[l]("offs_ready", 1))
            n = eng.value_load(offs[0:1, ROUNDS * EXPERTS:ROUNDS * EXPERTS + 1], min_val=0, max_val=SEQ)
            return n > WIN

        def routing():
            c, at_ = {}, 0
            for name, n in (("score", 64), ("sel", 64), ("mx2", 32), ("mn2", 32), ("t1", 16), ("t2", 16), ("t3", 16),
                            ("gs", 16), ("gmax", 2), ("gkey", 16), ("gmask", 16), ("masked", 64), ("m1", 2),
                            ("e1", 64), ("k1", 2), ("oh", 128), ("prod", 128), ("cnt", 32), ("pre", 64),
                            ("rank", 64), ("start", 64), ("s12", 4), ("chosen", 32)):
                c[name] = top[:, at_:at_ + n]
                at_ += n
            c["chosen"] = c["chosen"].bitcast(BF16).rearrange("p (t e) -> p t e", t=TT)
            return c

        def rotate(eng, link, dst, src, t, tmp, heads):
            shape = [P, heads, 32]
            c = cos[:, t, :].unsqueeze(1).broadcast_to(shape)
            s = sin[:, t, :].unsqueeze(1).broadcast_to(shape)
            lo, hi = slice(0, 32), slice(32, 64)
            link(eng.tensor_tensor(dst[:, :, lo], src[:, :, lo], c, ALU.mult))
            link(eng.tensor_tensor(tmp, src[:, :, hi], s, ALU.mult))
            link(eng.tensor_tensor(dst[:, :, lo], dst[:, :, lo], tmp, ALU.subtract))
            link(eng.tensor_tensor(dst[:, :, hi], src[:, :, hi], c, ALU.mult))
            link(eng.tensor_tensor(tmp, src[:, :, lo], s, ALU.mult))
            return eng.tensor_tensor(dst[:, :, hi], dst[:, :, hi], tmp, ALU.add)

        block = ctx.enter_context(nc.Block())

        @block.sync
        def _(sp):
            sp.dma_start(cst[:, :], consts[:, 0:CONSTS]).then_inc(ld_cst, 16)
            for t in range(TT):
                sp.dma_start(xs[:, t, :], x[0, t * P:(t + 1) * P, :]).then_inc(ld_x[t], 16)
            wq = diff_w_qkv[0].rearrange("(p k) n -> p k n", k=KD)
            for c in range(6):
                sp.dma_start(wqkv[:, c, :, :], wq[:, :, c * 512:(c + 1) * 512]).then_inc(ld_qkv[c], 16)
            sp.dma_start(wo_a, diff_w_o[0].rearrange("(h p) n -> p h n", p=P)).then_inc(ld_wo_a, 16)

            def load_gate_up(l, i, s):
                for j in range(2):
                    for u, w in enumerate((moe_w_gate, moe_w_up)):
                        sp.dma_start(slot_gu(s, j)[:, u, :, :],
                                     w[l, i * 2 + j].rearrange("(p k) f -> p k f", k=KD)).then_inc(rings[l][s]["gu"], 16)

            def load_down(l, i, s):
                for j in range(2):
                    sp.dma_start(slot_dn(s, j), moe_w_down[l, i * 2 + j].rearrange("(k p) n -> p k n", p=P))\
                      .then_inc(rings[l][s]["dn"], 16)

            def load_pair(l, i, s):
                load_gate_up(l, i, s)
                load_down(l, i, s)

            def load_ln(n):
                sp.dma_start(gb[n][:, 0, :], ln_g[n // 2, n % 2].partition_broadcast(P)).then_inc(ld_gb[n]["gb"], 16)
                sp.dma_start(gb[n][:, 1, :], ln_b[n // 2, n % 2].partition_broadcast(P)).then_inc(ld_gb[n]["gb"], 16)

            def load_router(l):
                sp.wait_ge(*at[l]("o_ps", HEADS))
                sp.dma_start(rw, router_w.rearrange("(p k) n -> p k n", k=KD)).then_inc(ld_rw[l], 16)

            def moe(l):
                def reload(i, s):
                    sp.wait_ge(*mo[l]("gu_ps", i - 2))
                    load_gate_up(l, i, s)
                    sp.wait_ge(*mo[l]("y_ps", i - 2))
                    load_down(l, i, s)

                reload(3, 0)
                for_pairs_4_up(sp, reload)

            def overflow(l):
                with sp.If(overflows(sp, l)):
                    sp.wait_ge(*mo[l]("y_ps", PAIRS))

                    def step(i, r, n):
                        sp.wait_ge(ov[l]["free"], n + 1)
                        for j in range(2):
                            for u, w in enumerate((moe_w_gate, moe_w_up)):
                                sp.dma_start(slot_gu(0, j)[:, u, :, :],
                                             w[l, i * 2 + j].rearrange("(p k) f -> p k f", k=KD))\
                                  .then_inc(ov[l]["w"], 16)
                            sp.dma_start(slot_dn(0, j), moe_w_down[l, i * 2 + j].rearrange("(k p) n -> p k n", p=P))\
                              .then_inc(ov[l]["w"], 16)

                    overflow_steps(sp, step)
                    sp.wait_ge(ov[l]["y_ps"], PAIRS * (ROUNDS - 1))

            sp.wait_ge(qkv_ps, 12)
            load_pair(0, 0, 0)
            load_pair(0, 1, 1)
            sp.wait_ge(*at[0]("sc_ps", 2 * HEADS))
            load_ln(0)
            load_router(0)
            sp.wait_ge(wo_ps[0], 4)
            load_pair(0, 2, 2)
            moe(0)
            sp.wait_ge(*mo[0]("gu_ps", 14))
            sp.dma_start(qa, mla_w_q_a[0].rearrange("(p k) n -> p k n", k=KD)).then_inc(ld_qa, 16)
            sp.dma_start(kva, mla_w_kv_a.rearrange("(p k) n -> p k n", k=KD)).then_inc(ld_kva, 16)
            sp.wait_ge(*mo[0]("y_ps", 14))
            load_ln(1)
            sp.dma_start(qb, mla_w_q_b[0].rearrange("(k p) n -> p k n", p=P)).then_inc(ld_qb, 16)
            sp.wait_ge(*mo[0]("y_ps", 15))
            sp.dma_start(kvb, mla_w_kv_b.rearrange("(k p) n -> p k n", p=P)).then_inc(ld_kvb, 16)
            sp.dma_start(wo_b, mla_w_o[0].rearrange("(h p) n -> p h n", p=P)).then_inc(ld_wo_b, 16)
            overflow(0)
            sp.wait_ge(*mo[0]("y_ps", PAIRS))
            load_pair(1, 0, 0)
            sp.wait_ge(mq["b_ps"], 4)
            sp.wait_ge(*ln[1]("x_dve", 1))
            sp.wait_ge(*ln[1]("x_pool", 1))
            load_pair(1, 1, 1)
            sp.wait_ge(*at[1]("sc_ps", HEADS))
            load_ln(2)
            load_router(1)
            sp.wait_ge(wo_ps[1], 4)
            load_pair(1, 2, 2)
            moe(1)
            overflow(1)
            sp.wait_ge(*mo[1]("xg_ready", 2 * PAIRS))
            load_ln(3)
            for t in range(TT):
                sp.wait_ge(*ln[3](("x_dve", "x_pool")[t], 1))
                sp.dma_start(out[0, t * P:(t + 1) * P, :], xs[:, t, :]).then_inc(out_done, 16)
            sp.wait_ge(out_done, 16 * TT)

        @block.tensor
        def _(pe):
            def mm(dst, lhsT, rhs, start, stop):
                return pe.matmul(dst, lhsT, rhs, start=start, stop=stop, skip_group_check=True)

            def transpose_x(n):
                for t in range(TT):
                    if n:
                        pe.wait_ge(*ln[n - 1]("norm", (1, 3)[t]))
                    for k in range(KD):
                        at_ = (k % 2) * SEQ + t * P
                        last = pe.transpose(psum[:, 4 + k // 2, at_:at_ + P], xs[:, t, k::KD], ident)
                        if t and k % 2:
                            last.then_inc(xt[n]["ps"], 1)
                pe.wait_ge(*xt[n]("sb", KD))

            def out_projection(l, w, ld):
                pe.wait_ge(ld, 16)
                for t in range(TT):
                    for c in range(2):
                        for h in range(HEADS):
                            last = mm(psum[:, 2 * t + c, :], oT[:, h, t * P:(t + 1) * P],
                                      w[:, h, c * 512:(c + 1) * 512], h == 0, h == HEADS - 1)
                        last.then_inc(wo_ps[l], 1)

            def diff_attention():
                pe.wait_ge(ld_cst, 16)
                for t in range(TT):
                    pe.wait_ge(ld_x[t], 16)
                transpose_x(0)
                g = 0
                for c in range(4):
                    pe.wait_ge(ld_qkv[c], 16)
                    for m in range(4):
                        for k in range(KD):
                            last = mm(psum[:, g % 8, (m % 2) * SEQ:(m % 2 + 1) * SEQ],
                                      wqkv[:, c, k, m * P:(m + 1) * P], xT[:, k, :], k == 0, k == KD - 1)
                        if m % 2:
                            last.then_inc(qkv_ps, 1)
                            g += 1
                for c in range(4, 6):
                    pe.wait_ge(ld_qkv[c], 16)
                    for t in range(TT):
                        pe.wait_ge((qkv_act, qkv_dve)[g % 2], 2 * ((g - 8) // 2 + 1))
                        for k in range(KD):
                            last = mm(psum[:, g % 8, :], xT[:, k, t * P:(t + 1) * P], wqkv[:, c, k, :],
                                      k == 0, k == KD - 1)
                        last.then_inc(qkv_ps, 1)
                        g += 1
                s = at[0]
                pe.wait_ge(qkv_act, 8)
                pe.wait_ge(qkv_dve, 8)
                pe.wait_ge(zeroed, 2)

                def scores(h):
                    if h >= 2:
                        pe.wait_ge(*s("sc_read", 2 * (h - 1)))
                    for c in range(2):
                        bank = psum[:, 2 * (h % 2) + c, :]
                        mm(bank[:, 0:P], qz[:, h, c, 0:P], kT[:, h, 0:P], True, True)
                        mm(bank[:, P:3 * P], qz[:, h, c, P:SEQ], kT[:, h, :], True, True).then_inc(s["sc_ps"], 1)

                def transposes(h):
                    pe.wait_ge(*s("p_ready", 2 * (h + 1)))
                    if h >= 2:
                        pe.wait_ge(*s("pt_sb", h - 1))
                    for b in range(3):
                        last = pe.transpose(psum[:, 4 + h % 2, b * P:(b + 1) * P], lg[:, h % 2, 0, b * P:(b + 1) * P],
                                            ident)
                    last.then_inc(s["pt_ps"], 1)

                def values(h):
                    pe.wait_ge(*s("pt_sb", h + 1))
                    if h >= 2:
                        pe.wait_ge(*s("o_sb", h - 1))
                    bank = psum[:, 6 + h % 2, :]
                    hv = slice(h * P, (h + 1) * P)
                    mm(bank[:, 0:P], aT[:, 0:P], v[:, 0, hv], True, True)
                    mm(bank[:, P:SEQ], aT[:, P:2 * P], v[:, 0, hv], True, False)
                    mm(bank[:, P:SEQ], aT[:, 2 * P:3 * P], v[:, 1, hv], False, True).then_inc(s["o_ps"], 1)

                scores(0)
                scores(1)
                for h in range(HEADS):
                    transposes(h)
                    if h + 2 < HEADS:
                        scores(h + 2)
                    values(h)
                for b in range(4):
                    pe.wait_ge((on_dve, on_pool)[b // 2], 1)
                    for h in (2 * b, 2 * b + 1):
                        for t in range(TT):
                            a = (h % 2) * SEQ + t * P
                            last = pe.transpose(psum[:, 4 + b, a:a + P], o_sb[:, h, t * P:(t + 1) * P], ident)
                    last.then_inc(ot_ps, 1)
                pe.wait_ge(ot_sb, 4)
                out_projection(0, wo_a, ld_wo_a)

            def mla_attention():
                transpose_x(2)
                pe.wait_ge(ld_qa, 16)
                for t in range(TT):
                    for k in range(KD):
                        last = mm(psum[:, 2 + t, 0:QR], xT[:, k, t * P:(t + 1) * P], qa[:, k, :], k == 0, k == KD - 1)
                    last.then_inc(mq["a_ps"], 1)
                pe.wait_ge(ld_kva, 16)
                for t in range(TT):
                    for k in range(KD):
                        last = mm(psum[:, t, 0:KVR + ROPE], xT[:, k, t * P:(t + 1) * P], kva[:, k, :],
                                  k == 0, k == KD - 1)
                    last.then_inc(mq["a_ps"], 1)
                pe.wait_ge(mq["c_ready"], 2)
                for k in range(QR // P):
                    for t in range(TT):
                        a = (k % 2) * SEQ + t * P
                        last = pe.transpose(psum[:, 4 + k // 2, a:a + P], c_q[:, t, k * P:(k + 1) * P], ident)
                last.then_inc(mq["ct_ps"], 1)
                pe.wait_ge(mq["c_ready"], 4)
                for k in range(KVR // P):
                    for t in range(TT):
                        a = k * SEQ + t * P
                        last = pe.transpose(psum[:, 6, a:a + P], c_kv[:, t, k * P:(k + 1) * P], ident)
                last.then_inc(mq["ct_ps"], 1)
                pe.wait_ge(ld_qb, 16)
                pe.wait_ge(mq["ct_sb"], 5)
                qb_h = qb.rearrange("p k (h n) -> p k h n", h=HEADS)
                for t in range(TT):
                    for k in range(QR // P):
                        last = mm(psum[:, 2 + t, :], cqT[:, k, t * P:(t + 1) * P], qb_h[:, k, :, NOPE:],
                                  k == 0, k == QR // P - 1)
                    last.then_inc(mq["qr_ps"], 1)
                banks = [4, 5, 0, 1, 6, 7, 4, 5, 0, 1, 2, 3]
                kvb_h = kvb.rearrange("p k (h n) -> p k h n", h=HEADS)
                for g in range(12):
                    if 6 <= g < 10:
                        pe.wait_ge((mq["b_act"], mq["b_dve"])[g % 2], (g - 6) // 2 + 1)
                    if g >= 10:
                        pe.wait_ge(mq["qr_raw"], 2)
                    if g == 4:
                        pe.wait_ge(ld_kvb, 16)
                    if g < 8:
                        w, src, n = (qb_h, cqT, QR // P) if g < 4 else (kvb_h, ckvT, KVR // P)
                        for h in (2 * (g % 4), 2 * (g % 4) + 1):
                            for k in range(n):
                                last = mm(psum[:, banks[g], (h % 2) * SEQ:(h % 2 + 1) * SEQ], w[:, k, h, 0:NOPE],
                                          src[:, k, :], k == 0, k == n - 1)
                    else:
                        t, half = (g - 8) // 2, (g - 8) % 2
                        for k in range(KVR // P):
                            last = mm(psum[:, banks[g], :], ckvT[:, k, t * P:(t + 1) * P],
                                      kvb_h[:, k, 4 * half:4 * half + 4, NOPE:], k == 0, k == KVR // P - 1)
                    last.then_inc(mq["b_ps"], 1)
                pe.wait_ge(mq["kr_rot"], 1)
                pe.wait_ge(mq["b_act"], 4)
                pe.wait_ge(mq["b_dve"], 4)
                for t in range(TT):
                    last = pe.transpose(psum[:, 6, t * P:(t + 1) * P], kr2[:, t, :], ident)
                last.then_inc(mq["krt_ps"], 1)
                pe.wait_ge(mq["qr_rot_dve"], 1)
                pe.wait_ge(mq["qr_rot_pool"], 1)
                for b in range(2):
                    for hp in (2 * b, 2 * b + 1):
                        for t in range(TT):
                            a = (hp % 2) * SEQ + t * P
                            last = pe.transpose(psum[:, (7, 4)[b], a:a + P],
                                                qr_rot[:, t, 2 * hp:2 * hp + 2, :].rearrange("p h d -> p (h d)"), ident)
                    last.then_inc(mq["qt_ps"], 1)
                s = at[1]
                pe.wait_ge(mq["b_act"], 6)
                pe.wait_ge(mq["b_dve"], 6)
                pe.wait_ge(mq["krt_sb"], 1)
                pe.wait_ge(mq["zeroed"], 2)
                pe.wait_ge(mq["qt_sb"], 4)

                def scores(h):
                    if h >= 2:
                        pe.wait_ge(*s("sc_read", h - 1))
                    bank = psum[:, h % 2, :]
                    mm(bank[:, 0:P], qnT[:, h, 0:P], knT[:, h, 0:P], True, False)
                    mm(bank[:, 0:P], qrz[:, h, 0:P], krT2[:, 0:P], False, True)
                    mm(bank[:, P:3 * P], qnT[:, h, P:SEQ], knT[:, h, :], True, False)
                    mm(bank[:, P:3 * P], qrz[:, h, P:SEQ], krT2, False, True).then_inc(s["sc_ps"], 1)

                def transposes(h):
                    pe.wait_ge(*s("p_ready", 2 * (h + 1)))
                    if h >= 2:
                        pe.wait_ge(*s("pt_sb", h - 1))
                    for b in range(3):
                        last = pe.transpose(psum[:, 2 + h % 2, b * P:(b + 1) * P], mlg[:, h % 2, b * P:(b + 1) * P],
                                            ident)
                    last.then_inc(s["pt_ps"], 1)

                def values(h):
                    pe.wait_ge(*s("pt_sb", h + 1))
                    if h >= 2:
                        pe.wait_ge(*s("o_sb", h - 1))
                    bank = psum[:, 4 + h % 2, :]
                    hv = slice(h * P, (h + 1) * P)
                    mm(bank[:, 0:SEQ], v[:, 0, hv], pT[:, 0:SEQ], True, False)
                    mm(bank[:, P:SEQ], v[:, 1, hv], pT[:, SEQ:3 * P], False, True).then_inc(s["o_ps"], 1)

                scores(0)
                scores(1)
                for h in range(HEADS):
                    transposes(h)
                    if h + 2 < HEADS:
                        scores(h + 2)
                    values(h)
                pe.wait_ge(*s("o_sb", HEADS))
                out_projection(1, wo_b, ld_wo_b)

            def moe(l):
                m = mo[l]
                transpose_x(2 * l + 1)
                pe.wait_ge(ld_rw[l], 16)
                for k in range(KD):
                    last = mm(psum[0:EXPERTS, 0, 0:SEQ], rw[:, k, :], xT[:, k, :], k == 0, k == KD - 1)
                last.then_inc(m["lgt_ps"], 1)
                pe.wait_ge(*m("lgt_sb", 1))
                for t in range(TT):
                    last = pe.transpose(psum[:, 1, t * EXPERTS:(t + 1) * EXPERTS], logit_T[:, t * P:(t + 1) * P],
                                        ident[0:EXPERTS, 0:EXPERTS])
                last.then_inc(m["lg_ps"], 1)
                pe.wait_ge(*m("m_ready", 1))
                pe.wait_ge(cast_ready, 3)
                chosen = routing()["chosen"]
                rank = psum[:, 2, :]
                mm(rank[:, 0:32], tri_b[:, :], chosen[:, 0, :], True, True)
                mm(rank[:, 32:64], tri_b[:, :], chosen[:, 1, :], True, False)
                mm(rank[:, 32:64], ones_b[:, :], chosen[:, 0, :], False, True)
                mm(rank[:, 64:96], ones_b[:, :], chosen[:, 0, :], True, False)
                mm(rank[:, 64:96], ones_b[:, :], chosen[:, 1, :], False, True).then_inc(m["rank_ps"], 1)
                pe.wait_ge(*m("hi_ready", 3))
                pe.wait_ge(*m("lo_ready", 3))
                pe.wait_ge(*m("hot_ready", TT))
                for k in range(KD):
                    for t in range(TT):
                        for half, part in enumerate((xs_hi(t, k), xs_lo[:, t, k, :])):
                            last = mm(psum[:, k, :], part, onehot_r[:, t, :],
                                      t == 0 and half == 0, t == TT - 1 and half == 1)
                    last.then_inc(m["sort_ps"], 1)
                pe.wait_ge(*m("diag_ready", 8))
                pe.wait_ge(*m("sort_act", 1))
                pe.wait_ge(*m("sort_dve", 1))
                for t in range(TT):
                    last = mm(psum[:, t, :], ones, diag[:, t, :, :].rearrange("p q n -> p (q n)"), True, True)
                last.then_inc(m["row_ps"], 1)
                pe.wait_ge(*m("sort_act", 4))
                pe.wait_ge(*m("sort_dve", 4))
                pe.wait_ge(*m("row_sb_a", TT))
                pe.wait_ge(*m("row_sb_d", TT))
                for b in range(4):
                    mm(psum[:, b, :], zeros_b[:, 0:P], zeros_b[:, :], True, False)

                def up(s, buf):
                    for k in range(KD):
                        for j in range(2):
                            last = mm(psum[j * WIN:(j + 1) * WIN, 6, :], xg[:, buf, k, j * WIN:(j + 1) * WIN],
                                      slot_gu(s, j)[:, :, k, :], k == 0, k == KD - 1)
                    return last

                def transpose_h():
                    for k in range(FF // P):
                        last = pe.transpose(psum[:, 7, k * P:(k + 1) * P], h_sb[:, k * P:(k + 1) * P], ident)
                    return last

                def down(s):
                    for c in range(2):
                        for k in range(FF // P):
                            for j in range(2):
                                last = mm(psum[j * WIN:(j + 1) * WIN, 4 + c, :], hT[:, k, j * WIN:(j + 1) * WIN],
                                          slot_dn(s, j)[:, k, c * 512:(c + 1) * 512], k == 0, k == FF // P - 1)
                    return last

                def combine(buf, t):
                    for c in range(2):
                        last = mm(psum[:, 2 * t + c, :], comb[:, buf, t * P:(t + 1) * P],
                                  y_sb[:, c * 512:(c + 1) * 512], False, False)
                    return last

                def pair(i, s, first=False):
                    prev = (s + SLOTS - 1) % SLOTS
                    pe.wait_ge(*m("xg_ready", i * 2 + 2))
                    pe.wait_ge(*rings[l][s]("gu", turn(i, s) * 64))
                    if not first:
                        pe.wait_ge(*m("h_ready", i))
                    up(s, s).then_inc(m["gu_ps"], 1)
                    if not first:
                        pe.wait_ge(*m("y_act", i))
                        pe.wait_ge(*m("y_dve", i))
                        pe.wait_ge(*m("g_ready", i))
                        combine(prev, 0)
                    pe.wait_ge(*m("h_ready", i + 1))
                    if not first:
                        pe.wait_ge(*m("ht_sb", i))
                    transpose_h().then_inc(m["ht_ps"], 1)
                    if not first:
                        combine(prev, 1).then_inc(m["c_ps"], 1)
                    pe.wait_ge(*m("ht_sb", i + 1))
                    pe.wait_ge(*rings[l][s]("dn", turn(i, s) * 32))
                    down(s).then_inc(m["y_ps"], 1)

                def turn(i, s):
                    return (i - s) // SLOTS + 1 if isinstance(i, int) else turns[s]

                pair(0, 0, True)
                turns = [None] * SLOTS
                with pe.Fori(0, (PAIRS - 1) // SLOTS) as it:
                    for j in range(SLOTS):
                        i, s = it * SLOTS + (1 + j), (1 + j) % SLOTS
                        turns[s] = it + (1 + (1 + j) // SLOTS)
                        pair(i, s)
                s = (PAIRS - 1) % SLOTS
                pe.wait_ge(*m("y_act", PAIRS))
                pe.wait_ge(*m("y_dve", PAIRS))
                pe.wait_ge(*m("g_ready", PAIRS))
                combine(s, 0)
                combine(s, 1).then_inc(m["c_ps"], 1)
                with pe.If(overflows(pe, l)):
                    o = ov[l]
                    pe.sem_inc(o["free"], 1)

                    def step(i, r, n):
                        pe.wait_ge(o["w"], n * 96 + 96)
                        pe.wait_ge(o["xg"], n * 2 + 2)
                        up(0, 0).then_inc(o["gu"], 1)
                        pe.wait_ge(o["h"], n + 1)
                        transpose_h().then_inc(o["ht_ps"], 1)
                        pe.wait_ge(o["ht_sb"], n + 1)
                        down(0).then_inc(o["y_ps"], 1)
                        pe.wait_ge(o["y_act"], n + 1)
                        pe.wait_ge(o["y_dve"], n + 1)
                        pe.wait_ge(o["g"], n + 1)
                        combine(0, 0)
                        combine(0, 1).then_inc(o["free"], 1)

                    overflow_steps(pe, step)
                for b in range(4):
                    last = mm(psum[:, b, :], zeros_b[:, 0:P], zeros_b[:, :], False, True)
                last.then_inc(m["sum_ps"], 1)

            diff_attention()
            moe(0)
            mla_attention()
            moe(1)

        @block.scalar
        def _(act):
            chain = Chain(act, act_chain)

            def act_xt(n):
                for b in (0, 2):
                    act.wait_ge(*xt[n]("ps", b + 1))
                    if n == 0:
                        act.copy(xT[:, 2 * b:2 * b + 2, :], psum[:, 4 + b, :].rearrange("p (k t) -> p k t", k=2))\
                           .then_inc(xt[n]["sb"], 2)
                        continue
                    for k in (2 * b, 2 * b + 1):
                        act.activation(xT[:, k, :], psum[:, 4 + b, (k % 2) * SEQ:(k % 2 + 1) * SEQ], ACT.Identity,
                                       scale=gcol[:, n - 1, k:k + 1], bias=bcol[:, n - 1, k:k + 1])\
                           .then_inc(xt[n]["sb"], 1)

            def layer_norm(n):
                for t in range(TT):
                    act.wait_ge(*ln[n]("var", t + 1))
                    act.activation(ln_sd[:, t:t + 1], ln_mv[:, t, 1:2], ACT.Sqrt, bias=eps[:, :]).then_inc(ln[n]["sd"], 1)
                    cols = (slice(0, D), slice(0, D // 2))[t]
                    act.wait_ge(*ln[n]("rstd", t + 1))
                    act.activation(xs[:, t, cols], xs[:, t, cols], ACT.Identity, scale=ln_rstd[:, t:t + 1],
                                   bias=ln_nb[:, t:t + 1]).then_inc(ln[n]["norm"], 1)

            def diff_attention():
                act_xt(0)
                act.wait_ge(lam_ready, 2)
                act.activation(lam_dot, lam_dot, ACT.Exp).then_inc(lam_exp, 1)
                for g in (0, 2):
                    act.wait_ge(qkv_ps, g + 1)
                    for c in range(2):
                        rows = slice(c * DH, (c + 1) * DH)
                        act.mul(qz[rows, 2 * g:2 * g + 2, c, :], psum[rows, g, :].rearrange("p (h t) -> p h t", h=2),
                                DH ** -0.5).then_inc(qkv_act, 1)
                for g in (4, 6):
                    act.wait_ge(qkv_ps, g + 1)
                    act.copy(kT[:, 2 * (g - 4):2 * (g - 4) + 2, :], psum[:, g, :].rearrange("p (h t) -> p h t", h=2))\
                       .then_inc(qkv_act, 1)
                for g in (8, 10):
                    act.wait_ge(qkv_ps, g + 1)
                    c = (g - 8) // 2
                    act.copy(v[:, 0, c * 512:(c + 1) * 512], psum[:, g % 8, :]).then_inc(qkv_act, 1)
                s = at[0]
                nmx = small[:, 0:8].rearrange("p (b q c) -> p b q c", b=2, q=2)
                sums = small[:, 8:16].rearrange("p (b q c) -> p b q c", b=2, q=2)
                nlr = small[:, 24:28].rearrange("p (b q) -> p b q", b=2)
                part = (slice(0, P), slice(P, 3 * P))

                def exps(h):
                    act.wait_ge(*s("mx_ready", 2 * (h + 1)))
                    for c in range(2):
                        for q in range(2):
                            e = lg[:, h % 2, c, part[q]]
                            act.activation(e, e, ACT.Exp, bias=nmx[:, h % 2, q, c:c + 1],
                                           accum_out=sums[:, h % 2, q, c:c + 1]).then_inc(s["e_ready"], 1)

                def scale_second(h):
                    act.wait_ge(*s("r_ready", h + 1))
                    for q in range(2):
                        e = lg[:, h % 2, 1, part[q]]
                        act.activation(e, e, ACT.Copy, scale=nlr[:, h % 2, q:q + 1]).then_inc(s["e1_scaled"], 1)

                def out(h):
                    act.wait_ge(*s("o_ps", h + 1))
                    act.copy(o_sb[:, h, :], psum[:, 6 + h % 2, 0:SEQ]).then_inc(s["o_sb"], 1)

                exps(0)
                for h in range(HEADS):
                    scale_second(h)
                    if h + 1 < HEADS:
                        exps(h + 1)
                    if h >= 1:
                        out(h - 1)
                out(HEADS - 1)
                ss, sd = small[:, 32:48], small[:, 48:64]
                act.wait_ge(ss_ready, 1)
                act.activation(sd, ss, ACT.Sqrt, scale=1.0 / P, bias=eps[:, :]).then_inc(sd_ready, 1)
                for b in (0, 2):
                    act.wait_ge(ot_ps, b + 1)
                    act.activation(oT[:, 2 * b:2 * b + 2, :], psum[:, 4 + b, :].rearrange("p (h t) -> p h t", h=2),
                                   ACT.Copy, scale=subg[:, :]).then_inc(ot_sb, 1)

            def mla_attention():
                act_xt(2)
                ss, sd = small[:, 0:4], small[:, 4:8]
                for i, (bank, n) in enumerate(((2, QR), (3, QR), (0, KVR), (1, KVR))):
                    act.wait_ge(mq["a_ps"], i + 1)
                    chain(act.activation(sq_junk[:, 0:n], psum[:, bank, 0:n], ACT.Square, accum_out=ss[:, i:i + 1]))
                    act.activation(sd[:, i:i + 1], ss[:, i:i + 1], ACT.Sqrt, scale=1.0 / n, bias=eps[:, :])\
                       .then_inc(mq["sd"], 1)
                act.wait_ge(mq["ct_ps"], 1)
                act.activation(cqT[:, 0, :], psum[:, 4, 0:SEQ], ACT.Copy, scale=qg[:, 0:1]).then_inc(mq["ct_sb"], 1)
                act.activation(cqT[:, 1, :], psum[:, 4, SEQ:], ACT.Copy, scale=qg[:, 1:2]).then_inc(mq["ct_sb"], 1)
                for t in range(TT):
                    act.wait_ge(mq["qr_ps"], t + 1)
                    act.mul(qr_raw[:, t, :, :], psum[:, 2 + t, :].rearrange("p (h d) -> p h d", h=HEADS), MLA_SCALE)\
                       .then_inc(mq["qr_raw"], 1)
                banks = [4, 5, 0, 1, 6, 7, 4, 5, 0, 1, 2, 3]
                for g in range(0, 12, 2):
                    act.wait_ge(mq["b_ps"], g + 1)
                    src = psum[:, banks[g], :]
                    if g < 4:
                        act.mul(qnT[:, 2 * g:2 * g + 2, :], src.rearrange("p (h t) -> p h t", h=2), MLA_SCALE)\
                           .then_inc(mq["b_act"], 1)
                    elif g < 8:
                        act.copy(knT[:, 2 * (g - 4):2 * (g - 4) + 2, :], src.rearrange("p (h t) -> p h t", h=2))\
                           .then_inc(mq["b_act"], 1)
                    else:
                        act.wait_ge(mq["krt_ps"], 1)
                        act.copy(v[:, (g - 8) // 2, 0:512], src).then_inc(mq["b_act"], 1)
                for b in range(2):
                    act.wait_ge(mq["qt_ps"], b + 1)
                    src = psum[0:ROPE, (7, 4)[b], :].rearrange("p (h t) -> p h t", h=2)
                    act.copy(qrz[0:ROPE, 4 * b:4 * b + 4:2, :], src).then_inc(mq["qt_sb"], 1)
                s = at[1]
                nmx = small[:, 16:20].rearrange("p (b q) -> p b q", b=2)
                sums = small[:, 20:24].rearrange("p (b q) -> p b q", b=2)

                def exps(h):
                    act.wait_ge(*s("mx_ready", 2 * (h + 1)))
                    for q, part in enumerate((slice(0, P), slice(P, 3 * P))):
                        e = mlg[:, h % 2, part]
                        act.activation(e, e, ACT.Exp, bias=nmx[:, h % 2, q:q + 1],
                                       accum_out=sums[:, h % 2, q:q + 1]).then_inc(s["e_ready"], 1)

                def out(h):
                    act.wait_ge(*s("o_ps", h + 1))
                    act.copy(oT[:, h, :], psum[:, 4 + h % 2, 0:SEQ]).then_inc(s["o_sb"], 1)

                exps(0)
                for h in range(HEADS):
                    if h + 1 < HEADS:
                        exps(h + 1)
                    act.wait_ge(*s("pt_ps", h + 1))
                    if h >= 1:
                        act.wait_ge(*s("o_ps", h))
                        out(h - 1)
                    act.copy(pT, psum[:, 2 + h % 2, 0:3 * P]).then_inc(s["pt_sb"], 1)
                out(HEADS - 1)

            def moe(l):
                m = mo[l]
                act_xt(2 * l + 1)
                act.wait_ge(*m("lg_ps", 1))
                act.activation(routing()["score"], psum[:, 1, 0:64], ACT.Sigmoid).then_inc(m["score"], 1)
                for part, (t, k0, k1) in zip(hi_parts, hi_of):
                    act.wait_ge(*ln[2 * l](("x_dve", "x_pool")[t], 1))
                    act.copy(part, xs_tiles(t, k0, k1)).then_inc(m["hi_ready"], 1)
                for k in range(0, KD, 2):
                    act.wait_ge(*m("sort_ps", k + 1))
                    act.copy(xsT[:, k, 0:NSLOT], psum[:, k, :]).then_inc(m["sort_act"], 1)
                act.wait_ge(*m("row_ps", 1))
                for t in range(TT):
                    act.copy(gate_row[:, :, t * P:(t + 1) * P],
                             psum[:, t, 2 * P:4 * P].rearrange("p (j n) -> p j n", j=2)).then_inc(m["row_sb_a"], 1)

                def pair(i, s, first=False):
                    act.wait_ge(*m("gu_ps", i + 1))
                    if not first:
                        act.wait_ge(*m("h_ready", i))
                    act.activation(act_s, psum[:, 6, 0:FF], ACT.Silu).then_inc(m["s_ready"], 1)
                    act.wait_ge(*m("ht_ps", i + 1))
                    if not first:
                        act.wait_ge(*m("y_ps", i))
                    act.copy(hT, psum[:, 7, 0:FF].rearrange("p (k c) -> p k c", k=2)).then_inc(m["ht_sb"], 1)
                    act.wait_ge(*m("y_ps", i + 1))
                    if not first:
                        act.wait_ge(*m("c_ps", i))
                    act.copy(y_sb[:, 0:512], psum[:, 4, :]).then_inc(m["y_act"], 1)

                pair(0, 0, True)
                for_pairs_1_up(act, pair)
                with act.If(overflows(act, l)):
                    o = ov[l]

                    def step(i, r, n):
                        act.wait_ge(o["gu"], n + 1)
                        act.activation(act_s, psum[:, 6, 0:FF], ACT.Silu).then_inc(o["s"], 1)
                        act.wait_ge(o["ht_ps"], n + 1)
                        act.copy(hT, psum[:, 7, 0:FF].rearrange("p (k c) -> p k c", k=2)).then_inc(o["ht_sb"], 1)
                        act.wait_ge(o["y_ps"], n + 1)
                        act.copy(y_sb[:, 0:512], psum[:, 4, :]).then_inc(o["y_act"], 1)

                    overflow_steps(act, step)

            act.dma_start(tri_f, consts[:, CONSTS:CONSTS + P]).then_inc(ld_misc, 16)
            act.dma_start(lam_in, diff_lambda[0].partition_broadcast(P)).then_inc(ld_lam, 16)
            act.dma_start(rb[:, :], router_b.partition_broadcast(P)).then_inc(ld_misc, 16)
            with nc.allow_non_contiguous_dma(reason="norm scales as columns, once"):
                act.dma_start(subg[:, :], diff_subln_g[0].rearrange("(p a) -> p a", a=1)).then_inc(ld_misc, 16)
                act.dma_start(qg[:, :], mla_q_norm_g[0].rearrange("(k p) -> p k", p=P)).then_inc(ld_misc, 16)
                act.dma_start(kvg[:, :], mla_kv_norm_g.rearrange("(k p) -> p k", p=P)).then_inc(ld_misc, 16)
                for col, w in ((gcol, ln_g), (bcol, ln_b)):
                    act.dma_start(col[:, :, :], w.rearrange("l j (p k) -> p (l j) k", k=KD)[:, 0:3, :])\
                       .then_inc(ld_misc, 16)
            diff_attention()
            layer_norm(0)
            act.wait_ge(ld_misc, 16 * MISC)
            moe(0)
            layer_norm(1)
            mla_attention()
            layer_norm(2)
            moe(1)
            layer_norm(3)

        @block.vector
        def _(dve):
            chain = Chain(dve, dve_chain)

            def dve_xt(n):
                for b in (1, 3):
                    dve.wait_ge(*xt[n]("ps", b + 1))
                    if n == 0:
                        dve.tensor_copy(xT[:, 2 * b:2 * b + 2, :], psum[:, 4 + b, :].rearrange("p (k t) -> p k t", k=2))\
                           .then_inc(xt[n]["sb"], 2)
                        continue
                    for k in (2 * b, 2 * b + 1):
                        dve.tensor_scalar(xT[:, k, :], psum[:, 4 + b, (k % 2) * SEQ:(k % 2 + 1) * SEQ],
                                          gcol[:, n - 1, k:k + 1], bcol[:, n - 1, k:k + 1], ALU.mult, ALU.add)\
                           .then_inc(xt[n]["sb"], 1)

            def layer_norm(n, ready):
                def add(t):
                    ready(t)
                    chain(dve.scalar_tensor_tensor(out=xs[:, t, :], in0=xs[:, t, :], scalar=ALPHA,
                                                   in1=psum[:, 2 * t:2 * t + 2, :].rearrange("p b n -> p (b n)"),
                                                   op0=ALU.mult, op1=ALU.add))

                def statistics(t):
                    for c in range(2):
                        chain(dve.bn_stats(ln_stats[:, t, c, :], xs[:, t, c * 512:(c + 1) * 512]))
                    dve.bn_aggr(ln_mv[:, t, :], ln_stats[:, t, :, :].rearrange("p c s -> p (c s)"))\
                       .then_inc(ln[n]["var"], 1)

                def scales(t):
                    dve.wait_ge(*ln[n]("sd", t + 1))
                    chain(dve.reciprocal(ln_rstd[:, t:t + 1], ln_sd[:, t:t + 1]))
                    dve.tensor_scalar(ln_nb[:, t:t + 1], ln_mv[:, t, 0:1], ln_rstd[:, t:t + 1], -1.0, ALU.mult,
                                      ALU.mult).then_inc(ln[n]["rstd"], 1)

                add(0)
                statistics(0)
                add(1)
                scales(0)
                statistics(1)
                scales(1)
                dve.wait_ge(*ln[n]("rstd", 2))
                dve.tensor_scalar(xs[:, 1, D // 2:], xs[:, 1, D // 2:], ln_rstd[:, 1:2], ln_nb[:, 1:2], ALU.mult,
                                  ALU.add).then_inc(ln[n]["norm"], 1)

            def scale_shift(n):
                dve.wait_ge(*ln[n]("norm", 3))
                dve.wait_ge(*ld_gb[n]("gb", 32))
                chain(dve.tensor_tensor(xs[:, 0, :], xs[:, 0, :], gb[n][:, 0, :], ALU.mult))
                dve.tensor_tensor(xs[:, 0, :], xs[:, 0, :], gb[n][:, 1, :], ALU.add).then_inc(ln[n]["x_dve"], 1)

            def prepare():
                dve.memset(zeros_b[:, :], 0.0).then_inc(cast_ready, 1)
                dve.memset(eps[:, :], EPS).then_inc(lam_ready, 1)
                dve.wait_ge(ld_cst, 16)
                dve.tensor_copy(ones_b[:, :], ones).then_inc(cast_ready, 1)

            def diff_attention():
                dve_xt(0)
                dve.wait_ge(ld_misc, 16 * MISC)
                dve.tensor_copy(tri_b[:, :], tri_f).then_inc(cast_ready, 1)
                dve.wait_ge(ld_lam, 16)
                chain(dve.tensor_tensor(lam_prod, lam_in[:, 0::2, :], lam_in[:, 1::2, :], ALU.mult))
                dve.tensor_reduce(lam_dot, lam_prod, AX.X, ALU.add).then_inc(lam_ready, 1)
                dve.wait_ge(lam_exp, 1)
                chain(dve.tensor_tensor(nlam[:, :], lam_dot[:, 1:2], lam_dot[:, 0:1], ALU.subtract))
                chain(dve.tensor_scalar(nlam[:, :], nlam[:, :], LAMBDA_INIT, None, ALU.subtract))
                chain(dve.tensor_scalar(subg[:, :], subg[:, :], 1.0 - LAMBDA_INIT, None, ALU.mult))
                for g in (1, 3):
                    dve.wait_ge(qkv_ps, g + 1)
                    for c in range(2):
                        rows = slice(c * DH, (c + 1) * DH)
                        dve.tensor_scalar(qz[rows, 2 * g:2 * g + 2, c, :],
                                          psum[rows, g, :].rearrange("p (h t) -> p h t", h=2), DH ** -0.5, None,
                                          ALU.mult).then_inc(qkv_dve, 1)
                for g in (5, 7):
                    dve.wait_ge(qkv_ps, g + 1)
                    dve.tensor_copy(kT[:, 2 * (g - 4):2 * (g - 4) + 2, :],
                                    psum[:, g, :].rearrange("p (h t) -> p h t", h=2)).then_inc(qkv_dve, 1)
                dve.wait_ge(cast_ready, 3)
                for g in (9, 11):
                    dve.wait_ge(qkv_ps, g + 1)
                    c = (g - 8) // 2
                    dve.tensor_copy(v[:, 1, c * 512:(c + 1) * 512], psum[:, g % 8, :]).then_inc(qkv_dve, 1)
                s = at[0]
                nmx = small[:, 0:8].rearrange("p (b q c) -> p b q c", b=2, q=2)
                sums = small[:, 8:16].rearrange("p (b q c) -> p b q c", b=2, q=2)
                rec = small[:, 16:24].rearrange("p (b q c) -> p b q c", b=2, q=2)
                nlr = small[:, 24:28].rearrange("p (b q) -> p b q", b=2)

                def logits(h):
                    if h >= 2:
                        dve.wait_ge(*s("pt_ps", h - 1))
                    for c in range(2):
                        dve.wait_ge(*s("sc_ps", 2 * h + c + 1))
                        dve.scalar_tensor_tensor(out=lg[:, h % 2, c, :], in0=dist, scalar=-(2.0 ** -(h + 1)),
                                                 in1=psum[:, 2 * (h % 2) + c, 0:3 * P], op0=ALU.mult, op1=ALU.add)\
                           .then_inc(s["sc_read"], 1)
                    dve.wait_ge(*s("sc_read", 2 * (h + 1)))
                    dve.tensor_reduce(nmx[:, h % 2, 0, :], lg[:, h % 2, :, 0:P], AX.X, ALU.max, negate=True)\
                       .then_inc(s["mx_ready"], 1)
                    dve.tensor_reduce(nmx[:, h % 2, 1, :], lg[:, h % 2, :, P:3 * P], AX.X, ALU.max, negate=True)\
                       .then_inc(s["mx_ready"], 1)

                def reciprocals(h):
                    dve.wait_ge(*s("e_ready", 4 * (h + 1)))
                    chain(dve.reciprocal(rec[:, h % 2, :, :], sums[:, h % 2, :, :]))
                    dve.tensor_scalar(nlr[:, h % 2, :], rec[:, h % 2, :, 1], nlam[:, :], None, ALU.mult)\
                       .then_inc(s["r_ready"], 1)

                def probabilities(h):
                    dve.wait_ge(*s("e1_scaled", 2 * (h + 1)))
                    for q, part in enumerate((slice(0, P), slice(P, 3 * P))):
                        dve.scalar_tensor_tensor(out=lg[:, h % 2, 0, part], in0=lg[:, h % 2, 0, part],
                                                 scalar=rec[:, h % 2, q, 0:1], in1=lg[:, h % 2, 1, part],
                                                 op0=ALU.mult, op1=ALU.add).then_inc(s["p_ready"], 1)

                def transposed(h):
                    dve.wait_ge(*s("pt_ps", h + 1))
                    if h >= 1:
                        dve.wait_ge(*s("o_ps", h))
                    dve.tensor_copy(aT, psum[:, 4 + h % 2, 0:3 * P]).then_inc(s["pt_sb"], 1)

                logits(0)
                for h in range(HEADS):
                    if h + 1 < HEADS:
                        logits(h + 1)
                    reciprocals(h)
                    if h >= 1:
                        transposed(h - 1)
                    probabilities(h)
                transposed(HEADS - 1)
                ss, sd = small[:, 32:48], small[:, 48:64]
                dve.wait_ge(*s("o_sb", HEADS))
                chain(dve.tensor_tensor(o_sq[:, 0:4, :], o_sb[:, 0:4, :], o_sb[:, 0:4, :], ALU.mult))
                dve.wait_ge(sq_ready, 1)
                dve.tensor_reduce(ss, o_sq.rearrange("p h (q d) -> p h q d", q=2), AX.X, ALU.add)\
                   .then_inc(ss_ready, 1)
                dve.wait_ge(sd_ready, 1)
                rs = small[:, 32:48].rearrange("p (h q) -> p h q", h=HEADS)
                dve.reciprocal(small[:, 32:48], sd).then_inc(rs_ready, 1)
                dve.wait_ge(rs_ready, 1)
                o4 = o_sb[:, 0:4, :].rearrange("p h (q d) -> p h q d", q=2)
                dve.tensor_tensor(o4, o4, rs[:, 0:4, :].unsqueeze(3).broadcast_to([P, 4, 2, P]), ALU.mult)\
                   .then_inc(on_dve, 1)
                for b in (1, 3):
                    dve.wait_ge(ot_ps, b + 1)
                    dve.tensor_scalar(oT[:, 2 * b:2 * b + 2, :], psum[:, 4 + b, :].rearrange("p (h t) -> p h t", h=2),
                                      subg[:, :], None, ALU.mult).then_inc(ot_sb, 1)

            def mla_attention():
                dve_xt(2)
                dve.wait_ge(*xt[2]("ps", 4))
                scale_shift(1)
                sd, rstd = small[:, 4:8], small[:, 8:12]
                for i, (bank, n) in enumerate(((2, QR), (3, QR), (0, KVR), (1, KVR))):
                    dve.wait_ge(mq["sd"], i + 1)
                    chain(dve.reciprocal(rstd[:, i:i + 1], sd[:, i:i + 1]))
                    dst = c_q[:, i, :] if i < 2 else c_kv[:, i - 2, :]
                    dve.tensor_scalar(dst, psum[:, bank, 0:n], rstd[:, i:i + 1], None, ALU.mult)\
                       .then_inc(mq["c_ready"], 1)
                    if i >= 2:
                        chain(dve.tensor_copy(kr_raw[:, i - 2, :], psum[:, bank, KVR:KVR + ROPE]))
                dve.wait_ge(mq["ct_ps"], 1)
                dve.tensor_scalar(cqT[:, 2, :], psum[:, 5, 0:SEQ], qg[:, 2:3], None, ALU.mult).then_inc(mq["ct_sb"], 1)
                dve.wait_ge(mq["ct_ps"], 2)
                for k in range(2):
                    dve.tensor_scalar(ckvT[:, k, :], psum[:, 6, k * SEQ:(k + 1) * SEQ], kvg[:, k:k + 1], None, ALU.mult)\
                       .then_inc(mq["ct_sb"], 1)
                for t in range(TT):
                    dst = kr2[:, t, 0:ROPE].unsqueeze(1)
                    chain(rotate(dve, chain, dst, kr_raw[:, t, :].unsqueeze(1), t, rope_tmp[:, 0:1, :], 1))
                dve.tensor_copy(kr2[:, :, ROPE:2 * ROPE], kr2[:, :, 0:ROPE]).then_inc(mq["kr_rot"], 1)
                banks = [4, 5, 0, 1, 6, 7, 4, 5, 0, 1, 2, 3]
                for g in range(1, 12, 2):
                    if g == 3:
                        dve.wait_ge(mq["qr_raw"], 1)
                        rotate(dve, chain, qr_rot[:, 0, :, :], qr_raw[:, 0, :, :], 0, rope_tmp, HEADS)\
                            .then_inc(mq["qr_rot_dve"], 1)
                    dve.wait_ge(mq["b_ps"], g + 1)
                    src = psum[:, banks[g], :]
                    if g < 4:
                        dve.tensor_scalar(qnT[:, 2 * g:2 * g + 2, :], src.rearrange("p (h t) -> p h t", h=2), MLA_SCALE,
                                          None, ALU.mult).then_inc(mq["b_dve"], 1)
                    elif g < 8:
                        dve.tensor_copy(knT[:, 2 * (g - 4):2 * (g - 4) + 2, :],
                                        src.rearrange("p (h t) -> p h t", h=2)).then_inc(mq["b_dve"], 1)
                    else:
                        dve.wait_ge(mq["krt_ps"], 1)
                        dve.wait_ge(mq["qr_rot_pool"], 1)
                        dve.tensor_copy(v[:, (g - 8) // 2, 512:1024], src).then_inc(mq["b_dve"], 1)
                dve.wait_ge(mq["krt_ps"], 1)
                dve.tensor_copy(krT2, psum[:, 6, 0:SEQ]).then_inc(mq["krt_sb"], 1)
                for b in range(2):
                    dve.wait_ge(mq["qt_ps"], b + 1)
                    src = psum[ROPE:P, (7, 4)[b], :].rearrange("p (h t) -> p h t", h=2)
                    dve.tensor_copy(qrz[ROPE:P, 4 * b + 1:4 * b + 4:2, :], src).then_inc(mq["qt_sb"], 1)
                s = at[1]
                nmx = small[:, 16:20].rearrange("p (b q) -> p b q", b=2)
                sums = small[:, 20:24].rearrange("p (b q) -> p b q", b=2)
                rec = small[:, 24:28].rearrange("p (b q) -> p b q", b=2)

                def logits(h):
                    if h >= 2:
                        dve.wait_ge(*s("pt_ps", h - 1))
                    dve.wait_ge(*s("sc_ps", h + 1))
                    dve.tensor_tensor(mlg[:, h % 2, :], psum[:, h % 2, 0:3 * P], mask, ALU.add)\
                       .then_inc(s["sc_read"], 1)
                    dve.wait_ge(*s("sc_read", h + 1))
                    for q, part in enumerate((slice(0, P), slice(P, 3 * P))):
                        dve.tensor_reduce(nmx[:, h % 2, q:q + 1], mlg[:, h % 2, part], AX.X, ALU.max, negate=True)\
                           .then_inc(s["mx_ready"], 1)

                def probabilities(h):
                    dve.wait_ge(*s("e_ready", 2 * (h + 1)))
                    chain(dve.reciprocal(rec[:, h % 2, :], sums[:, h % 2, :]))
                    for q, part in enumerate((slice(0, P), slice(P, 3 * P))):
                        dve.tensor_scalar(mlg[:, h % 2, part], mlg[:, h % 2, part], rec[:, h % 2, q:q + 1], None,
                                          ALU.mult).then_inc(s["p_ready"], 1)

                dve.wait_ge(mq["b_ps"], 12)
                logits(0)
                for h in range(HEADS):
                    if h + 1 < HEADS:
                        logits(h + 1)
                    probabilities(h)

            def moe(l):
                m = mo[l]
                dve_xt(2 * l + 1)
                dve.wait_ge(*xt[2 * l + 1]("ps", 4))
                scale_shift(2 * l)
                dve.wait_ge(*m("lgt_ps", 1))
                dve.tensor_copy(logit_T, psum[0:EXPERTS, 0, 0:SEQ]).then_inc(m["lgt_sb"], 1)
                c = routing()
                both = TT * EXPERTS

                def tt(dst, a, b, op):
                    chain(dve.tensor_tensor(dst, a, b, op))

                def te(a):
                    return a.rearrange("p (t e) -> p t e", t=TT)

                def spread(a, n):
                    return a.unsqueeze(2).broadcast_to([P, TT, n])

                def per_tile(a, n):
                    return a.unsqueeze(1).broadcast_to([P, TT, n])

                dve.wait_ge(*m("score", 1))
                tt(te(c["sel"]), te(c["score"]), per_tile(rb[:, :], EXPERTS), ALU.add)
                quad = c["sel"].rearrange("p (g e) -> p g e", e=PER_GROUP)
                mx2, mn2 = (c[n].rearrange("p (g e) -> p g e", e=2) for n in ("mx2", "mn2"))
                tt(mx2, quad[:, :, 0::2], quad[:, :, 1::2], ALU.max)
                tt(mn2, quad[:, :, 0::2], quad[:, :, 1::2], ALU.min)
                tt(c["t1"], mx2[:, :, 0], mx2[:, :, 1], ALU.max)
                tt(c["t2"], mx2[:, :, 0], mx2[:, :, 1], ALU.min)
                tt(c["t3"], mn2[:, :, 0], mn2[:, :, 1], ALU.max)
                tt(c["t2"], c["t2"], c["t3"], ALU.max)
                tt(c["gs"], c["t1"], c["t2"], ALU.add)
                chain(dve.tensor_reduce(c["gmax"], te(c["gs"]), AX.X, ALU.max))
                tt(te(c["gkey"]), te(c["gs"]), spread(c["gmax"], GROUPS), ALU.is_equal)
                tt(te(c["gkey"]), te(c["gkey"]), per_tile(w8, GROUPS), ALU.mult)
                chain(dve.tensor_reduce(c["gmax"], te(c["gkey"]), AX.X, ALU.max))
                tt(te(c["gmask"]), te(c["gkey"]), spread(c["gmax"], GROUPS), ALU.is_equal)
                masked = c["masked"].rearrange("p (g e) -> p g e", e=PER_GROUP)
                wide = [P, TT * GROUPS, PER_GROUP]
                tt(masked, quad, c["gmask"].unsqueeze(2).broadcast_to(wide), ALU.mult)
                chain(dve.tensor_scalar(c["gmask"], c["gmask"], 1.0, BIG, ALU.subtract, ALU.mult))
                tt(masked, masked, c["gmask"].unsqueeze(2).broadcast_to(wide), ALU.add)
                oh = c["oh"].rearrange("p (j t e) -> p j t e", j=2, t=TT)
                for j in range(2):
                    chain(dve.tensor_reduce(c["m1"], te(c["masked"]), AX.X, ALU.max))
                    tt(te(c["e1"]), te(c["masked"]), spread(c["m1"], EXPERTS), ALU.is_equal)
                    tt(te(c["e1"]), te(c["e1"]), per_tile(w32, EXPERTS), ALU.mult)
                    chain(dve.tensor_reduce(c["k1"], te(c["e1"]), AX.X, ALU.max))
                    tt(oh[:, j], te(c["e1"]), spread(c["k1"], EXPERTS), ALU.is_equal)
                    if j == 0:
                        chain(dve.scalar_tensor_tensor(out=c["masked"], in0=c["oh"][:, 0:both], scalar=-3 * BIG,
                                                       in1=c["masked"], op0=ALU.mult, op1=ALU.add))
                dve.tensor_tensor(c["chosen"], oh[:, 0], oh[:, 1], ALU.add).then_inc(m["m_ready"], 1)
                kg = small[:, 0:8].rearrange("p (q t) -> p q t", q=4)
                slot = small[:, 8:12].rearrange("p (j t) -> p j t", j=2)
                total = small[:, 12:14]
                prod = c["prod"].rearrange("p (j n) -> p j n", j=2)
                oh2 = c["oh"].rearrange("p (j n) -> p j n", j=2)

                def pick(dst, src):
                    tt(prod, oh2, src.unsqueeze(1).broadcast_to([P, 2, both]), ALU.mult)
                    chain(dve.tensor_reduce(dst, c["prod"].rearrange("p (j t e) -> p j t e", j=2, t=TT), AX.X, ALU.add))

                pick(kg[:, 2:4, :], c["score"])
                tt(total, kg[:, 2, :], kg[:, 3, :], ALU.add)
                chain(dve.reciprocal(total, total))
                tt(kg[:, 2:4, :], kg[:, 2:4, :], total.unsqueeze(1).broadcast_to([P, 2, TT]), ALU.mult)
                dve.wait_ge(*m("rank_ps", 1))
                pre = [c["pre"][:, 0:32], c["pre"][:, 32:64]]
                chain(dve.memset(pre[0][:, 0:1], 0.0))
                chain(dve.tensor_copy(pre[0][:, 1:32], psum[:, 2, 64:95]))
                for n, d in enumerate((1, 2, 4, 8, 16)):
                    a, b = pre[n % 2], pre[(n + 1) % 2]
                    chain(dve.tensor_copy(b[:, 0:d], a[:, 0:d]))
                    tt(b[:, d:], a[:, d:], a[:, 0:32 - d], ALU.add)
                start = pre[1]
                for r in range(ROUNDS):
                    chain(dve.tensor_scalar(offs[:, r * EXPERTS:(r + 1) * EXPERTS], start, float(WIN * r), float(NSLOT),
                                            ALU.add, ALU.min))
                chain(dve.tensor_reduce(c["cnt"][:, 0:1], psum[:, 2, 64:96], AX.X, ALU.max))
                dve.tensor_copy(offs[:, ROUNDS * EXPERTS:ROUNDS * EXPERTS + 1], c["cnt"][:, 0:1])\
                   .then_inc(m["offs_ready"], 1)
                rank = psum[:, 2, 0:both]
                tt(te(c["start"]), te(rank), per_tile(start, EXPERTS), ALU.add)
                pick(slot, c["start"])
                tt(te(c["rank"]), te(rank), per_tile(ekey, EXPERTS), ALU.add)
                tt(prod, oh2, c["rank"].unsqueeze(1).broadcast_to([P, 2, both]), ALU.mult)
                dve.tensor_reduce(kg[:, 0:2, :], c["prod"].rearrange("p (j t e) -> p j t e", j=2, t=TT), AX.X, ALU.add)\
                   .then_inc(m["key_ready"], 1)
                dve.wait_ge(*m("iota_ready", 1))
                for t in range(TT):
                    chain(dve.tensor_scalar(onehot_r[:, t, :], iota, slot[:, 0, t:t + 1], None, ALU.is_equal))
                    dve.scalar_tensor_tensor(out=onehot_r[:, t, :], in0=iota, scalar=slot[:, 1, t:t + 1],
                                             in1=onehot_r[:, t, :], op0=ALU.is_equal, op1=ALU.add)\
                       .then_inc(m["hot_ready"], 1)
                for k in range(1, KD, 2):
                    dve.wait_ge(*m("sort_ps", k + 1))
                    dve.tensor_copy(xsT[:, k, 0:NSLOT], psum[:, k, :]).then_inc(m["sort_dve"], 1)
                dve.wait_ge(*m("row_ps", 1))
                dve.wait_ge(*m("row_sb_a", TT))
                for t in range(TT):
                    dve.tensor_scalar(key_row[:, :, t * P:(t + 1) * P],
                                      psum[:, t, 0:2 * P].rearrange("p (j n) -> p j n", j=2), rowc, None,
                                      ALU.subtract).then_inc(m["row_sb_d"], 1)
                dve.wait_ge(*m("row_sb_d", TT))

                def weights(i, r, buf, part, ready, n):
                    at_ = ecol[:, bass.ds(i + r * PAIRS, 1)]
                    dve.scalar_tensor_tensor(out=comb[:, buf, :], in0=key_row[:, 0, :], scalar=at_,
                                             in1=gate_row[:, 0, :], op0=ALU.is_equal, op1=ALU.mult).then_inc(part, 1)
                    dve.scalar_tensor_tensor(out=g_tmp, in0=key_row[:, 1, :], scalar=at_,
                                             in1=gate_row[:, 1, :], op0=ALU.is_equal, op1=ALU.mult).then_inc(part, 1)
                    dve.wait_ge(part, n * 2 + 2)
                    dve.tensor_tensor(comb[:, buf, :], comb[:, buf, :], g_tmp, ALU.add).then_inc(ready, 1)

                def pair(i, s, first=False):
                    dve.wait_ge(*m("s_ready", i + 1))
                    if not first:
                        dve.wait_ge(*m("ht_ps", i))
                    dve.tensor_tensor(h_sb, psum[:, 6, FF:2 * FF], act_s, ALU.mult).then_inc(m["h_ready"], 1)
                    if not first:
                        dve.wait_ge(*m("g_ready", i))
                    weights(i, 0, s, m["g_part"], m["g_ready"], i + l * PAIRS)
                    dve.wait_ge(*m("y_ps", i + 1))
                    if not first:
                        dve.wait_ge(*m("c_ps", i))
                    dve.tensor_copy(y_sb[:, 512:1024], psum[:, 5, :]).then_inc(m["y_dve"], 1)

                pair(0, 0, True)
                for_pairs_1_up(dve, pair)
                with dve.If(overflows(dve, l)):
                    o = ov[l]
                    dve.wait_ge(*m("c_ps", PAIRS))

                    def step(i, r, n):
                        dve.wait_ge(o["free"], n + 1)
                        dve.wait_ge(o["s"], n + 1)
                        dve.tensor_tensor(h_sb, psum[:, 6, FF:2 * FF], act_s, ALU.mult).then_inc(o["h"], 1)
                        weights(i, r, 0, o["g_part"], o["g"], n)
                        dve.wait_ge(o["y_ps"], n + 1)
                        dve.tensor_copy(y_sb[:, 512:1024], psum[:, 5, :]).then_inc(o["y_dve"], 1)

                    overflow_steps(dve, step)

            prepare()
            diff_attention()
            layer_norm(0, lambda t: dve.wait_ge(wo_ps[0], 2 * t + 2))
            moe(0)
            layer_norm(1, lambda t: dve.wait_ge(*mo[0]("sum_ps", 1)))
            mla_attention()
            layer_norm(2, lambda t: dve.wait_ge(wo_ps[1], 2 * t + 2))
            moe(1)
            layer_norm(3, lambda t: dve.wait_ge(*mo[1]("sum_ps", 1)))
            scale_shift(3)

        @block.gpsimd
        def _(pool):
            chain = Chain(pool, pool_chain)

            def layer_norm(n):
                pool.wait_ge(*ln[n]("norm", 3))
                if n < 3:
                    pool.wait_ge(*xt[n + 1]("ps", 4))
                pool.wait_ge(*ld_gb[n]("gb", 32))
                chain(pool.tensor_tensor(xs[:, 1, :], xs[:, 1, :], gb[n][:, 0, :], ALU.mult))
                pool.tensor_tensor(xs[:, 1, :], xs[:, 1, :], gb[n][:, 1, :], ALU.add).then_inc(ln[n]["x_pool"], 1)

            def windows(i, r, buf, ready):
                for j in range(2):
                    a = pool.value_load(offs[0:1, bass.ds(r * EXPERTS + i * 2 + j, 1)], min_val=0, max_val=NSLOT)
                    last = pool.tensor_copy(xg[:, buf, :, j * WIN:(j + 1) * WIN], xsT[:, :, bass.ds(a, WIN)])
                    last.then_inc(ready, 1)

            def moe(l):
                m = mo[l]
                pool.wait_ge(*ln[2 * l]("x_dve", 1))
                pool.iota(iota, pattern=[[1, NSLOT]], base=0, channel_multiplier=0,
                          allow_small_or_imprecise_dtypes=True).then_inc(m["iota_ready"], 1)
                pool.memset(xsT[:, :, NSLOT:], 0.0).then_inc(m["pad_zero"], 1)
                pool.wait_ge(*ln[2 * l]("x_pool", 1))
                for n, (part, (t, k0, k1)) in enumerate(zip(hi_parts, hi_of)):
                    pool.wait_ge(*m("hi_ready", n + 1))
                    pool.tensor_tensor(xs_lo[:, t, k0:k1, :], xs_tiles(t, k0, k1), part, ALU.subtract)\
                        .then_inc(m["lo_ready"], 1)
                pool.wait_ge(*m("key_ready", 1))
                kg = small[:, 0:8].rearrange("p (q t) -> p q t", q=4)
                for t in range(TT):
                    for q in range(4):
                        pool.tensor_scalar(diag[:, t, q, :], ident, kg[:, q, t:t + 1], None, ALU.mult)\
                            .then_inc(m["diag_ready"], 1)
                pool.wait_ge(*m("offs_ready", 1))
                pool.wait_ge(*m("sort_act", 4))
                pool.wait_ge(*m("sort_dve", 4))
                pool.wait_ge(*m("pad_zero", 1))

                def pair(i, s):
                    pool.wait_ge(*m("gu_ps", i - 2))
                    windows(i, 0, s, m["xg_ready"])

                for i in range(3):
                    windows(i, 0, i, m["xg_ready"])
                pair(3, 0)
                for_pairs_4_up(pool, pair)
                with pool.If(overflows(pool, l)):
                    pool.wait_ge(*m("gu_ps", PAIRS))

                    def step(i, r, n):
                        pool.wait_ge(ov[l]["free"], n + 1)
                        windows(i, r, 0, ov[l]["xg"])

                    overflow_steps(pool, step)
                    pool.wait_ge(ov[l]["xg"], 2 * PAIRS * (ROUNDS - 1))

            pool.memset(qz[DH:P, :, 0, :], 0.0).then_inc(zeroed, 1)
            pool.memset(qz[0:DH, :, 1, :], 0.0).then_inc(zeroed, 1)
            pool.wait_ge(*at[0]("o_sb", HEADS))
            pool.tensor_tensor(o_sq[:, 4:8, :], o_sb[:, 4:8, :], o_sb[:, 4:8, :], ALU.mult).then_inc(sq_ready, 1)
            pool.wait_ge(rs_ready, 1)
            rs = small[:, 32:48].rearrange("p (h q) -> p h q", h=HEADS)
            o4 = o_sb[:, 4:8, :].rearrange("p h (q d) -> p h q d", q=2)
            pool.tensor_tensor(o4, o4, rs[:, 4:8, :].unsqueeze(3).broadcast_to([P, 4, 2, P]), ALU.mult)\
                .then_inc(on_pool, 1)
            layer_norm(0)
            moe(0)
            pool.wait_ge(*mo[0]("xg_ready", 2 * PAIRS))
            pool.memset(qrz[ROPE:P, 0::2, :], 0.0).then_inc(mq["zeroed"], 1)
            pool.wait_ge(mq["zeroed"], 1)
            pool.memset(qrz[0:ROPE, 1::2, :], 0.0).then_inc(mq["zeroed"], 1)
            pool.wait_ge(mq["zeroed"], 2)
            layer_norm(1)
            pool.wait_ge(mq["qr_raw"], 2)
            rotate(pool, chain, qr_rot[:, 1, :, :], qr_raw[:, 1, :, :], 1, rope_tmp2, HEADS)\
                .then_inc(mq["qr_rot_pool"], 1)
            layer_norm(2)
            moe(1)
            layer_norm(3)


INPUTS = ["x", "diff_w_qkv", "diff_lambda", "diff_subln_g", "diff_w_o", "mla_w_kv_a", "mla_kv_norm_g", "mla_w_kv_b",
          "mla_w_q_a", "mla_q_norm_g", "mla_w_q_b", "mla_w_o", "router_w", "router_b", "moe_w_gate", "moe_w_up",
          "moe_w_down", "ln_g", "ln_b"]


def kernel(**inputs):
    import concourse.bacc as bacc
    from concourse.bass_utils import run_bass_kernel_spmd

    nc = bacc.Bacc("TRN2", target_bir_lowering=False, num_devices=1)
    arrays = {"in_shape_constants": shape_constants()}
    for name in INPUTS:
        arrays[f"in_{name}"] = np.ascontiguousarray(inputs[name])
    args = [nc.dram_tensor(n, a.shape, mybir.dt.from_np(a.dtype), kind="ExternalInput").ap()
            for n, a in arrays.items()]
    args.append(nc.dram_tensor("out_x", (1, SEQ, D), F32, kind="ExternalOutput").ap())
    build(nc, *args)
    r = run_bass_kernel_spmd(nc, [arrays], core_ids=[0])
    return r.results[0]["out_x"]
```

```python
import math
from contextlib import ExitStack

import numpy as np

import concourse.bass as bass
from concourse import mybir

F32 = mybir.dt.float32
F32R = mybir.dt.float32r
BF16 = mybir.dt.bfloat16
I32 = mybir.dt.int32
ALU = mybir.AluOpType
ACT = mybir.ActivationFunctionType
AX = mybir.AxisListType

P = 128
SEQ = 256
TT = SEQ // P
D = 1024
KD = D // P
CHUNK = 64
EPS = 1e-5
ALPHA = 4.0 ** 0.25
HEADS = 8
DH = 64
NOPE, ROPE, KVR, QR = 128, 64, 256, 384
LAMBDA_INIT = 0.8 - 0.6 * math.exp(-0.3 * 0)
MLA_SCALE = (NOPE + ROPE) ** -0.5
EXPERTS, GROUPS, FF = 32, 8, 256
PER_GROUP = EXPERTS // GROUPS
WIN = 64
ROUNDS = SEQ // WIN
PAIRS = EXPERTS // 2
SLOTS = 3
KEY = 1024
NSLOT = 2 * SEQ
BIG = 1e30
SORT_BANKS = (0, 1, 3, 4, 5, 6, 7, 2)
START_WAIT, NORM_WAIT, TOP_WAIT, SORT_WAIT = 12, (8, 4), 26, 6

GU = KD * FF
DN = (FF // P) * D
SLOT = 4 * GU + 2 * DN

CONST = {}
_at = 0
for _name, _n in (("ident", P), ("ones", P), ("dist", 3 * P), ("mask", 3 * P), ("cos", TT * 32), ("sin", TT * 32),
                  ("ecol", ROUNDS * PAIRS), ("rowc", 1), ("w8", GROUPS), ("w32", EXPERTS), ("key", EXPERTS)):
    CONST[_name] = (_at, _at + _n)
    _at += _n
CONSTS = _at


def shape_constants():
    c = np.zeros((P, CONSTS + P), np.float32)

    def put(name, a):
        lo, hi = CONST[name]
        c[:, lo:hi] = a

    p = np.arange(P)
    put("ident", np.eye(P))
    put("ones", 1.0)
    q0, q1, k = p, p + P, np.arange(SEQ)

    def blocked(f):
        return np.concatenate([f(q0[:, None], k[None, :P]), f(q1[:, None], k[None, :])], axis=1)

    seen = blocked(lambda q, k: (k // CHUNK) <= (q // CHUNK))
    put("dist", np.where(seen, blocked(lambda q, k: np.abs(q - k)), BIG))
    put("mask", np.where(seen, 0.0, -BIG))
    inv = (np.float32(10000.0) ** (-np.arange(0, ROPE, 2, dtype=np.float32) / np.float32(ROPE))).astype(np.float32)
    ang = (np.arange(SEQ, dtype=np.float32)[:, None] * inv[None, :]).astype(np.float32).astype(np.float64)
    put("cos", np.cos(ang).reshape(TT, P, 32).transpose(1, 0, 2).reshape(P, -1))
    put("sin", np.sin(ang).reshape(TT, P, 32).transpose(1, 0, 2).reshape(P, -1))
    put("ecol", (2 * KEY * np.arange(PAIRS)[None, :] + WIN * np.arange(ROUNDS)[:, None]).reshape(1, -1))
    put("rowc", (p % WIN + KEY * (p // WIN))[:, None])
    put("w8", GROUPS - np.arange(GROUPS))
    put("w32", EXPERTS - np.arange(EXPERTS))
    put("key", KEY * np.arange(EXPERTS))
    c[:, CONSTS:] = p[:, None] < p[None, :]
    return c


class Chain:

    def __init__(self, eng, sem):
        self.eng, self.sem, self.n = eng, sem, 0

    def __call__(self, ins):
        ins.then_inc(self.sem, 1)
        self.n += 1
        self.eng.wait_ge(self.sem, self.n)


class Phase:

    def __init__(self, sems, totals, layer):
        self.sems, self.totals, self.layer = sems, totals, layer

    def __getitem__(self, name):
        return self.sems[name]

    def __call__(self, name, n):
        return self.sems[name], n + self.layer * self.totals[name]


def build(nc, consts, x, diff_w_qkv, diff_lambda, diff_subln_g, diff_w_o, mla_w_kv_a, mla_kv_norm_g, mla_w_kv_b,
          mla_w_q_a, mla_q_norm_g, mla_w_q_b, mla_w_o, router_w, router_b, moe_w_gate, moe_w_up, moe_w_down,
          ln_g, ln_b, out):
    with ExitStack() as ctx:
        def sb(name, shape, dt=F32):
            return ctx.enter_context(nc.sbuf_tensor(name, shape, dt))

        def sb_and_rounded(name, shape):
            t = sb(name, shape)
            size = 4 * int(np.prod(shape[1:]))
            return t, nc.alloc_sbuf_tensor_at(name + "_rounded", shape, F32R, offset=nc.sbuf_base - size)

        def sem(name):
            return ctx.enter_context(nc.semaphore(name))

        ring, ring_r = zip(*(sb_and_rounded(f"ring{s}", [P, SLOT]) for s in range(SLOTS)))
        xs = sb("x_res", [P, TT, D])
        xT, xT_r = sb_and_rounded("x_T", [P, KD, SEQ])
        work, work_r = sb_and_rounded("work", [P, 8192])
        scratch = sb("scratch", [P, 1920])
        cst = sb("cst", [P, CONSTS])
        tri_b = sb("tri_b", [P, P], BF16)
        ones_b = sb("ones_b", [P, P], BF16)
        zeros_b = sb("zeros_b", [P, 512], BF16)
        rb = sb("router_b_sb", [P, EXPERTS])
        eps = sb("eps", [P, 1])
        subg = sb("subln_g_sb", [P, 1])
        qg = sb("q_norm_g_sb", [P, QR // P])
        kvg = sb("kv_norm_g_sb", [P, KVR // P])
        gcol = sb("ln_g_cols", [P, 3, KD])
        bcol = sb("ln_b_cols", [P, 3, KD])
        nlam = sb("neg_lambda", [P, 1])
        ln_stats = sb("ln_stats", [P, TT, 2, 6])
        ln_mv = sb("ln_mean_var", [P, TT, 2])
        ln_sd = sb("ln_sd", [P, TT])
        ln_rstd = sb("ln_rstd", [P, TT])
        ln_nb = sb("ln_neg_mean_rstd", [P, TT])
        small = sb("small", [P, 64])
        offs = sb("window_offsets", [P, ROUNDS * EXPERTS + 2], I32)

        ident, ones = (cst[:, slice(*CONST[n])] for n in ("ident", "ones"))
        dist, mask = (cst[:, slice(*CONST[n])] for n in ("dist", "mask"))
        cos, sin = (cst[:, slice(*CONST[n])].rearrange("p (t f) -> p t f", t=TT) for n in ("cos", "sin"))
        ecol, rowc = (cst[:, slice(*CONST[n])] for n in ("ecol", "rowc"))
        w8, w32, ekey = (cst[:, slice(*CONST[n])] for n in ("w8", "w32", "key"))
        tri_f = work[:, 8064:8192]

        psum = ctx.enter_context(nc.psum_tensor("psum", [P, 8, 512], F32))

        def qkv_chunk(r, c):
            a = (c % 3) * 4096
            return r[2 - c // 3][:, a:a + 4096].rearrange("p (k n) -> p k n", k=KD)

        w_hi = ring_r[0][:, 0:8192].rearrange("p (b k n) -> p b k n", b=2, k=KD)
        x_lo = ring_r[0][:, 8192:10240].rearrange("p (k t) -> p k t", k=KD)
        wo_a, wo_b = 0, 4096

        def wo(r, at_, h):
            return r[2][:, at_ + h * D:at_ + (h + 1) * D]

        def wo_hi(at_, h):
            a = (8192 if h < 4 or at_ == wo_a else 0) + (h % 4) * D
            return ring_r[1 + h // 4][:, a:a + D]

        qz = work[:, 0:4096].rearrange("p (h c t) -> p h c t", h=HEADS, c=2)
        kT = work[:, 4096:6144].rearrange("p (h t) -> p h t", h=HEADS)
        v = work[:, 6144:8192].rearrange("p (t n) -> p t n", t=TT)
        o_sb = qz[:, :, 0, :]
        o_sq = qz[:, :, 1, :]
        oT = xT_r
        o_lo_a = work_r[:, 0:4096].rearrange("p (h c t) -> p h c t", h=HEADS, c=2)[:, :, 1, :]
        o_lo_b = work_r[:, 0:2048].rearrange("p (h t) -> p h t", h=HEADS)
        x_flat = xT.rearrange("p k t -> p (k t)")
        lg = [a.rearrange("p (c n) -> p c n", c=2) for a in (
            scratch[:, 0:768], scratch[:, 768:1536], x_flat[:, 0:768], x_flat[:, 768:1536])]
        aT = [scratch[:, 1536:1920], x_flat[:, 1536:1920]]
        lam_in = scratch[:, 0:256].rearrange("p (i d) -> p i d", i=4)
        lam_prod = scratch[:, 256:384].rearrange("p (i d) -> p i d", i=2)
        lam_dot = small[:, 28:30]
        kva = ring[1][:, 0:2560].rearrange("p (k n) -> p k n", k=KD)
        qa = ring[1][:, 2560:5632].rearrange("p (k n) -> p k n", k=KD)
        qb = ring[1][:, 5632:10240].rearrange("p (k n) -> p k n", k=QR // P)
        kvb = ring[2][:, 0:4096].rearrange("p (k n) -> p k n", k=KVR // P)
        qnT = work[:, 0:2048].rearrange("p (h t) -> p h t", h=HEADS)
        qrz = work[:, 2048:4096].rearrange("p (h t) -> p h t", h=HEADS)
        knT = kT
        c_q = work[:, 6144:6912].rearrange("p (t n) -> p t n", t=TT)
        c_kv = work[:, 6912:7424].rearrange("p (t n) -> p t n", t=TT)
        kr_raw = work[:, 7424:7552].rearrange("p (t n) -> p t n", t=TT)
        kr2 = work[:, 7552:7808].rearrange("p (t n) -> p t n", t=TT)
        sq_junk = work[:, 7808:8192]
        qr_raw = xT[:, 0:4, :].rearrange("p a b -> p (a b)").rearrange("p (t h d) -> p t h d", t=TT, h=HEADS)
        qr_rot = xT[:, 4:8, :].rearrange("p a b -> p (a b)").rearrange("p (t h d) -> p t h d", t=TT, h=HEADS)
        cqT = scratch[:, 0:768].rearrange("p (k t) -> p k t", k=QR // P)
        ckvT = scratch[:, 768:1280].rearrange("p (k t) -> p k t", k=KVR // P)
        krT2 = scratch[:, 1280:1536]
        rope_tmp = scratch[:, 1536:1792].rearrange("p (h d) -> p h d", h=HEADS)
        rope_tmp2 = sq_junk[:, 0:256].rearrange("p (h d) -> p h d", h=HEADS)
        mlg = [scratch[:, 0:384], scratch[:, 384:768], scratch[:, 1536:1920]]
        pT = [scratch[:, 768:1152], ring[2][:, 0:384]]
        gb = [a.rearrange("p (s n) -> p s n", s=2) for a in (
            work[:, 4096:6144], ring[1][:, 10240:SLOT], work[:, 4096:6144], work[:, 0:2048])]
        XW = NSLOT + WIN
        xsT = work[:, 0:KD * XW].rearrange("p (k s) -> p k s", k=KD)
        xg = work[:, KD * XW:KD * XW + SLOTS * KD * P].rearrange("p (b k c) -> p b k c", b=SLOTS, k=KD)
        top = work[:, KD * XW + 2 * KD * P:KD * XW + 3 * KD * P]
        rw = work[:, 7680:7936].rearrange("p (k e) -> p k e", k=KD)
        hi_parts = [xT_r[:, 4:8, :].rearrange("p a b -> p (a b)").rearrange("p (k n) -> p k n", k=KD),
                    work_r[:, 7680:8192].rearrange("p (k n) -> p k n", k=4),
                    work_r[:, 7 * XW:7 * XW + NSLOT].rearrange("p (k n) -> p k n", k=4)]
        hi_of = [(0, 0, KD), (1, 0, 4), (1, 4, KD)]
        xs_lo = work_r[:, KD * XW:KD * XW + TT * D].rearrange("p (t k n) -> p t k n", t=TT, k=KD)

        def xs_tiles(t, k0, k1):
            return xs[:, t, :].rearrange("p (n k) -> p k n", k=KD)[:, k0:k1, :]

        def xs_hi(t, k):
            part, first = (0, 0) if t == 0 else (1 + k // 4, 4 * (k // 4))
            return hi_parts[part][:, k - first, :]

        onehot_r = xT_r[:, 0:4, :].rearrange("p a b -> p (a b)").rearrange("p (t s) -> p t s", t=TT)
        y_sb = xT[:, 0:4, :].rearrange("p a b -> p (a b)")
        key_row = xT[:, 4:6, :]
        gate_row = xT[:, 6:8, :]
        diag = scratch[:, 768:1792].rearrange("p (t q n) -> p t q n", t=TT, q=4)
        logit_T = scratch[0:EXPERTS, 0:256]
        iota = scratch[:, 256:768]
        comb = scratch[:, 0:768].rearrange("p (b t) -> p b t", b=SLOTS)
        act_s = scratch[:, 768:1024]
        h_sb = scratch[:, 1024:1280]
        hT = scratch[:, 1280:1536].rearrange("p (k c) -> p k c", k=FF // P)
        g_tmp = scratch[:, 1536:1792]

        def slot_gu(s, j):
            a = j * 2 * GU
            return ring[s][:, a:a + 2 * GU].rearrange("p (u k f) -> p u k f", u=2, k=KD)

        def slot_dn(s, j):
            a = 4 * GU + j * DN
            return ring[s][:, a:a + DN].rearrange("p (k n) -> p k n", k=FF // P)

        ld_x = [sem(f"ld_x{t}") for t in range(TT)]
        MISC = 7
        ld_ident, ld_cst, ld_misc, ld_lam = sem("ld_ident"), sem("ld_cst"), sem("ld_misc"), sem("ld_lam")
        x_hi_ready, w_hi_ready, w_lo_ready, w_pool_ready = (
            sem(n) for n in ("x_hi_ready", "w_hi_ready", "w_lo_ready", "w_pool_ready"))
        ld_rw = [sem(f"ld_router{l}") for l in range(2)]
        ld_qkv = [sem(f"ld_qkv{c}") for c in range(6)]
        ld_qkv0b = sem("ld_qkv0b")
        ld_wo_a = sem("ld_wo_a")
        ld_kva, ld_qa, ld_qb, ld_kvb, ld_wo_b = (sem(n) for n in ("ld_kva", "ld_qa", "ld_qb", "ld_kvb", "ld_wo_b"))
        sems = {"gb": sem("ld_ln")}
        ld_gb = [Phase(sems, {"gb": 32}, n) for n in range(4)]
        cast_ready, zeroed, lam_ready, lam_exp = (sem(n) for n in ("cast_ready", "zeroed", "lam_ready", "lam_exp"))
        totals = {"ps": 4, "sb": KD}
        sems = {n: sem("xt_" + n) for n in totals}
        xt = [Phase(sems, totals, n) for n in range(4)]
        qkv_ps, qkv_act, qkv_dve = sem("qkv_ps"), sem("qkv_act"), sem("qkv_dve")
        totals = {"sc_ps": 2 * HEADS, "sc_read": 2 * HEADS, "mx_ready": 2 * HEADS, "e_ready": 4 * HEADS,
                  "r_ready": HEADS, "e1_scaled": 2 * HEADS, "p_ready": 2 * HEADS, "pt_ps": HEADS, "pt_sb": HEADS,
                  "o_ps": HEADS, "o_sb": HEADS}
        sems = {n: sem(n) for n in totals}
        at = [Phase(sems, totals, l) for l in range(2)]
        sq_ready, ss_ready, sd_ready, rs_ready = sem("sq_ready"), sem("ss_ready"), sem("sd_ready"), sem("rs_ready")
        on_dve, on_pool, ot_ps, ot_sb = sem("on_dve"), sem("on_pool"), sem("ot_ps"), sem("ot_sb")
        o_lo_ready = sem("o_lo_ready")
        wo_ps = [sem(f"wo_ps{l}") for l in range(2)]
        totals = {"var": TT, "sd": TT, "rstd": TT, "norm": TT + 1, "x_dve": 1, "x_pool": 1}
        sems = {n: sem("ln_" + n) for n in totals}
        ln = [Phase(sems, totals, n) for n in range(4)]
        mq = {n: sem("mla_" + n) for n in (
            "a_ps", "sd", "rstd", "c_ready", "kr_rot", "ct_ps", "ct_sb", "qr_ps", "qr_raw", "qr_rot_dve",
            "qr_rot_pool", "b_ps", "b_act", "b_dve", "qt_ps", "qt_sb", "krt_ps", "krt_sb", "zeroed")}
        totals = {"lgt_ps": 1, "lgt_sb": 1, "lg_ps": 1, "score": 1, "m_ready": 1, "cnt_ps": 1, "cnt_sb": 1,
                  "rank_ps": 1, "offs_ready": 1,
                  "iota_ready": 1, "hi_ready": 3, "lo_ready": 3, "hot_ready": TT, "pad_zero": 1, "key_ready": 1, "sort_ps": KD, "sort_act": KD // 2,
                  "sort_dve": KD // 2, "diag_ready": 4 * TT, "row_ps": 1, "row_sb_a": TT, "row_sb_d": TT,
                  "xg0_ready": 2, "gate0_ps": 1, "xg_ready": 2 * PAIRS - 2, "gu_ps": PAIRS, "s_ready": PAIRS, "h_ready": PAIRS, "ht_ps": PAIRS,
                  "ht_sb": PAIRS, "y_ps": PAIRS, "y_act": PAIRS, "y_dve": PAIRS, "g_part": 2 * PAIRS,
                  "g_ready": PAIRS, "c_ps": PAIRS, "sum_ps": TT}
        sems = {n: sem("moe_" + n) for n in totals}
        mo = [Phase(sems, totals, l) for l in range(2)]
        uses = [len(range(s, PAIRS, SLOTS)) for s in range(SLOTS)]
        sems = [{n: sem(f"ring_{n}{s}") for n in ("gu", "dn")} for s in range(SLOTS)]
        rings = [[Phase(sems[s], {"gu": 64 * uses[s], "dn": 32 * uses[s]}, l) for s in range(SLOTS)]
                 for l in range(2)]
        names = ("w", "xg", "gu", "s", "h", "ht_ps", "ht_sb", "y_ps", "y_act", "y_dve", "g_part", "g", "free")
        ov = [{n: sem(f"ov_{n}{l}") for n in names} for l in range(2)]
        out_done = sem("out_done")
        dve_chain, act_chain, pool_chain = sem("dve_chain"), sem("act_chain"), sem("pool_chain")

        def for_pairs_4_up(eng, body):
            with eng.Fori(0, (PAIRS - 4) // SLOTS) as it:
                for j in range(SLOTS):
                    body(it * SLOTS + (4 + j), (4 + j) % SLOTS)

        def for_pairs_1_up(eng, body):
            with eng.Fori(0, (PAIRS - 1) // SLOTS) as it:
                for j in range(SLOTS):
                    body(it * SLOTS + (1 + j), (1 + j) % SLOTS)

        def overflow_steps(eng, body):
            with eng.Fori(1, ROUNDS) as r:
                with eng.Fori(0, PAIRS) as i:
                    body(i, r, (r - 1) * PAIRS + i)

        def overflows(eng, l):
            eng.wait_ge(*mo[l]("offs_ready", 1))
            n = eng.value_load(offs[0:1, ROUNDS * EXPERTS:ROUNDS * EXPERTS + 1], min_val=0, max_val=SEQ)
            return n > WIN

        def routing():
            c, at_ = {}, 0
            for name, n in (("score", 64), ("sel", 64), ("mx2", 32), ("sm2", 32), ("t1", 16), ("t2", 16),
                            ("gs", 16), ("gmax", 2), ("gkey", 16), ("gmask", 16), ("masked", 64), ("m1", 2),
                            ("e1", 64), ("k1", 2), ("oh", 128), ("prod", 128), ("cnt", 32), ("pre", 64),
                            ("rank", 64), ("chosen", 32), ("cnt_col", 64)):
                c[name] = top[:, at_:at_ + n]
                at_ += n
            c["cnt_col"] = c["cnt_col"].bitcast(BF16)[0:EXPERTS, :]
            c["chosen"] = c["chosen"].bitcast(BF16).rearrange("p (t e) -> p t e", t=TT)
            return c

        def rotate(eng, link, dst, src, t, tmp, heads):
            shape = [P, heads, 32]
            c = cos[:, t, :].unsqueeze(1).broadcast_to(shape)
            s = sin[:, t, :].unsqueeze(1).broadcast_to(shape)
            lo, hi = slice(0, 32), slice(32, 64)
            link(eng.tensor_tensor(dst[:, :, lo], src[:, :, lo], c, ALU.mult))
            link(eng.tensor_tensor(tmp, src[:, :, hi], s, ALU.mult))
            link(eng.tensor_tensor(dst[:, :, lo], dst[:, :, lo], tmp, ALU.subtract))
            link(eng.tensor_tensor(dst[:, :, hi], src[:, :, hi], c, ALU.mult))
            link(eng.tensor_tensor(tmp, src[:, :, lo], s, ALU.mult))
            return eng.tensor_tensor(dst[:, :, hi], dst[:, :, hi], tmp, ALU.add)

        block = ctx.enter_context(nc.Block())

        @block.sync
        def _(sp):
            sp.dma_start(ident, consts[:, 0:P]).then_inc(ld_ident, 16)
            for t in range(TT):
                sp.dma_start(xs[:, t, :], x[0, t * P:(t + 1) * P, :]).then_inc(ld_x[t], 16)
            wq = diff_w_qkv[0].rearrange("(p k) n -> p k n", k=KD)
            for half, ld in enumerate((ld_qkv[0], ld_qkv0b)):
                cols = slice(half * 256, (half + 1) * 256)
                sp.dma_start(qkv_chunk(ring, 0)[:, :, cols], wq[:, :, cols]).then_inc(ld, 16)
            for c in range(1, 6):
                sp.dma_start(qkv_chunk(ring, c), wq[:, :, c * 512:(c + 1) * 512]).then_inc(ld_qkv[c], 16)
                if c == 1:
                    sp.dma_start(cst[:, P:], consts[:, P:CONSTS]).then_inc(ld_cst, 16)

            def load_wo(w, at_, ld):
                sp.dma_start(ring[2][:, at_:at_ + HEADS * D].rearrange("p (h n) -> p h n", h=HEADS),
                             w[0].rearrange("(h p) n -> p h n", p=P)).then_inc(ld, 16)

            sp.wait_ge(qkv_ps, 4)
            load_wo(diff_w_o, wo_a, ld_wo_a)

            def load_gate_up(l, i, s, which=(0, 1)):
                for u in which:
                    for j in range(2):
                        sp.dma_start(slot_gu(s, j)[:, u, :, :], (moe_w_gate, moe_w_up)[u][l, i * 2 + j]
                                     .rearrange("(p k) f -> p k f", k=KD)).then_inc(rings[l][s]["gu"], 16)

            def load_down(l, i, s):
                for j in range(2):
                    sp.dma_start(slot_dn(s, j), moe_w_down[l, i * 2 + j].rearrange("(k p) n -> p k n", p=P))\
                      .then_inc(rings[l][s]["dn"], 16)

            def load_pair(l, i, s):
                load_gate_up(l, i, s)
                load_down(l, i, s)

            def load_ln(n):
                sp.dma_start(gb[n][:, 0, :], ln_g[n // 2, n % 2].partition_broadcast(P)).then_inc(ld_gb[n]["gb"], 16)
                sp.dma_start(gb[n][:, 1, :], ln_b[n // 2, n % 2].partition_broadcast(P)).then_inc(ld_gb[n]["gb"], 16)

            def load_router(l):
                sp.wait_ge(*at[l]("o_ps", HEADS))
                sp.dma_start(rw, router_w.rearrange("(p k) n -> p k n", k=KD)).then_inc(ld_rw[l], 16)

            def moe(l):
                def reload(i, s):
                    sp.wait_ge(*mo[l]("gu_ps", i - 2))
                    load_gate_up(l, i, s)
                    sp.wait_ge(*mo[l]("y_ps", i - 2))
                    load_down(l, i, s)

                sp.wait_ge(*mo[l]("gate0_ps", 1))
                load_gate_up(l, 3, 0, (0,))
                sp.wait_ge(*mo[l]("gu_ps", 1))
                load_gate_up(l, 3, 0, (1,))
                sp.wait_ge(*mo[l]("y_ps", 1))
                load_down(l, 3, 0)
                for_pairs_4_up(sp, reload)

            def overflow(l):
                with sp.If(overflows(sp, l)):
                    sp.wait_ge(*mo[l]("y_ps", PAIRS))

                    def step(i, r, n):
                        sp.wait_ge(ov[l]["free"], n + 1)
                        for j in range(2):
                            for u, w in enumerate((moe_w_gate, moe_w_up)):
                                sp.dma_start(slot_gu(0, j)[:, u, :, :],
                                             w[l, i * 2 + j].rearrange("(p k) f -> p k f", k=KD))\
                                  .then_inc(ov[l]["w"], 16)
                            sp.dma_start(slot_dn(0, j), moe_w_down[l, i * 2 + j].rearrange("(k p) n -> p k n", p=P))\
                              .then_inc(ov[l]["w"], 16)

                    overflow_steps(sp, step)
                    sp.wait_ge(ov[l]["y_ps"], PAIRS * (ROUNDS - 1))

            sp.wait_ge(qkv_ps, 12)
            load_pair(0, 0, 0)
            load_gate_up(0, 1, 1)
            sp.wait_ge(*at[0]("sc_ps", 2 * HEADS))
            load_ln(0)
            load_router(0)
            sp.wait_ge(wo_ps[0], 4)
            load_down(0, 1, 1)
            load_pair(0, 2, 2)
            moe(0)
            sp.wait_ge(*mo[0]("gu_ps", 14))
            sp.dma_start(qa, mla_w_q_a[0].rearrange("(p k) n -> p k n", k=KD)).then_inc(ld_qa, 16)
            sp.dma_start(kva, mla_w_kv_a.rearrange("(p k) n -> p k n", k=KD)).then_inc(ld_kva, 16)
            sp.wait_ge(*mo[0]("y_ps", 14))
            load_ln(1)
            sp.dma_start(qb, mla_w_q_b[0].rearrange("(k p) n -> p k n", p=P)).then_inc(ld_qb, 16)
            sp.wait_ge(*mo[0]("y_ps", 15))
            sp.dma_start(kvb, mla_w_kv_b.rearrange("(k p) n -> p k n", p=P)).then_inc(ld_kvb, 16)
            load_wo(mla_w_o, wo_b, ld_wo_b)
            overflow(0)
            sp.wait_ge(*mo[0]("y_ps", PAIRS))
            load_pair(1, 0, 0)
            sp.wait_ge(mq["b_ps"], 4)
            sp.wait_ge(*ln[1]("x_dve", 1))
            sp.wait_ge(*ln[1]("x_pool", 1))
            load_gate_up(1, 1, 1)
            sp.wait_ge(*at[1]("sc_ps", HEADS))
            load_ln(2)
            load_router(1)
            sp.wait_ge(wo_ps[1], 4)
            load_down(1, 1, 1)
            load_pair(1, 2, 2)
            moe(1)
            overflow(1)
            sp.wait_ge(*mo[1]("xg_ready", 2 * PAIRS - 2))
            load_ln(3)
            for t in range(TT):
                sp.wait_ge(*ln[3](("x_dve", "x_pool")[t], 1))
                sp.dma_start(out[0, t * P:(t + 1) * P, :], xs[:, t, :]).then_inc(out_done, 16)
            sp.wait_ge(out_done, 16 * TT)

        @block.tensor
        def _(pe):
            def mm(dst, lhsT, rhs, start, stop):
                return pe.matmul(dst, lhsT, rhs, start=start, stop=stop, skip_group_check=True)

            def keep_clock(n, bank=4):
                for _ in range(n):
                    mm(psum[:, bank, :], zeros_b[:, 0:P], zeros_b[:, :], True, True)

            def transpose_x(n):
                for t in range(TT):
                    if n:
                        keep_clock(NORM_WAIT[t], (4, 0)[t])
                        pe.wait_ge(*ln[n - 1]("norm", (1, 3)[t]))
                    for k in range(KD):
                        at_ = (k % 2) * SEQ + t * P
                        last = pe.transpose(psum[:, 4 + k // 2, at_:at_ + P], xs[:, t, k::KD], ident)
                        if t and k % 2:
                            last.then_inc(xt[n]["ps"], 1)
                pe.wait_ge(*xt[n]("sb", KD))

            def products(dst, lhsT, rhs, first, last):
                (a_hi, a_lo), (b_hi, b_lo) = lhsT, rhs
                mm(dst, a_hi, b_hi, first, False)
                mm(dst, a_hi, b_lo, False, False)
                return mm(dst, a_lo, b_hi, False, last)

            def out_projection(l, w, o_lo):
                for t in range(TT):
                    tok = slice(t * P, (t + 1) * P)
                    for c in range(2):
                        cols = slice(c * 512, (c + 1) * 512)
                        for h in range(HEADS):
                            if t == 0 and c == 0 and h < 4:
                                pe.wait_ge(w_pool_ready, 4 * l + h + 1)
                            if t == 0 and c == 0 and h >= 4:
                                pe.wait_ge(w_lo_ready, 24 + 4 * l + h - 3)
                            last = products(psum[:, 2 * t + c, :], (oT[:, h, tok], o_lo[:, h, tok]),
                                            (wo_hi(w, h)[:, cols], wo(ring_r, w, h)[:, cols]), h == 0, h == HEADS - 1)
                        last.then_inc(wo_ps[l], 1)

            def diff_attention():
                pe.wait_ge(cast_ready, 1)
                keep_clock(START_WAIT)
                pe.wait_ge(ld_ident, 16)
                for t in range(TT):
                    pe.wait_ge(ld_x[t], 16)
                transpose_x(0)
                g = 0
                for c in range(4):
                    for m in range(4):
                        pe.wait_ge(w_lo_ready, 4 * c + m + 1)
                        cols = slice(m * P, (m + 1) * P)
                        for k in range(KD):
                            last = products(psum[:, g % 8, (m % 2) * SEQ:(m % 2 + 1) * SEQ],
                                            (w_hi[:, c % 2, k, cols], qkv_chunk(ring_r, c)[:, k, cols]),
                                            (xT_r[:, k, :], x_lo[:, k, :]), k == 0, k == KD - 1)
                        if m % 2:
                            last.then_inc(qkv_ps, 1)
                            g += 1
                for c in range(4, 6):
                    pe.wait_ge(w_lo_ready, 4 * c + 4)
                    for t in range(TT):
                        pe.wait_ge((qkv_act, qkv_dve)[g % 2], 2 * ((g - 8) // 2 + 1))
                        tok = slice(t * P, (t + 1) * P)
                        for k in range(KD):
                            last = products(psum[:, g % 8, :], (xT_r[:, k, tok], x_lo[:, k, tok]),
                                            (w_hi[:, c % 2, k, :], qkv_chunk(ring_r, c)[:, k, :]), k == 0, k == KD - 1)
                        last.then_inc(qkv_ps, 1)
                        g += 1
                s = at[0]
                pe.wait_ge(qkv_act, 8)
                pe.wait_ge(qkv_dve, 8)
                pe.wait_ge(zeroed, 2)

                def scores(h):
                    if h >= 2:
                        pe.wait_ge(*s("sc_read", 2 * (h - 1)))
                    for c in range(2):
                        bank = psum[:, 2 * (h % 2) + c, :]
                        mm(bank[:, 0:P], qz[:, h, c, 0:P], kT[:, h, 0:P], True, True)
                        mm(bank[:, P:3 * P], qz[:, h, c, P:SEQ], kT[:, h, :], True, True).then_inc(s["sc_ps"], 1)

                def transposes(h):
                    pe.wait_ge(*s("p_ready", 2 * (h + 1)))
                    if h >= 2:
                        pe.wait_ge(*s("pt_sb", h - 1))
                    for b in range(3):
                        last = pe.transpose(psum[:, 4 + h % 2, b * P:(b + 1) * P], lg[h % 4][:, 0, b * P:(b + 1) * P],
                                            ident)
                    last.then_inc(s["pt_ps"], 1)

                def values(h):
                    pe.wait_ge(*s("pt_sb", h + 1))
                    if h >= 2:
                        pe.wait_ge(*s("o_sb", h - 1))
                    bank = psum[:, 6 + h % 2, :]
                    hv = slice(h * P, (h + 1) * P)
                    a = aT[h % 2]
                    mm(bank[:, 0:P], a[:, 0:P], v[:, 0, hv], True, True)
                    mm(bank[:, P:SEQ], a[:, P:2 * P], v[:, 0, hv], True, False)
                    mm(bank[:, P:SEQ], a[:, 2 * P:3 * P], v[:, 1, hv], False, True).then_inc(s["o_ps"], 1)

                for h in range(3):
                    scores(h)
                for h in range(HEADS):
                    if h + 3 < HEADS:
                        scores(h + 3)
                    transposes(h)
                    if h >= 1:
                        values(h - 1)
                values(HEADS - 1)
                keep_clock(NORM_WAIT[0], 0)
                for b in range(4):
                    pe.wait_ge(on_dve, min(b + 1, 2))
                    if b >= 2:
                        pe.wait_ge(on_pool, 1)
                    for h in (2 * b, 2 * b + 1):
                        for t in range(TT):
                            a = (h % 2) * SEQ + t * P
                            last = pe.transpose(psum[:, 4 + b, a:a + P], o_sb[:, h, t * P:(t + 1) * P], ident)
                    last.then_inc(ot_ps, 1)
                keep_clock(NORM_WAIT[1], 0)
                pe.wait_ge(ot_sb, 4)
                out_projection(0, wo_a, o_lo_a)

            def mla_attention():
                transpose_x(2)
                pe.wait_ge(ld_qa, 16)
                for t in range(TT):
                    for k in range(KD):
                        last = mm(psum[:, 2 + t, 0:QR], xT[:, k, t * P:(t + 1) * P], qa[:, k, :], k == 0, k == KD - 1)
                    last.then_inc(mq["a_ps"], 1)
                pe.wait_ge(ld_kva, 16)
                for t in range(TT):
                    for k in range(KD):
                        last = mm(psum[:, t, 0:KVR + ROPE], xT[:, k, t * P:(t + 1) * P], kva[:, k, :],
                                  k == 0, k == KD - 1)
                    last.then_inc(mq["a_ps"], 1)
                pe.wait_ge(mq["c_ready"], 2)
                for k in range(QR // P):
                    for t in range(TT):
                        a = (k % 2) * SEQ + t * P
                        last = pe.transpose(psum[:, 4 + k // 2, a:a + P], c_q[:, t, k * P:(k + 1) * P], ident)
                last.then_inc(mq["ct_ps"], 1)
                pe.wait_ge(mq["c_ready"], 4)
                for k in range(KVR // P):
                    for t in range(TT):
                        a = k * SEQ + t * P
                        last = pe.transpose(psum[:, 6, a:a + P], c_kv[:, t, k * P:(k + 1) * P], ident)
                last.then_inc(mq["ct_ps"], 1)
                pe.wait_ge(ld_qb, 16)
                pe.wait_ge(mq["ct_sb"], 5)
                qb_h = qb.rearrange("p k (h n) -> p k h n", h=HEADS)
                for t in range(TT):
                    for k in range(QR // P):
                        last = mm(psum[:, 2 + t, :], cqT[:, k, t * P:(t + 1) * P], qb_h[:, k, :, NOPE:],
                                  k == 0, k == QR // P - 1)
                    last.then_inc(mq["qr_ps"], 1)
                banks = [4, 5, 0, 1, 6, 7, 4, 5, 0, 1, 2, 3]
                kvb_h = kvb.rearrange("p k (h n) -> p k h n", h=HEADS)
                for g in range(12):
                    if 6 <= g < 10:
                        pe.wait_ge((mq["b_act"], mq["b_dve"])[g % 2], (g - 6) // 2 + 1)
                    if g >= 10:
                        pe.wait_ge(mq["qr_raw"], 2)
                    if g == 4:
                        pe.wait_ge(ld_kvb, 16)
                    if g < 8:
                        w, src, n = (qb_h, cqT, QR // P) if g < 4 else (kvb_h, ckvT, KVR // P)
                        for h in (2 * (g % 4), 2 * (g % 4) + 1):
                            for k in range(n):
                                last = mm(psum[:, banks[g], (h % 2) * SEQ:(h % 2 + 1) * SEQ], w[:, k, h, 0:NOPE],
                                          src[:, k, :], k == 0, k == n - 1)
                    else:
                        t, half = (g - 8) // 2, (g - 8) % 2
                        for k in range(KVR // P):
                            last = mm(psum[:, banks[g], :], ckvT[:, k, t * P:(t + 1) * P],
                                      kvb_h[:, k, 4 * half:4 * half + 4, NOPE:], k == 0, k == KVR // P - 1)
                    last.then_inc(mq["b_ps"], 1)
                pe.wait_ge(mq["kr_rot"], 1)
                pe.wait_ge(mq["b_act"], 4)
                pe.wait_ge(mq["b_dve"], 4)
                for t in range(TT):
                    last = pe.transpose(psum[:, 6, t * P:(t + 1) * P], kr2[:, t, :], ident)
                last.then_inc(mq["krt_ps"], 1)
                pe.wait_ge(mq["qr_rot_dve"], 1)
                pe.wait_ge(mq["qr_rot_pool"], 1)
                for b in range(2):
                    for hp in (2 * b, 2 * b + 1):
                        for t in range(TT):
                            a = (hp % 2) * SEQ + t * P
                            last = pe.transpose(psum[:, (7, 4)[b], a:a + P],
                                                qr_rot[:, t, 2 * hp:2 * hp + 2, :].rearrange("p h d -> p (h d)"), ident)
                    last.then_inc(mq["qt_ps"], 1)
                s = at[1]
                pe.wait_ge(mq["b_act"], 6)
                pe.wait_ge(mq["b_dve"], 6)
                pe.wait_ge(mq["krt_sb"], 1)
                pe.wait_ge(mq["zeroed"], 2)
                pe.wait_ge(mq["qt_sb"], 4)

                def scores(h):
                    if h >= 2:
                        pe.wait_ge(*s("sc_read", h - 1))
                    bank = psum[:, h % 2, :]
                    mm(bank[:, 0:P], qnT[:, h, 0:P], knT[:, h, 0:P], True, False)
                    mm(bank[:, 0:P], qrz[:, h, 0:P], krT2[:, 0:P], False, True)
                    mm(bank[:, P:3 * P], qnT[:, h, P:SEQ], knT[:, h, :], True, False)
                    mm(bank[:, P:3 * P], qrz[:, h, P:SEQ], krT2, False, True).then_inc(s["sc_ps"], 1)

                def transposes(h):
                    pe.wait_ge(*s("p_ready", 2 * (h + 1)))
                    if h >= 2:
                        pe.wait_ge(*s("pt_sb", h - 1))
                    for b in range(3):
                        last = pe.transpose(psum[:, 2 + h % 2, b * P:(b + 1) * P], mlg[h % 3][:, b * P:(b + 1) * P],
                                            ident)
                    last.then_inc(s["pt_ps"], 1)

                def values(h):
                    pe.wait_ge(*s("pt_sb", h + 1))
                    if h >= 2:
                        pe.wait_ge(o_lo_ready, h - 1)
                    bank = psum[:, 4 + h % 2, :]
                    hv = slice(h * P, (h + 1) * P)
                    mm(bank[:, 0:SEQ], v[:, 0, hv], pT[h % 2][:, 0:SEQ], True, False)
                    mm(bank[:, P:SEQ], v[:, 1, hv], pT[h % 2][:, SEQ:3 * P], False, True).then_inc(s["o_ps"], 1)

                for h in range(3):
                    scores(h)
                for h in range(HEADS):
                    if h + 3 < HEADS:
                        scores(h + 3)
                    transposes(h)
                    if h >= 1:
                        values(h - 1)
                values(HEADS - 1)
                pe.wait_ge(o_lo_ready, HEADS)
                out_projection(1, wo_b, o_lo_b)

            def moe(l):
                m = mo[l]
                transpose_x(2 * l + 1)
                pe.wait_ge(ld_rw[l], 16)
                for k in range(KD):
                    last = mm(psum[0:EXPERTS, 0, 0:SEQ], rw[:, k, :], xT[:, k, :], k == 0, k == KD - 1)
                last.then_inc(m["lgt_ps"], 1)
                pe.wait_ge(*m("lgt_sb", 1))
                for t in range(TT):
                    last = pe.transpose(psum[:, 1, t * EXPERTS:(t + 1) * EXPERTS], logit_T[:, t * P:(t + 1) * P],
                                        ident[0:EXPERTS, 0:EXPERTS])
                last.then_inc(m["lg_ps"], 1)
                pe.wait_ge(cast_ready, 3)
                keep_clock(TOP_WAIT)
                pe.wait_ge(*m("m_ready", 1))
                chosen = routing()["chosen"]
                count = psum[0:EXPERTS, 3, 0:P]
                for t in range(TT):
                    last = mm(count, chosen[:, t, :], ones_b[:, :], t == 0, t == TT - 1)
                last.then_inc(m["cnt_ps"], 1)
                rank = psum[:, 2, :]
                mm(rank[:, 0:32], tri_b[:, :], chosen[:, 0, :], True, True)
                mm(rank[:, 32:64], tri_b[:, :], chosen[:, 1, :], True, False)
                mm(rank[:, 32:64], ones_b[:, :], chosen[:, 0, :], False, True)
                mm(rank[:, 128:160], ones_b[:, :], chosen[:, 0, :], True, False)
                mm(rank[:, 128:160], ones_b[:, :], chosen[:, 1, :], False, True)
                pe.wait_ge(*m("cnt_sb", 1))
                count, before = routing()["cnt_col"], tri_b[0:EXPERTS, 0:EXPERTS]
                mm(rank[:, 160:192], count, before, True, True)
                mm(rank[:, 64:96], count, before, True, False)
                mm(rank[:, 64:96], tri_b[:, :], chosen[:, 0, :], False, True)
                mm(rank[:, 96:128], count, before, True, False)
                mm(rank[:, 96:128], tri_b[:, :], chosen[:, 1, :], False, False)
                mm(rank[:, 96:128], ones_b[:, :], chosen[:, 0, :], False, True).then_inc(m["rank_ps"], 1)
                keep_clock(SORT_WAIT)
                pe.wait_ge(*m("hi_ready", 3))
                pe.wait_ge(*m("lo_ready", 3))
                for t in range(TT):
                    pe.wait_ge(*m("hot_ready", t + 1))
                    for k in range(KD):
                        if t == 0 and k == KD - 1:
                            pe.wait_ge(*m("offs_ready", 1))
                        for half, part in enumerate((xs_hi(t, k), xs_lo[:, t, k, :])):
                            last = mm(psum[:, SORT_BANKS[k], :], part, onehot_r[:, t, :],
                                      t == 0 and half == 0, t == TT - 1 and half == 1)
                        if t == TT - 1:
                            last.then_inc(m["sort_ps"], 1)
                pe.wait_ge(*m("diag_ready", 8))
                pe.wait_ge(*m("sort_act", 1))
                pe.wait_ge(*m("sort_dve", 1))
                for t in range(TT):
                    last = mm(psum[:, t, :], ones, diag[:, t, :, :].rearrange("p q n -> p (q n)"), True, True)
                last.then_inc(m["row_ps"], 1)
                pe.wait_ge(*m("sort_act", 4))
                pe.wait_ge(*m("sort_dve", 4))
                pe.wait_ge(*m("row_sb_a", TT))
                pe.wait_ge(*m("row_sb_d", TT))
                for b in range(4):
                    mm(psum[:, b, :], zeros_b[:, 0:P], zeros_b[:, :], True, False)

                def up(s, buf):
                    for k in range(KD):
                        for j in range(2):
                            last = mm(psum[j * WIN:(j + 1) * WIN, 6, :], xg[:, buf, k, j * WIN:(j + 1) * WIN],
                                      slot_gu(s, j)[:, :, k, :], k == 0, k == KD - 1)
                    return last

                def up_first():
                    for u in range(2):
                        for k in range(KD):
                            for j in range(2):
                                last = mm(psum[j * WIN:(j + 1) * WIN, 6, u * FF:(u + 1) * FF],
                                          xg[:, 0, k, j * WIN:(j + 1) * WIN], slot_gu(0, j)[:, u, k, :],
                                          k == 0, k == KD - 1)
                        last.then_inc(m[("gate0_ps", "gu_ps")[u]], 1)

                def transpose_h():
                    for k in range(FF // P):
                        last = pe.transpose(psum[:, 7, k * P:(k + 1) * P], h_sb[:, k * P:(k + 1) * P], ident)
                    return last

                def down(s):
                    for c in range(2):
                        for k in range(FF // P):
                            for j in range(2):
                                last = mm(psum[j * WIN:(j + 1) * WIN, 4 + c, :], hT[:, k, j * WIN:(j + 1) * WIN],
                                          slot_dn(s, j)[:, k, c * 512:(c + 1) * 512], k == 0, k == FF // P - 1)
                    return last

                def combine(buf, t):
                    for c in range(2):
                        last = mm(psum[:, 2 * t + c, :], comb[:, buf, t * P:(t + 1) * P],
                                  y_sb[:, c * 512:(c + 1) * 512], False, False)
                    return last

                def pair(i, s, first=False):
                    prev = (s + SLOTS - 1) % SLOTS
                    if first:
                        pe.wait_ge(*m("xg0_ready", 2))
                    else:
                        pe.wait_ge(*m("xg_ready", i * 2))
                    pe.wait_ge(*rings[l][s]("gu", turn(i, s) * 64))
                    if not first:
                        pe.wait_ge(*m("h_ready", i))
                    if first:
                        up_first()
                    else:
                        up(s, s).then_inc(m["gu_ps"], 1)
                    if not first:
                        pe.wait_ge(*m("y_act", i))
                        pe.wait_ge(*m("y_dve", i))
                        pe.wait_ge(*m("g_ready", i))
                        combine(prev, 0)
                    pe.wait_ge(*m("h_ready", i + 1))
                    if not first:
                        pe.wait_ge(*m("ht_sb", i))
                    transpose_h().then_inc(m["ht_ps"], 1)
                    if not first:
                        combine(prev, 1).then_inc(m["c_ps"], 1)
                    pe.wait_ge(*m("ht_sb", i + 1))
                    pe.wait_ge(*rings[l][s]("dn", turn(i, s) * 32))
                    down(s).then_inc(m["y_ps"], 1)

                def turn(i, s):
                    return (i - s) // SLOTS + 1 if isinstance(i, int) else turns[s]

                pair(0, 0, True)
                turns = [None] * SLOTS
                with pe.Fori(0, (PAIRS - 1) // SLOTS) as it:
                    for j in range(SLOTS):
                        i, s = it * SLOTS + (1 + j), (1 + j) % SLOTS
                        turns[s] = it + (1 + (1 + j) // SLOTS)
                        pair(i, s)
                s = (PAIRS - 1) % SLOTS
                pe.wait_ge(*m("y_act", PAIRS))
                pe.wait_ge(*m("y_dve", PAIRS))
                pe.wait_ge(*m("g_ready", PAIRS))

                def close(t):
                    for c in range(2):
                        last = mm(psum[:, 2 * t + c, :], zeros_b[:, 0:P], zeros_b[:, :], False, True)
                    last.then_inc(m["sum_ps"], 1)

                with pe.If(overflows(pe, l)):
                    o = ov[l]
                    combine(s, 0)
                    combine(s, 1).then_inc(m["c_ps"], 1)
                    pe.sem_inc(o["free"], 1)

                    def step(i, r, n):
                        pe.wait_ge(o["w"], n * 96 + 96)
                        pe.wait_ge(o["xg"], n * 2 + 2)
                        up(0, 0).then_inc(o["gu"], 1)
                        pe.wait_ge(o["h"], n + 1)
                        transpose_h().then_inc(o["ht_ps"], 1)
                        pe.wait_ge(o["ht_sb"], n + 1)
                        down(0).then_inc(o["y_ps"], 1)
                        pe.wait_ge(o["y_act"], n + 1)
                        pe.wait_ge(o["y_dve"], n + 1)
                        pe.wait_ge(o["g"], n + 1)
                        combine(0, 0)
                        combine(0, 1).then_inc(o["free"], 1)

                    overflow_steps(pe, step)
                    close(0)
                    close(1)
                with pe.Else():
                    combine(s, 0)
                    close(0)
                    combine(s, 1).then_inc(m["c_ps"], 1)
                    close(1)

            diff_attention()
            moe(0)
            mla_attention()
            moe(1)

        @block.scalar
        def _(act):
            chain = Chain(act, act_chain)

            def act_xt(n):
                for b in (0, 2):
                    act.wait_ge(*xt[n]("ps", b + 1))
                    for k in (2 * b, 2 * b + 1):
                        act.activation(xT[:, k, :], psum[:, 4 + b, (k % 2) * SEQ:(k % 2 + 1) * SEQ], ACT.Identity,
                                       scale=gcol[:, n - 1, k:k + 1], bias=bcol[:, n - 1, k:k + 1])\
                           .then_inc(xt[n]["sb"], 1)

            def wo_upper(w, heads):
                for h in heads:
                    act.copy(wo_hi(w, h), wo(ring, w, h)).then_inc(w_hi_ready, 1)

            def layer_norm(n):
                for t in range(TT):
                    act.wait_ge(*ln[n]("var", t + 1))
                    act.activation(ln_sd[:, t:t + 1], ln_mv[:, t, 1:2], ACT.Sqrt, bias=eps[:, :]).then_inc(ln[n]["sd"], 1)
                    cols = (slice(0, D), slice(0, D // 2))[t]
                    act.wait_ge(*ln[n]("rstd", t + 1))
                    act.activation(xs[:, t, cols], xs[:, t, cols], ACT.Identity, scale=ln_rstd[:, t:t + 1],
                                   bias=ln_nb[:, t:t + 1]).then_inc(ln[n]["norm"], 1)

            def diff_attention():
                for b in range(4):
                    act.wait_ge(*xt[0]("ps", b + 1))
                    act.copy(xT_r[:, 2 * b:2 * b + 2, :], psum[:, 4 + b, :].rearrange("p (k t) -> p k t", k=2))\
                       .then_inc(x_hi_ready, 1)

                def move(g):
                    act.wait_ge(qkv_ps, g + 1)
                    src = psum[:, g % 8, :]
                    if g < 4:
                        for c in range(2):
                            rows = slice(c * DH, (c + 1) * DH)
                            act.mul(qz[rows, 2 * g:2 * g + 2, c, :], src[rows, :].rearrange("p (h t) -> p h t", h=2),
                                    DH ** -0.5).then_inc(qkv_act, 1)
                    elif g < 8:
                        act.copy(kT[:, 2 * (g - 4):2 * (g - 4) + 2, :], src.rearrange("p (h t) -> p h t", h=2))\
                           .then_inc(qkv_act, 1)
                    else:
                        c = (g - 8) // 2
                        act.copy(v[:, 0, c * 512:(c + 1) * 512], src).then_inc(qkv_act, 1)

                for c in range(6):
                    for m in range(4):
                        if m % 2 == 0 or c == 1:
                            act.wait_ge(ld_qkv0b if c == 0 and m else ld_qkv[c], 16)
                        if c >= 2:
                            act.wait_ge(qkv_ps, 2 * (c - 2) + m // 2 + 1)
                        cols = slice(m * P, (m + 1) * P)
                        act.copy(w_hi[:, c % 2, :, cols], qkv_chunk(ring, c)[:, :, cols]).then_inc(w_hi_ready, 1)
                    if c >= 1:
                        move(2 * (c - 1))
                    if c == 3:
                        act.wait_ge(lam_ready, 2)
                        act.activation(lam_dot, lam_dot, ACT.Exp).then_inc(lam_exp, 1)
                move(10)
                s = at[0]
                nmx = small[:, 0:8].rearrange("p (b q c) -> p b q c", b=2, q=2)
                sums = small[:, 8:16].rearrange("p (b q c) -> p b q c", b=2, q=2)
                nlr = small[:, 24:28].rearrange("p (b q) -> p b q", b=2)
                part = (slice(0, P), slice(P, 3 * P))

                def exps(h):
                    act.wait_ge(*s("mx_ready", 2 * (h + 1)))
                    for c in range(2):
                        for q in range(2):
                            e = lg[h % 4][:, c, part[q]]
                            act.activation(e, e, ACT.Exp, bias=nmx[:, h % 2, q, c:c + 1],
                                           accum_out=sums[:, h % 2, q, c:c + 1]).then_inc(s["e_ready"], 1)

                def scale_second(h):
                    act.wait_ge(*s("r_ready", h + 1))
                    for q in range(2):
                        e = lg[h % 4][:, 1, part[q]]
                        act.activation(e, e, ACT.Copy, scale=nlr[:, h % 2, q:q + 1]).then_inc(s["e1_scaled"], 1)

                def out(h):
                    act.wait_ge(*s("o_ps", h + 1))
                    act.copy(o_sb[:, h, :], psum[:, 6 + h % 2, 0:SEQ]).then_inc(s["o_sb"], 1)

                def transposed(h):
                    act.wait_ge(*s("pt_ps", h + 1))
                    if h >= 2:
                        act.wait_ge(*s("o_ps", h - 1))
                    act.copy(aT[h % 2], psum[:, 4 + h % 2, 0:3 * P]).then_inc(s["pt_sb"], 1)

                exps(0)
                exps(1)
                for h in range(HEADS):
                    scale_second(h)
                    if h >= 1:
                        transposed(h - 1)
                    if h >= 2:
                        out(h - 2)
                    if h + 2 < HEADS:
                        exps(h + 2)
                transposed(HEADS - 1)
                out(HEADS - 2)
                out(HEADS - 1)
                ss, sd = small[:, 32:48], small[:, 48:64]
                act.wait_ge(ss_ready, 2)
                act.activation(sd, ss, ACT.Sqrt, scale=1.0 / P, bias=eps[:, :]).then_inc(sd_ready, 1)
                act.wait_ge(ld_wo_a, 16)
                wo_upper(wo_a, (4, 5, 6))
                for b in range(4):
                    act.wait_ge(ot_ps, b + 1)
                    act.activation(oT[:, 2 * b:2 * b + 2, :], psum[:, 4 + b, :].rearrange("p (h t) -> p h t", h=2),
                                   ACT.Copy, scale=subg[:, :]).then_inc(x_hi_ready, 1)
                wo_upper(wo_a, (7,))

            def mla_attention():
                act_xt(2)
                ss, sd = small[:, 0:4], small[:, 4:8]
                for i, (bank, n) in enumerate(((2, QR), (3, QR), (0, KVR), (1, KVR))):
                    act.wait_ge(mq["a_ps"], i + 1)
                    chain(act.activation(sq_junk[:, 0:n], psum[:, bank, 0:n], ACT.Square, accum_out=ss[:, i:i + 1]))
                    act.activation(sd[:, i:i + 1], ss[:, i:i + 1], ACT.Sqrt, scale=1.0 / n, bias=eps[:, :])\
                       .then_inc(mq["sd"], 1)
                act.wait_ge(mq["ct_ps"], 1)
                act.activation(cqT[:, 0, :], psum[:, 4, 0:SEQ], ACT.Copy, scale=qg[:, 0:1]).then_inc(mq["ct_sb"], 1)
                act.activation(cqT[:, 1, :], psum[:, 4, SEQ:], ACT.Copy, scale=qg[:, 1:2]).then_inc(mq["ct_sb"], 1)
                for t in range(TT):
                    act.wait_ge(mq["qr_ps"], t + 1)
                    act.mul(qr_raw[:, t, :, :], psum[:, 2 + t, :].rearrange("p (h d) -> p h d", h=HEADS), MLA_SCALE)\
                       .then_inc(mq["qr_raw"], 1)
                banks = [4, 5, 0, 1, 6, 7, 4, 5, 0, 1, 2, 3]
                for g in range(0, 12, 2):
                    act.wait_ge(mq["b_ps"], g + 1)
                    src = psum[:, banks[g], :]
                    if g < 4:
                        act.mul(qnT[:, 2 * g:2 * g + 2, :], src.rearrange("p (h t) -> p h t", h=2), MLA_SCALE)\
                           .then_inc(mq["b_act"], 1)
                    elif g < 8:
                        act.copy(knT[:, 2 * (g - 4):2 * (g - 4) + 2, :], src.rearrange("p (h t) -> p h t", h=2))\
                           .then_inc(mq["b_act"], 1)
                    else:
                        act.wait_ge(mq["krt_ps"], 1)
                        act.copy(v[:, (g - 8) // 2, 0:512], src).then_inc(mq["b_act"], 1)
                for b in range(2):
                    act.wait_ge(mq["qt_ps"], b + 1)
                    src = psum[0:ROPE, (7, 4)[b], :].rearrange("p (h t) -> p h t", h=2)
                    act.copy(qrz[0:ROPE, 4 * b:4 * b + 4:2, :], src).then_inc(mq["qt_sb"], 1)
                s = at[1]
                nmx = small[:, 16:20].rearrange("p (b q) -> p b q", b=2)
                sums = small[:, 20:24].rearrange("p (b q) -> p b q", b=2)

                def exps(h):
                    act.wait_ge(*s("mx_ready", 2 * (h + 1)))
                    for q, part in enumerate((slice(0, P), slice(P, 3 * P))):
                        e = mlg[h % 3][:, part]
                        act.activation(e, e, ACT.Exp, bias=nmx[:, h % 2, q:q + 1],
                                       accum_out=sums[:, h % 2, q:q + 1]).then_inc(s["e_ready"], 1)

                def out(h):
                    act.wait_ge(*s("o_ps", h + 1))
                    act.copy(oT[:, h, :], psum[:, 4 + h % 2, 0:SEQ]).then_inc(s["o_sb"], 1)

                def transposed(h):
                    act.wait_ge(*s("pt_ps", h + 1))
                    if h >= 2:
                        act.wait_ge(*s("o_ps", h - 1))
                    act.copy(pT[h % 2], psum[:, 2 + h % 2, 0:3 * P]).then_inc(s["pt_sb"], 1)

                exps(0)
                exps(1)
                for h in range(HEADS):
                    if h >= 1:
                        transposed(h - 1)
                    if h >= 2:
                        out(h - 2)
                    if h + 2 < HEADS:
                        exps(h + 2)
                transposed(HEADS - 1)
                out(HEADS - 2)
                out(HEADS - 1)
                act.wait_ge(ld_wo_b, 16)
                wo_upper(wo_b, range(4, HEADS))

            def moe(l):
                m = mo[l]
                act_xt(2 * l + 1)
                act.wait_ge(*m("lg_ps", 1))
                act.activation(routing()["score"], psum[:, 1, 0:64], ACT.Sigmoid).then_inc(m["score"], 1)
                for part, (t, k0, k1) in zip(hi_parts, hi_of):
                    act.wait_ge(*ln[2 * l](("x_dve", "x_pool")[t], 1))
                    act.copy(part, xs_tiles(t, k0, k1)).then_inc(m["hi_ready"], 1)
                for k in range(0, KD, 2):
                    act.wait_ge(*m("sort_ps", k + 1))
                    act.copy(xsT[:, k, 0:NSLOT], psum[:, SORT_BANKS[k], :]).then_inc(m["sort_act"], 1)
                act.wait_ge(*m("row_ps", 1))
                for t in range(TT):
                    act.copy(gate_row[:, :, t * P:(t + 1) * P],
                             psum[:, t, 2 * P:4 * P].rearrange("p (j n) -> p j n", j=2)).then_inc(m["row_sb_a"], 1)

                def pair(i, s, first=False):
                    act.wait_ge(*m("gu_ps", i + 1))
                    if not first:
                        act.wait_ge(*m("h_ready", i))
                    act.activation(act_s, psum[:, 6, 0:FF], ACT.Silu).then_inc(m["s_ready"], 1)
                    act.wait_ge(*m("ht_ps", i + 1))
                    if not first:
                        act.wait_ge(*m("y_ps", i))
                    act.copy(hT, psum[:, 7, 0:FF].rearrange("p (k c) -> p k c", k=2)).then_inc(m["ht_sb"], 1)
                    act.wait_ge(*m("y_ps", i + 1))
                    if not first:
                        act.wait_ge(*m("c_ps", i))
                    act.copy(y_sb[:, 0:512], psum[:, 4, :]).then_inc(m["y_act"], 1)

                pair(0, 0, True)
                for_pairs_1_up(act, pair)
                with act.If(overflows(act, l)):
                    o = ov[l]

                    def step(i, r, n):
                        act.wait_ge(o["gu"], n + 1)
                        act.activation(act_s, psum[:, 6, 0:FF], ACT.Silu).then_inc(o["s"], 1)
                        act.wait_ge(o["ht_ps"], n + 1)
                        act.copy(hT, psum[:, 7, 0:FF].rearrange("p (k c) -> p k c", k=2)).then_inc(o["ht_sb"], 1)
                        act.wait_ge(o["y_ps"], n + 1)
                        act.copy(y_sb[:, 0:512], psum[:, 4, :]).then_inc(o["y_act"], 1)

                    overflow_steps(act, step)

            act.dma_start(tri_f, consts[:, CONSTS:CONSTS + P]).then_inc(ld_misc, 16)
            act.dma_start(lam_in, diff_lambda[0].partition_broadcast(P)).then_inc(ld_lam, 16)
            act.dma_start(rb[:, :], router_b.partition_broadcast(P)).then_inc(ld_misc, 16)
            with nc.allow_non_contiguous_dma(reason="norm scales as columns, once"):
                act.dma_start(subg[:, :], diff_subln_g[0].rearrange("(p a) -> p a", a=1)).then_inc(ld_misc, 16)
                act.dma_start(qg[:, :], mla_q_norm_g[0].rearrange("(k p) -> p k", p=P)).then_inc(ld_misc, 16)
                act.dma_start(kvg[:, :], mla_kv_norm_g.rearrange("(k p) -> p k", p=P)).then_inc(ld_misc, 16)
                for col, w in ((gcol, ln_g), (bcol, ln_b)):
                    act.dma_start(col[:, :, :], w.rearrange("l j (p k) -> p (l j) k", k=KD)[:, 0:3, :])\
                       .then_inc(ld_misc, 16)
            diff_attention()
            layer_norm(0)
            act.wait_ge(ld_misc, 16 * MISC)
            moe(0)
            layer_norm(1)
            mla_attention()
            layer_norm(2)
            moe(1)
            layer_norm(3)

        @block.vector
        def _(dve):
            chain = Chain(dve, dve_chain)

            def dve_xt(n):
                for b in (1, 3):
                    dve.wait_ge(*xt[n]("ps", b + 1))
                    for k in (2 * b, 2 * b + 1):
                        dve.tensor_scalar(xT[:, k, :], psum[:, 4 + b, (k % 2) * SEQ:(k % 2 + 1) * SEQ],
                                          gcol[:, n - 1, k:k + 1], bcol[:, n - 1, k:k + 1], ALU.mult, ALU.add)\
                           .then_inc(xt[n]["sb"], 1)

            def wo_lower(l, w):
                for h in range(4, HEADS):
                    dve.wait_ge(w_hi_ready, 24 + 4 * l + h - 3)
                    dve.tensor_tensor(wo(ring_r, w, h), wo(ring, w, h), wo_hi(w, h), ALU.subtract)\
                       .then_inc(w_lo_ready, 1)

            def layer_norm(n, ready):
                def add(t, c):
                    ready(t, c)
                    cols = slice(c * 512, (c + 1) * 512)
                    chain(dve.scalar_tensor_tensor(out=xs[:, t, cols], in0=xs[:, t, cols], scalar=ALPHA,
                                                   in1=psum[:, 2 * t + c, :], op0=ALU.mult, op1=ALU.add))
                    chain(dve.bn_stats(ln_stats[:, t, c, :], xs[:, t, cols]))

                def statistics(t):
                    dve.bn_aggr(ln_mv[:, t, :], ln_stats[:, t, :, :].rearrange("p c s -> p (c s)"))\
                       .then_inc(ln[n]["var"], 1)

                def scales(t):
                    dve.wait_ge(*ln[n]("sd", t + 1))
                    chain(dve.reciprocal(ln_rstd[:, t:t + 1], ln_sd[:, t:t + 1]))
                    dve.tensor_scalar(ln_nb[:, t:t + 1], ln_mv[:, t, 0:1], ln_rstd[:, t:t + 1], -1.0, ALU.mult,
                                      ALU.mult).then_inc(ln[n]["rstd"], 1)

                add(0, 0)
                add(0, 1)
                statistics(0)
                add(1, 0)
                scales(0)
                add(1, 1)
                statistics(1)
                scales(1)
                dve.wait_ge(*ln[n]("rstd", 2))
                dve.tensor_scalar(xs[:, 1, D // 2:], xs[:, 1, D // 2:], ln_rstd[:, 1:2], ln_nb[:, 1:2], ALU.mult,
                                  ALU.add).then_inc(ln[n]["norm"], 1)

            def scale_shift(n):
                dve.wait_ge(*ln[n]("norm", 3))
                dve.wait_ge(*ld_gb[n]("gb", 32))
                chain(dve.tensor_tensor(xs[:, 0, :], xs[:, 0, :], gb[n][:, 0, :], ALU.mult))
                dve.tensor_tensor(xs[:, 0, :], xs[:, 0, :], gb[n][:, 1, :], ALU.add).then_inc(ln[n]["x_dve"], 1)

            def prepare():
                dve.memset(zeros_b[:, :], 0.0).then_inc(cast_ready, 1)
                dve.memset(eps[:, :], EPS).then_inc(lam_ready, 1)
            def constants():
                dve.wait_ge(ld_cst, 16)
                dve.tensor_copy(ones_b[:, :], ones).then_inc(cast_ready, 1)
                dve.wait_ge(ld_misc, 16 * MISC)
                dve.tensor_copy(tri_b[:, :], tri_f).then_inc(cast_ready, 1)
                dve.wait_ge(ld_lam, 16)
                chain(dve.tensor_tensor(lam_prod, lam_in[:, 0::2, :], lam_in[:, 1::2, :], ALU.mult))
                dve.tensor_reduce(lam_dot, lam_prod, AX.X, ALU.add).then_inc(lam_ready, 1)

            def diff_attention():
                for b in range(4):
                    dve.wait_ge(x_hi_ready, b + 1)
                    dve.tensor_tensor(x_lo[:, 2 * b:2 * b + 2, :], psum[:, 4 + b, :].rearrange("p (k t) -> p k t", k=2),
                                      xT_r[:, 2 * b:2 * b + 2, :], ALU.subtract).then_inc(xt[0]["sb"], 2)

                def move(g):
                    dve.wait_ge(qkv_ps, g + 1)
                    src = psum[:, g % 8, :]
                    if g < 4:
                        for c in range(2):
                            rows = slice(c * DH, (c + 1) * DH)
                            dve.tensor_scalar(qz[rows, 2 * g:2 * g + 2, c, :],
                                              src[rows, :].rearrange("p (h t) -> p h t", h=2), DH ** -0.5, None,
                                              ALU.mult).then_inc(qkv_dve, 1)
                    elif g < 8:
                        dve.tensor_copy(kT[:, 2 * (g - 4):2 * (g - 4) + 2, :],
                                        src.rearrange("p (h t) -> p h t", h=2)).then_inc(qkv_dve, 1)
                    else:
                        dve.wait_ge(cast_ready, 3)
                        c = (g - 8) // 2
                        dve.tensor_copy(v[:, 1, c * 512:(c + 1) * 512], src).then_inc(qkv_dve, 1)

                for c in range(6):
                    for m in range(4):
                        dve.wait_ge(w_hi_ready, 4 * c + m + 1)
                        cols = slice(m * P, (m + 1) * P)
                        dve.tensor_tensor(qkv_chunk(ring_r, c)[:, :, cols], qkv_chunk(ring, c)[:, :, cols],
                                          w_hi[:, c % 2, :, cols], ALU.subtract).then_inc(w_lo_ready, 1)
                    if c >= 1:
                        move(2 * (c - 1) + 1)
                    if c == 2:
                        constants()
                move(11)
                dve.wait_ge(lam_exp, 1)
                chain(dve.tensor_tensor(nlam[:, :], lam_dot[:, 1:2], lam_dot[:, 0:1], ALU.subtract))
                chain(dve.tensor_scalar(nlam[:, :], nlam[:, :], LAMBDA_INIT, None, ALU.subtract))
                chain(dve.tensor_scalar(subg[:, :], subg[:, :], 1.0 - LAMBDA_INIT, None, ALU.mult))
                s = at[0]
                nmx = small[:, 0:8].rearrange("p (b q c) -> p b q c", b=2, q=2)
                sums = small[:, 8:16].rearrange("p (b q c) -> p b q c", b=2, q=2)
                rec = small[:, 16:24].rearrange("p (b q c) -> p b q c", b=2, q=2)
                nlr = small[:, 24:28].rearrange("p (b q) -> p b q", b=2)

                def logits(h):
                    if h >= 4:
                        dve.wait_ge(*s("pt_ps", h - 3))
                    b = lg[h % 4]
                    for c in range(2):
                        dve.wait_ge(*s("sc_ps", 2 * h + c + 1))
                        dve.scalar_tensor_tensor(out=b[:, c, :], in0=dist, scalar=-(2.0 ** -(h + 1)),
                                                 in1=psum[:, 2 * (h % 2) + c, 0:3 * P], op0=ALU.mult, op1=ALU.add)\
                           .then_inc(s["sc_read"], 1)
                    dve.wait_ge(*s("sc_read", 2 * (h + 1)))
                    dve.tensor_reduce(nmx[:, h % 2, 0, :], b[:, :, 0:P], AX.X, ALU.max, negate=True)\
                       .then_inc(s["mx_ready"], 1)
                    dve.tensor_reduce(nmx[:, h % 2, 1, :], b[:, :, P:3 * P], AX.X, ALU.max, negate=True)\
                       .then_inc(s["mx_ready"], 1)

                def reciprocals(h):
                    dve.wait_ge(*s("e_ready", 4 * (h + 1)))
                    chain(dve.reciprocal(rec[:, h % 2, :, :], sums[:, h % 2, :, :]))
                    dve.tensor_scalar(nlr[:, h % 2, :], rec[:, h % 2, :, 1], nlam[:, :], None, ALU.mult)\
                       .then_inc(s["r_ready"], 1)

                def probabilities(h):
                    dve.wait_ge(*s("e1_scaled", 2 * (h + 1)))
                    e = lg[h % 4]
                    for q, part in enumerate((slice(0, P), slice(P, 3 * P))):
                        dve.scalar_tensor_tensor(out=e[:, 0, part], in0=e[:, 0, part], scalar=rec[:, h % 2, q, 0:1],
                                                 in1=e[:, 1, part], op0=ALU.mult, op1=ALU.add)\
                           .then_inc(s["p_ready"], 1)

                logits(0)
                logits(1)
                for h in range(HEADS):
                    reciprocals(h)
                    if h + 2 < HEADS:
                        logits(h + 2)
                    probabilities(h)
                ss, sd = small[:, 32:48], small[:, 48:64]
                for heads, n in (((0, 6), 6), ((6, 8), 8)):
                    dve.wait_ge(sq_ready, n)
                    dve.tensor_reduce(ss[:, 2 * heads[0]:2 * heads[1]],
                                      o_sq[:, heads[0]:heads[1], :].rearrange("p h (q d) -> p h q d", q=2), AX.X, ALU.add)\
                       .then_inc(ss_ready, 1)
                dve.wait_ge(sd_ready, 1)
                rs = small[:, 32:48].rearrange("p (h q) -> p h q", h=HEADS)
                dve.reciprocal(small[:, 32:48], sd).then_inc(rs_ready, 1)
                dve.wait_ge(rs_ready, 1)
                for lo, hi in ((0, 2), (2, 5)):
                    o4 = o_sb[:, lo:hi, :].rearrange("p h (q d) -> p h q d", q=2)
                    dve.tensor_tensor(o4, o4, rs[:, lo:hi, :].unsqueeze(3).broadcast_to([P, hi - lo, 2, P]), ALU.mult)\
                       .then_inc(on_dve, 1)
                for b in range(4):
                    dve.wait_ge(x_hi_ready, 4 + b + 1)
                    dve.scalar_tensor_tensor(out=o_lo_a[:, 2 * b:2 * b + 2, :], in0=psum[:, 4 + b, :]
                                             .rearrange("p (h t) -> p h t", h=2), scalar=subg[:, :],
                                             in1=oT[:, 2 * b:2 * b + 2, :], op0=ALU.mult, op1=ALU.subtract)\
                       .then_inc(ot_sb, 1)
                wo_lower(0, wo_a)

            def mla_attention():
                dve_xt(2)
                dve.wait_ge(*xt[2]("ps", 4))
                scale_shift(1)
                sd, rstd = small[:, 4:8], small[:, 8:12]
                for i, (bank, n) in enumerate(((2, QR), (3, QR), (0, KVR), (1, KVR))):
                    dve.wait_ge(mq["sd"], i + 1)
                    chain(dve.reciprocal(rstd[:, i:i + 1], sd[:, i:i + 1]))
                    dst = c_q[:, i, :] if i < 2 else c_kv[:, i - 2, :]
                    dve.tensor_scalar(dst, psum[:, bank, 0:n], rstd[:, i:i + 1], None, ALU.mult)\
                       .then_inc(mq["c_ready"], 1)
                    if i >= 2:
                        chain(dve.tensor_copy(kr_raw[:, i - 2, :], psum[:, bank, KVR:KVR + ROPE]))
                dve.wait_ge(mq["ct_ps"], 1)
                dve.tensor_scalar(cqT[:, 2, :], psum[:, 5, 0:SEQ], qg[:, 2:3], None, ALU.mult).then_inc(mq["ct_sb"], 1)
                dve.wait_ge(mq["ct_ps"], 2)
                for k in range(2):
                    dve.tensor_scalar(ckvT[:, k, :], psum[:, 6, k * SEQ:(k + 1) * SEQ], kvg[:, k:k + 1], None, ALU.mult)\
                       .then_inc(mq["ct_sb"], 1)
                for t in range(TT):
                    dst = kr2[:, t, 0:ROPE].unsqueeze(1)
                    chain(rotate(dve, chain, dst, kr_raw[:, t, :].unsqueeze(1), t, rope_tmp[:, 0:1, :], 1))
                dve.tensor_copy(kr2[:, :, ROPE:2 * ROPE], kr2[:, :, 0:ROPE]).then_inc(mq["kr_rot"], 1)
                banks = [4, 5, 0, 1, 6, 7, 4, 5, 0, 1, 2, 3]
                for g in range(1, 12, 2):
                    if g == 3:
                        dve.wait_ge(mq["qr_raw"], 1)
                        rotate(dve, chain, qr_rot[:, 0, :, :], qr_raw[:, 0, :, :], 0, rope_tmp, HEADS)\
                            .then_inc(mq["qr_rot_dve"], 1)
                    dve.wait_ge(mq["b_ps"], g + 1)
                    src = psum[:, banks[g], :]
                    if g < 4:
                        dve.tensor_scalar(qnT[:, 2 * g:2 * g + 2, :], src.rearrange("p (h t) -> p h t", h=2), MLA_SCALE,
                                          None, ALU.mult).then_inc(mq["b_dve"], 1)
                    elif g < 8:
                        dve.tensor_copy(knT[:, 2 * (g - 4):2 * (g - 4) + 2, :],
                                        src.rearrange("p (h t) -> p h t", h=2)).then_inc(mq["b_dve"], 1)
                    else:
                        dve.wait_ge(mq["krt_ps"], 1)
                        dve.wait_ge(mq["qr_rot_pool"], 1)
                        dve.tensor_copy(v[:, (g - 8) // 2, 512:1024], src).then_inc(mq["b_dve"], 1)
                dve.wait_ge(mq["krt_ps"], 1)
                dve.tensor_copy(krT2, psum[:, 6, 0:SEQ]).then_inc(mq["krt_sb"], 1)
                for b in range(2):
                    dve.wait_ge(mq["qt_ps"], b + 1)
                    src = psum[ROPE:P, (7, 4)[b], :].rearrange("p (h t) -> p h t", h=2)
                    dve.tensor_copy(qrz[ROPE:P, 4 * b + 1:4 * b + 4:2, :], src).then_inc(mq["qt_sb"], 1)
                s = at[1]
                nmx = small[:, 16:20].rearrange("p (b q) -> p b q", b=2)
                sums = small[:, 20:24].rearrange("p (b q) -> p b q", b=2)
                rec = small[:, 24:28].rearrange("p (b q) -> p b q", b=2)

                def logits(h):
                    if h >= 3:
                        dve.wait_ge(*s("pt_ps", h - 2))
                    dve.wait_ge(*s("sc_ps", h + 1))
                    dve.tensor_tensor(mlg[h % 3], psum[:, h % 2, 0:3 * P], mask, ALU.add).then_inc(s["sc_read"], 1)
                    dve.wait_ge(*s("sc_read", h + 1))
                    for q, part in enumerate((slice(0, P), slice(P, 3 * P))):
                        dve.tensor_reduce(nmx[:, h % 2, q:q + 1], mlg[h % 3][:, part], AX.X, ALU.max, negate=True)\
                           .then_inc(s["mx_ready"], 1)

                def reciprocals(h):
                    dve.wait_ge(*s("e_ready", 2 * (h + 1)))
                    dve.reciprocal(rec[:, h % 2, :], sums[:, h % 2, :]).then_inc(s["r_ready"], 1)

                def probabilities(h):
                    dve.wait_ge(*s("r_ready", h + 1))
                    for q, part in enumerate((slice(0, P), slice(P, 3 * P))):
                        dve.tensor_scalar(mlg[h % 3][:, part], mlg[h % 3][:, part], rec[:, h % 2, q:q + 1], None,
                                          ALU.mult).then_inc(s["p_ready"], 1)

                def o_lower(h):
                    dve.wait_ge(*s("o_sb", h + 1))
                    dve.tensor_tensor(o_lo_b[:, h, :], psum[:, 4 + h % 2, 0:SEQ], oT[:, h, :], ALU.subtract)\
                       .then_inc(o_lo_ready, 1)

                dve.wait_ge(mq["b_ps"], 12)
                logits(0)
                logits(1)
                for h in range(HEADS):
                    reciprocals(h)
                    if h >= 3:
                        o_lower(h - 3)
                    if h + 2 < HEADS:
                        logits(h + 2)
                    probabilities(h)
                o_lower(HEADS - 3)
                o_lower(HEADS - 2)
                o_lower(HEADS - 1)
                wo_lower(1, wo_b)

            def moe(l):
                m = mo[l]
                dve_xt(2 * l + 1)
                dve.wait_ge(*xt[2 * l + 1]("ps", 4))
                scale_shift(2 * l)
                dve.wait_ge(*m("lgt_ps", 1))
                dve.tensor_copy(logit_T, psum[0:EXPERTS, 0, 0:SEQ]).then_inc(m["lgt_sb"], 1)
                c = routing()
                both = TT * EXPERTS

                def tt(dst, a, b, op):
                    chain(dve.tensor_tensor(dst, a, b, op))

                def te(a):
                    return a.rearrange("p (t e) -> p t e", t=TT)

                def spread(a, n):
                    return a.unsqueeze(2).broadcast_to([P, TT, n])

                def per_tile(a, n):
                    return a.unsqueeze(1).broadcast_to([P, TT, n])

                dve.wait_ge(*m("score", 1))
                tt(te(c["sel"]), te(c["score"]), per_tile(rb[:, :], EXPERTS), ALU.add)
                quad = c["sel"].rearrange("p (g e) -> p g e", e=PER_GROUP)
                mx2, sm2 = (c[n].rearrange("p (g e) -> p g e", e=2) for n in ("mx2", "sm2"))
                tt(mx2, quad[:, :, 0::2], quad[:, :, 1::2], ALU.max)
                tt(sm2, quad[:, :, 0::2], quad[:, :, 1::2], ALU.add)
                tt(c["t1"], mx2[:, :, 0], mx2[:, :, 1], ALU.add)
                tt(c["t2"], sm2[:, :, 0], sm2[:, :, 1], ALU.max)
                tt(c["gs"], c["t1"], c["t2"], ALU.max)
                chain(dve.tensor_reduce(c["gmax"], te(c["gs"]), AX.X, ALU.max))
                tt(te(c["gkey"]), te(c["gs"]), spread(c["gmax"], GROUPS), ALU.is_equal)
                tt(te(c["gkey"]), te(c["gkey"]), per_tile(w8, GROUPS), ALU.mult)
                chain(dve.tensor_reduce(c["gmax"], te(c["gkey"]), AX.X, ALU.max))
                tt(te(c["gmask"]), te(c["gkey"]), spread(c["gmax"], GROUPS), ALU.is_equal)
                masked = c["masked"].rearrange("p (g e) -> p g e", e=PER_GROUP)
                wide = [P, TT * GROUPS, PER_GROUP]
                chain(dve.tensor_scalar(c["gmask"], c["gmask"], 1.0, BIG, ALU.subtract, ALU.mult))
                tt(masked, quad, c["gmask"].unsqueeze(2).broadcast_to(wide), ALU.add)
                oh = c["oh"].rearrange("p (j t e) -> p j t e", j=2, t=TT)
                for j in range(2):
                    chain(dve.tensor_reduce(c["m1"], te(c["masked"]), AX.X, ALU.max))
                    tt(te(c["e1"]), te(c["masked"]), spread(c["m1"], EXPERTS), ALU.is_equal)
                    tt(te(c["e1"]), te(c["e1"]), per_tile(w32, EXPERTS), ALU.mult)
                    chain(dve.tensor_reduce(c["k1"], te(c["e1"]), AX.X, ALU.max))
                    tt(oh[:, j], te(c["e1"]), spread(c["k1"], EXPERTS), ALU.is_equal)
                    if j == 0:
                        chain(dve.scalar_tensor_tensor(out=c["masked"], in0=c["oh"][:, 0:both], scalar=-3 * BIG,
                                                       in1=c["masked"], op0=ALU.mult, op1=ALU.add))
                dve.tensor_tensor(c["chosen"], oh[:, 0], oh[:, 1], ALU.add).then_inc(m["m_ready"], 1)
                kg = small[:, 0:8].rearrange("p (q t) -> p q t", q=4)
                slot = small[:, 8:12].rearrange("p (j t) -> p j t", j=2)
                total = small[:, 12:14]
                prod = c["prod"].rearrange("p (j n) -> p j n", j=2)
                oh2 = c["oh"].rearrange("p (j n) -> p j n", j=2)

                def pick(dst, src):
                    tt(prod, oh2, src.unsqueeze(1).broadcast_to([P, 2, both]), ALU.mult)
                    chain(dve.tensor_reduce(dst, c["prod"].rearrange("p (j t e) -> p j t e", j=2, t=TT), AX.X, ALU.add))

                pick(kg[:, 2:4, :], c["score"])
                dve.wait_ge(*m("cnt_ps", 1))
                dve.tensor_copy(c["cnt_col"], psum[0:EXPERTS, 3, 0:P]).then_inc(m["cnt_sb"], 1)
                tt(total, kg[:, 2, :], kg[:, 3, :], ALU.add)
                chain(dve.reciprocal(total, total))
                tt(kg[:, 2:4, :], kg[:, 2:4, :], total.unsqueeze(1).broadcast_to([P, 2, TT]), ALU.mult)
                dve.wait_ge(*m("rank_ps", 1))
                pick(slot, psum[:, 2, both:2 * both])
                dve.wait_ge(*m("iota_ready", 1))
                for t in range(TT):
                    chain(dve.tensor_scalar(onehot_r[:, t, :], iota, slot[:, 0, t:t + 1], None, ALU.is_equal))
                    dve.scalar_tensor_tensor(out=onehot_r[:, t, :], in0=iota, scalar=slot[:, 1, t:t + 1],
                                             in1=onehot_r[:, t, :], op0=ALU.is_equal, op1=ALU.add)\
                       .then_inc(m["hot_ready"], 1)
                tt(te(c["rank"]), te(psum[:, 2, 0:both]), per_tile(ekey, EXPERTS), ALU.add)
                tt(prod, oh2, c["rank"].unsqueeze(1).broadcast_to([P, 2, both]), ALU.mult)
                dve.tensor_reduce(kg[:, 0:2, :], c["prod"].rearrange("p (j t e) -> p j t e", j=2, t=TT), AX.X, ALU.add)\
                   .then_inc(m["key_ready"], 1)
                for r in range(ROUNDS):
                    chain(dve.tensor_scalar(offs[:, r * EXPERTS:(r + 1) * EXPERTS], psum[:, 2, 160:192], float(WIN * r),
                                            float(NSLOT), ALU.add, ALU.min))
                chain(dve.tensor_reduce(c["cnt"][:, 0:1], psum[:, 2, 128:160], AX.X, ALU.max))
                dve.tensor_copy(offs[:, ROUNDS * EXPERTS:ROUNDS * EXPERTS + 1], c["cnt"][:, 0:1])\
                   .then_inc(m["offs_ready"], 1)
                for k in range(1, KD, 2):
                    dve.wait_ge(*m("sort_ps", k + 1))
                    dve.tensor_copy(xsT[:, k, 0:NSLOT], psum[:, SORT_BANKS[k], :]).then_inc(m["sort_dve"], 1)
                dve.wait_ge(*m("sort_act", 4))
                dve.wait_ge(*m("sort_dve", 4))
                dve.wait_ge(*m("pad_zero", 1))
                dve.wait_ge(*m("offs_ready", 1))
                for j in range(2):
                    a = dve.value_load(offs[0:1, j:j + 1], min_val=0, max_val=NSLOT)
                    dve.tensor_copy(xg[:, 0, :, j * WIN:(j + 1) * WIN], xsT[:, :, bass.ds(a, WIN)])\
                       .then_inc(m["xg0_ready"], 1)
                dve.wait_ge(*m("row_ps", 1))
                dve.wait_ge(*m("row_sb_a", TT))
                for t in range(TT):
                    dve.tensor_scalar(key_row[:, :, t * P:(t + 1) * P],
                                      psum[:, t, 0:2 * P].rearrange("p (j n) -> p j n", j=2), rowc, None,
                                      ALU.subtract).then_inc(m["row_sb_d"], 1)
                dve.wait_ge(*m("row_sb_d", TT))

                def weights(i, r, buf, part, ready, n):
                    at_ = ecol[:, bass.ds(i + r * PAIRS, 1)]
                    dve.scalar_tensor_tensor(out=comb[:, buf, :], in0=key_row[:, 0, :], scalar=at_,
                                             in1=gate_row[:, 0, :], op0=ALU.is_equal, op1=ALU.mult).then_inc(part, 1)
                    dve.scalar_tensor_tensor(out=g_tmp, in0=key_row[:, 1, :], scalar=at_,
                                             in1=gate_row[:, 1, :], op0=ALU.is_equal, op1=ALU.mult).then_inc(part, 1)
                    dve.wait_ge(part, n * 2 + 2)
                    dve.tensor_tensor(comb[:, buf, :], comb[:, buf, :], g_tmp, ALU.add).then_inc(ready, 1)

                def pair(i, s, first=False):
                    dve.wait_ge(*m("s_ready", i + 1))
                    if not first:
                        dve.wait_ge(*m("ht_ps", i))
                    dve.tensor_tensor(h_sb, psum[:, 6, FF:2 * FF], act_s, ALU.mult).then_inc(m["h_ready"], 1)
                    if not first:
                        dve.wait_ge(*m("g_ready", i))
                    weights(i, 0, s, m["g_part"], m["g_ready"], i + l * PAIRS)
                    dve.wait_ge(*m("y_ps", i + 1))
                    if not first:
                        dve.wait_ge(*m("c_ps", i))
                    dve.tensor_copy(y_sb[:, 512:1024], psum[:, 5, :]).then_inc(m["y_dve"], 1)

                pair(0, 0, True)
                for_pairs_1_up(dve, pair)
                with dve.If(overflows(dve, l)):
                    o = ov[l]
                    dve.wait_ge(*m("c_ps", PAIRS))

                    def step(i, r, n):
                        dve.wait_ge(o["free"], n + 1)
                        dve.wait_ge(o["s"], n + 1)
                        dve.tensor_tensor(h_sb, psum[:, 6, FF:2 * FF], act_s, ALU.mult).then_inc(o["h"], 1)
                        weights(i, r, 0, o["g_part"], o["g"], n)
                        dve.wait_ge(o["y_ps"], n + 1)
                        dve.tensor_copy(y_sb[:, 512:1024], psum[:, 5, :]).then_inc(o["y_dve"], 1)

                    overflow_steps(dve, step)

            prepare()
            diff_attention()
            layer_norm(0, lambda t, c: dve.wait_ge(wo_ps[0], 2 * t + c + 1))
            moe(0)
            layer_norm(1, lambda t, c: dve.wait_ge(*mo[0]("sum_ps", t + 1)))
            mla_attention()
            layer_norm(2, lambda t, c: dve.wait_ge(wo_ps[1], 2 * t + c + 1))
            moe(1)
            layer_norm(3, lambda t, c: dve.wait_ge(*mo[1]("sum_ps", t + 1)))
            scale_shift(3)

        @block.gpsimd
        def _(pool):
            chain = Chain(pool, pool_chain)

            def layer_norm(n):
                pool.wait_ge(*ln[n]("norm", 3))
                if n < 3:
                    pool.wait_ge(*xt[n + 1]("ps", 4))
                pool.wait_ge(*ld_gb[n]("gb", 32))
                chain(pool.tensor_tensor(xs[:, 1, :], xs[:, 1, :], gb[n][:, 0, :], ALU.mult))
                pool.tensor_tensor(xs[:, 1, :], xs[:, 1, :], gb[n][:, 1, :], ALU.add).then_inc(ln[n]["x_pool"], 1)

            def split_wo(l, w, ld):
                pool.wait_ge(ld, 16)
                for h in range(4):
                    chain(pool.tensor_copy(wo_hi(w, h), wo(ring, w, h)))
                    pool.tensor_tensor(wo(ring_r, w, h), wo(ring, w, h), wo_hi(w, h), ALU.subtract)\
                        .then_inc(w_pool_ready, 1)

            def windows(i, r, buf, ready):
                for j in range(2):
                    a = pool.value_load(offs[0:1, bass.ds(r * EXPERTS + i * 2 + j, 1)], min_val=0, max_val=NSLOT)
                    last = pool.tensor_copy(xg[:, buf, :, j * WIN:(j + 1) * WIN], xsT[:, :, bass.ds(a, WIN)])
                    last.then_inc(ready, 1)

            def moe(l):
                m = mo[l]
                pool.wait_ge(*ln[2 * l]("x_dve", 1))
                pool.iota(iota, pattern=[[1, NSLOT]], base=0, channel_multiplier=0,
                          allow_small_or_imprecise_dtypes=True).then_inc(m["iota_ready"], 1)
                pool.memset(xsT[:, :, NSLOT:], 0.0).then_inc(m["pad_zero"], 1)
                pool.wait_ge(*ln[2 * l]("x_pool", 1))
                for n, (part, (t, k0, k1)) in enumerate(zip(hi_parts, hi_of)):
                    pool.wait_ge(*m("hi_ready", n + 1))
                    pool.tensor_tensor(xs_lo[:, t, k0:k1, :], xs_tiles(t, k0, k1), part, ALU.subtract)\
                        .then_inc(m["lo_ready"], 1)
                pool.wait_ge(*m("key_ready", 1))
                kg = small[:, 0:8].rearrange("p (q t) -> p q t", q=4)
                for t in range(TT):
                    for q in range(4):
                        pool.tensor_scalar(diag[:, t, q, :], ident, kg[:, q, t:t + 1], None, ALU.mult)\
                            .then_inc(m["diag_ready"], 1)
                pool.wait_ge(*m("offs_ready", 1))
                pool.wait_ge(*m("sort_act", 4))
                pool.wait_ge(*m("sort_dve", 4))
                pool.wait_ge(*m("pad_zero", 1))

                def pair(i, s):
                    pool.wait_ge(*m("gu_ps", i - 2))
                    windows(i, 0, s, m["xg_ready"])

                for i in (1, 2):
                    windows(i, 0, i, m["xg_ready"])
                pair(3, 0)
                for_pairs_4_up(pool, pair)
                with pool.If(overflows(pool, l)):
                    pool.wait_ge(*m("gu_ps", PAIRS))

                    def step(i, r, n):
                        pool.wait_ge(ov[l]["free"], n + 1)
                        windows(i, r, 0, ov[l]["xg"])

                    overflow_steps(pool, step)
                    pool.wait_ge(ov[l]["xg"], 2 * PAIRS * (ROUNDS - 1))

            pool.memset(qz[DH:P, :, 0, :], 0.0).then_inc(zeroed, 1)
            pool.memset(qz[0:DH, :, 1, :], 0.0).then_inc(zeroed, 1)
            pool.wait_ge(zeroed, 2)
            pool.wait_ge(qkv_ps, 12)
            split_wo(0, wo_a, ld_wo_a)
            for h in range(HEADS):
                pool.wait_ge(*at[0]("o_sb", h + 1))
                pool.tensor_tensor(o_sq[:, h, :], o_sb[:, h, :], o_sb[:, h, :], ALU.mult).then_inc(sq_ready, 1)
            pool.wait_ge(rs_ready, 1)
            rs = small[:, 32:48].rearrange("p (h q) -> p h q", h=HEADS)
            o4 = o_sb[:, 5:8, :].rearrange("p h (q d) -> p h q d", q=2)
            pool.tensor_tensor(o4, o4, rs[:, 5:8, :].unsqueeze(3).broadcast_to([P, 3, 2, P]), ALU.mult)\
                .then_inc(on_pool, 1)
            layer_norm(0)
            moe(0)
            pool.wait_ge(*mo[0]("xg_ready", 2 * PAIRS - 2))
            pool.memset(qrz[ROPE:P, 0::2, :], 0.0).then_inc(mq["zeroed"], 1)
            pool.wait_ge(mq["zeroed"], 1)
            pool.memset(qrz[0:ROPE, 1::2, :], 0.0).then_inc(mq["zeroed"], 1)
            pool.wait_ge(mq["zeroed"], 2)
            layer_norm(1)
            pool.wait_ge(mq["qr_raw"], 2)
            rotate(pool, chain, qr_rot[:, 1, :, :], qr_raw[:, 1, :, :], 1, rope_tmp2, HEADS)\
                .then_inc(mq["qr_rot_pool"], 1)
            pool.wait_ge(mq["b_ps"], 4)
            pool.wait_ge(*ln[1]("x_dve", 1))
            split_wo(1, wo_b, ld_wo_b)
            layer_norm(2)
            moe(1)
            layer_norm(3)


INPUTS = ["x", "diff_w_qkv", "diff_lambda", "diff_subln_g", "diff_w_o", "mla_w_kv_a", "mla_kv_norm_g", "mla_w_kv_b",
          "mla_w_q_a", "mla_q_norm_g", "mla_w_q_b", "mla_w_o", "router_w", "router_b", "moe_w_gate", "moe_w_up",
          "moe_w_down", "ln_g", "ln_b"]


def kernel(**inputs):
    import concourse.bacc as bacc
    from concourse.bass_utils import run_bass_kernel_spmd

    nc = bacc.Bacc("TRN2", target_bir_lowering=False, num_devices=1)
    arrays = {"in_shape_constants": shape_constants()}
    for name in INPUTS:
        arrays[f"in_{name}"] = np.ascontiguousarray(inputs[name])
    args = [nc.dram_tensor(n, a.shape, mybir.dt.from_np(a.dtype), kind="ExternalInput").ap()
            for n, a in arrays.items()]
    args.append(nc.dram_tensor("out_x", (1, SEQ, D), F32, kind="ExternalOutput").ap())
    build(nc, *args)
    r = run_bass_kernel_spmd(nc, [arrays], core_ids=[0])
    return r.results[0]["out_x"]
```

```python
import math
from contextlib import ExitStack

import numpy as np

import concourse.bass as bass
from concourse import mybir

F32 = mybir.dt.float32
F32R = mybir.dt.float32r
BF16 = mybir.dt.bfloat16
I32 = mybir.dt.int32
ALU = mybir.AluOpType
ACT = mybir.ActivationFunctionType
AX = mybir.AxisListType

P = 128
SEQ = 256
TT = SEQ // P
D = 1024
KD = D // P
CHUNK = 64
EPS = 1e-5
ALPHA = 4.0 ** 0.25
HEADS = 8
DH = 64
NOPE, ROPE, KVR, QR = 128, 64, 256, 384
LAMBDA_INIT = 0.8 - 0.6 * math.exp(-0.3 * 0)
MLA_SCALE = (NOPE + ROPE) ** -0.5
EXPERTS, GROUPS, FF = 32, 8, 256
PER_GROUP = EXPERTS // GROUPS
WIN = 64
ROUNDS = SEQ // WIN
PAIRS = EXPERTS // 2
SLOTS = 3
KEY = 1024
NSLOT = 2 * SEQ
BIG = 1e30
LOADED_TURNS = 4
LAST_SPLIT = 640
B_BANKS = (4, 5, 0, 1, 6, 7, 4, 5, 2, 3, 5, 6)
SORT_BANKS = (0, 1, 3, 4, 5, 6, 7, 2)
START_WAIT, NORM_WAIT, TOP_WAIT, SORT_WAIT = 12, (8, 4), 28, 8

GU = KD * FF
DN = (FF // P) * D
SLOT = 4 * GU + 2 * DN

CONST = {}
_at = 0
for _name, _n in (("ident", P), ("ones", P), ("dist", 3 * P), ("mask", 3 * P), ("cos", TT * 32), ("sin", TT * 32),
                  ("ecol", ROUNDS * PAIRS), ("rowc", 1), ("w8", GROUPS), ("w32", EXPERTS), ("key", EXPERTS),
                  ("fold", EXPERTS)):
    CONST[_name] = (_at, _at + _n)
    _at += _n
CONSTS = _at


def shape_constants():
    c = np.zeros((P, CONSTS + P), np.float32)

    def put(name, a):
        lo, hi = CONST[name]
        c[:, lo:hi] = a

    p = np.arange(P)
    put("ident", np.eye(P))
    put("ones", 1.0)
    q0, q1, k = p, p + P, np.arange(SEQ)

    def blocked(f):
        return np.concatenate([f(q0[:, None], k[None, :P]), f(q1[:, None], k[None, :])], axis=1)

    seen = blocked(lambda q, k: (k // CHUNK) <= (q // CHUNK))
    put("dist", np.where(seen, blocked(lambda q, k: np.abs(q - k)), BIG))
    put("mask", np.where(seen, 0.0, -BIG))
    inv = (np.float32(10000.0) ** (-np.arange(0, ROPE, 2, dtype=np.float32) / np.float32(ROPE))).astype(np.float32)
    ang = (np.arange(SEQ, dtype=np.float32)[:, None] * inv[None, :]).astype(np.float32).astype(np.float64)
    put("cos", np.cos(ang).reshape(TT, P, 32).transpose(1, 0, 2).reshape(P, -1))
    put("sin", np.sin(ang).reshape(TT, P, 32).transpose(1, 0, 2).reshape(P, -1))
    put("ecol", (2 * KEY * np.arange(PAIRS)[None, :] + WIN * np.arange(ROUNDS)[:, None]).reshape(1, -1))
    put("rowc", (p % WIN + KEY * (p // WIN))[:, None])
    put("w8", GROUPS - np.arange(GROUPS))
    put("w32", EXPERTS - np.arange(EXPERTS))
    put("key", KEY * np.arange(EXPERTS))
    put("fold", p[:, None] % EXPERTS == np.arange(EXPERTS))
    c[:, CONSTS:] = p[:, None] < p[None, :]
    return c


class Chain:

    def __init__(self, eng, sem):
        self.eng, self.sem, self.n = eng, sem, 0

    def __call__(self, ins):
        ins.then_inc(self.sem, 1)
        self.n += 1
        self.eng.wait_ge(self.sem, self.n)


class Phase:

    def __init__(self, sems, totals, layer):
        self.sems, self.totals, self.layer = sems, totals, layer

    def __getitem__(self, name):
        return self.sems[name]

    def __call__(self, name, n):
        return self.sems[name], n + self.layer * self.totals[name]


def build(nc, consts, x, diff_w_qkv, diff_lambda, diff_subln_g, diff_w_o, mla_w_kv_a, mla_kv_norm_g, mla_w_kv_b,
          mla_w_q_a, mla_q_norm_g, mla_w_q_b, mla_w_o, router_w, router_b, moe_w_gate, moe_w_up, moe_w_down,
          ln_g, ln_b, out):
    with ExitStack() as ctx:
        def sb(name, shape, dt=F32):
            return ctx.enter_context(nc.sbuf_tensor(name, shape, dt))

        def sb_and_rounded(name, shape):
            t = sb(name, shape)
            size = 4 * int(np.prod(shape[1:]))
            return t, nc.alloc_sbuf_tensor_at(name + "_rounded", shape, F32R, offset=nc.sbuf_base - size)

        def sem(name):
            return ctx.enter_context(nc.semaphore(name))

        ring, ring_r = zip(*(sb_and_rounded(f"ring{s}", [P, SLOT]) for s in range(SLOTS)))
        xs = sb("x_res", [P, TT, D])
        xT, xT_r = sb_and_rounded("x_T", [P, KD, SEQ])
        work, work_r = sb_and_rounded("work", [P, 8192])
        scratch, scratch_r = sb_and_rounded("scratch", [P, 1920])
        cst = sb("cst", [P, CONSTS])
        tri_b = sb("tri_b", [P, P], BF16)
        ones_b = sb("ones_b", [P, P], BF16)
        zeros_b = sb("zeros_b", [P, 512], BF16)
        rb = sb("router_b_sb", [P, EXPERTS])
        eps = sb("eps", [P, 1])
        subg = sb("subln_g_sb", [P, 1])
        qg = sb("q_norm_g_sb", [P, QR // P])
        kvg = sb("kv_norm_g_sb", [P, KVR // P])
        gcol = sb("ln_g_cols", [P, 3, KD])
        bcol = sb("ln_b_cols", [P, 3, KD])
        nlam = sb("neg_lambda", [P, 1])
        ln_stats = sb("ln_stats", [P, TT, 2, 6])
        ln_mv = sb("ln_mean_var", [P, TT, 2])
        ln_sd = sb("ln_sd", [P, TT])
        ln_rstd = sb("ln_rstd", [P, TT])
        ln_nb = sb("ln_neg_mean_rstd", [P, TT])
        small = sb("small", [P, 64])
        offs = sb("window_offsets", [P, ROUNDS * EXPERTS + 2], I32)

        ident, ones = (cst[:, slice(*CONST[n])] for n in ("ident", "ones"))
        dist, mask = (cst[:, slice(*CONST[n])] for n in ("dist", "mask"))
        cos, sin = (cst[:, slice(*CONST[n])].rearrange("p (t f) -> p t f", t=TT) for n in ("cos", "sin"))
        ecol, rowc = (cst[:, slice(*CONST[n])] for n in ("ecol", "rowc"))
        w8, w32, ekey, fold = (cst[:, slice(*CONST[n])] for n in ("w8", "w32", "key", "fold"))
        tri_f = work[:, 8064:8192]

        psum = ctx.enter_context(nc.psum_tensor("psum", [P, 8, 512], F32))

        def qkv_chunk(r, c):
            a = (c % 3) * 4096
            return r[2 - c // 3][:, a:a + 4096].rearrange("p (k n) -> p k n", k=KD)

        w_hi = ring_r[0][:, 0:8192].rearrange("p (b k n) -> p b k n", b=2, k=KD)
        x_lo = ring_r[0][:, 8192:10240].rearrange("p (k t) -> p k t", k=KD)
        wo_a, wo_b = 0, 4096

        def wo(r, at_, h):
            return r[2][:, at_ + h * D:at_ + (h + 1) * D]

        def wo_hi(at_, h):
            a = (8192 if h < 4 or at_ == wo_a else 0) + (h % 4) * D
            return ring_r[1 + h // 4][:, a:a + D]

        qz = work[:, 0:4096].rearrange("p (h c t) -> p h c t", h=HEADS, c=2)
        kT = work[:, 4096:6144].rearrange("p (h t) -> p h t", h=HEADS)
        v = work[:, 6144:8192].rearrange("p (t n) -> p t n", t=TT)
        o_sb = qz[:, :, 0, :]
        o_sq = qz[:, :, 1, :]
        oT = xT_r
        o_lo_a = work_r[:, 0:4096].rearrange("p (h c t) -> p h c t", h=HEADS, c=2)[:, :, 1, :]
        o_lo_b = work_r[:, 0:2048].rearrange("p (h t) -> p h t", h=HEADS)
        x_flat = xT.rearrange("p k t -> p (k t)")
        lg = [a.rearrange("p (c n) -> p c n", c=2) for a in (
            scratch[:, 0:768], scratch[:, 768:1536], x_flat[:, 0:768], x_flat[:, 768:1536])]
        aT = [scratch[:, 1536:1920], x_flat[:, 1536:1920]]
        lam_in = scratch[:, 0:256].rearrange("p (i d) -> p i d", i=4)
        lam_prod = scratch[:, 256:384].rearrange("p (i d) -> p i d", i=2)
        lam_dot = small[:, 28:30]
        kva = ring[1][:, 0:2560].rearrange("p (k n) -> p k n", k=KD)
        qa = ring[1][:, 2560:5632].rearrange("p (k n) -> p k n", k=KD)
        qb, qb_lo = (r[1][:, 5632:10240].rearrange("p (k n) -> p k n", k=QR // P) for r in (ring, ring_r))
        kvb, kvb_lo = (r[2][:, 0:4096].rearrange("p (k n) -> p k n", k=KVR // P) for r in (ring, ring_r))
        qb_hi = ring_r[0][:, 0:4608].rearrange("p (k n) -> p k n", k=QR // P)
        kvb_hi = ring_r[0][:, 4608:8704].rearrange("p (k n) -> p k n", k=KVR // P)
        cq_lo = ring_r[0][:, 8704:9472].rearrange("p (k t) -> p k t", k=QR // P)
        ckv_lo = ring_r[0][:, 9472:9984].rearrange("p (k t) -> p k t", k=KVR // P)
        b_parts = [(qb[:, k, :], qb_hi[:, k, :], qb_lo[:, k, :]) for k in range(QR // P)]
        b_parts += [(kvb[:, k, :], kvb_hi[:, k, :], kvb_lo[:, k, :]) for k in range(KVR // P)]
        qnT = work[:, 0:2048].rearrange("p (h t) -> p h t", h=HEADS)
        qrz = work[:, 2048:4096].rearrange("p (h t) -> p h t", h=HEADS)
        knT = kT
        c_q = work[:, 6144:6912].rearrange("p (t n) -> p t n", t=TT)
        c_kv = work[:, 6912:7424].rearrange("p (t n) -> p t n", t=TT)
        kr_raw = work[:, 7424:7552].rearrange("p (t n) -> p t n", t=TT)
        kr2 = work[:, 7552:7808].rearrange("p (t n) -> p t n", t=TT)
        sq_junk = work[:, 7808:8192]
        qr_raw = xT[:, 0:4, :].rearrange("p a b -> p (a b)").rearrange("p (t h d) -> p t h d", t=TT, h=HEADS)
        qr_rot = xT[:, 4:8, :].rearrange("p a b -> p (a b)").rearrange("p (t h d) -> p t h d", t=TT, h=HEADS)
        cqT = scratch_r[:, 0:768].rearrange("p (k t) -> p k t", k=QR // P)
        ckvT = scratch_r[:, 768:1280].rearrange("p (k t) -> p k t", k=KVR // P)
        krT2 = scratch[:, 1280:1536]
        rope_tmp = scratch[:, 1536:1792].rearrange("p (h d) -> p h d", h=HEADS)
        rope_tmp2 = sq_junk[:, 0:256].rearrange("p (h d) -> p h d", h=HEADS)
        mlg = [scratch[:, 0:384], scratch[:, 384:768], scratch[:, 1536:1920]]
        pT = [scratch[:, 768:1152], ring[2][:, 0:384]]
        gb = [a.rearrange("p (s n) -> p s n", s=2) for a in (
            work[:, 4096:6144], ring[1][:, 10240:SLOT], work[:, 4096:6144], work[:, 0:2048])]
        XW = NSLOT + WIN
        xsT = work[:, 0:KD * XW].rearrange("p (k s) -> p k s", k=KD)
        xg = work[:, KD * XW:KD * XW + SLOTS * KD * P].rearrange("p (b k c) -> p b k c", b=SLOTS, k=KD)
        top = work[:, KD * XW + 2 * KD * P:KD * XW + 3 * KD * P]
        rw = work[:, 7680:7936].rearrange("p (k e) -> p k e", k=KD)
        hi_parts = [xT_r[:, 4:8, :].rearrange("p a b -> p (a b)").rearrange("p (k n) -> p k n", k=KD),
                    work_r[:, 7680:8192].rearrange("p (k n) -> p k n", k=4),
                    work_r[:, 7 * XW:7 * XW + NSLOT].rearrange("p (k n) -> p k n", k=4)]
        hi_of = [(0, 0, KD), (1, 0, 4), (1, 4, KD)]
        xs_lo = work_r[:, KD * XW:KD * XW + TT * D].rearrange("p (t k n) -> p t k n", t=TT, k=KD)

        def xs_tiles(t, k0, k1):
            return xs[:, t, :].rearrange("p (n k) -> p k n", k=KD)[:, k0:k1, :]

        def xs_hi(t, k):
            part, first = (0, 0) if t == 0 else (1 + k // 4, 4 * (k // 4))
            return hi_parts[part][:, k - first, :]

        onehot_r = xT_r[:, 0:4, :].rearrange("p a b -> p (a b)").rearrange("p (t s) -> p t s", t=TT)
        y_sb = xT[:, 0:4, :].rearrange("p a b -> p (a b)")
        key_row = xT[:, 4:6, :]
        gate_row = xT[:, 6:8, :]
        diag = scratch[:, 768:1792].rearrange("p (t q n) -> p t q n", t=TT, q=4)
        logit_T = scratch[:, 0:256]
        iota = scratch[:, 256:768]
        comb = scratch[:, 0:768].rearrange("p (b t) -> p b t", b=SLOTS)
        act_s = scratch[:, 768:1024]
        h_sb = scratch[:, 1024:1280]
        hT = scratch[:, 1280:1536].rearrange("p (k c) -> p k c", k=FF // P)
        g_tmp = scratch[:, 1536:1792]

        def slot_gu(s, j):
            a = j * 2 * GU
            return ring[s][:, a:a + 2 * GU].rearrange("p (u k f) -> p u k f", u=2, k=KD)

        def slot_dn(s, j):
            a = 4 * GU + j * DN
            return ring[s][:, a:a + DN].rearrange("p (k n) -> p k n", k=FF // P)

        ld_x, ld_wo, ld_rw = sem("ld_x"), sem("ld_wo"), sem("ld_router")
        MISC = 7
        ld_ident, ld_cst, ld_misc, ld_lam = sem("ld_ident"), sem("ld_cst"), sem("ld_misc"), sem("ld_lam")
        x_hi_ready, w_hi_ready, w_lo_ready, w_pool_ready = (
            sem(n) for n in ("x_hi_ready", "w_hi_ready", "w_lo_ready", "w_pool_ready"))
        ld_qkv = [sem(f"ld_qkv{c}") for c in range(6)]
        ld_qkv0b = sem("ld_qkv0b")
        ld_kva, ld_qa, ld_qb, ld_kvb = (sem(n) for n in ("ld_kva", "ld_qa", "ld_qb", "ld_kvb"))
        sems = {"gb": sem("ld_ln")}
        ld_gb = [Phase(sems, {"gb": 32}, n) for n in range(4)]
        cast_ready, zeroed, lam_ready, lam_exp = (sem(n) for n in ("cast_ready", "zeroed", "lam_ready", "lam_exp"))
        totals = {"ps": 4, "sb": KD}
        sems = {n: sem("xt_" + n) for n in totals}
        xt = [Phase(sems, totals, n) for n in range(4)]
        qkv_ps, qkv_act, qkv_dve = sem("qkv_ps"), sem("qkv_act"), sem("qkv_dve")
        totals = {"sc_ps": 2 * HEADS, "sc_read": 2 * HEADS, "mx_ready": 2 * HEADS, "e_ready": 4 * HEADS,
                  "r_ready": HEADS, "e1_scaled": 2 * HEADS, "p_ready": 2 * HEADS, "pt_ps": HEADS, "pt_sb": HEADS,
                  "o_ps": HEADS, "o_sb": HEADS}
        sems = {n: sem(n) for n in totals}
        at = [Phase(sems, totals, l) for l in range(2)]
        sq_ready, ss_ready, sd_ready, rs_ready = sem("sq_ready"), sem("ss_ready"), sem("sd_ready"), sem("rs_ready")
        on_dve, on_pool, ot_ps, ot_sb = sem("on_dve"), sem("on_pool"), sem("ot_ps"), sem("ot_sb")
        o_lo_ready = sem("o_lo_ready")
        wo_ps = sem("wo_ps")
        totals = {"var": TT, "sd": TT, "rstd": TT, "norm": TT + 1, "x_dve": 1, "x_pool": 1}
        sems = {n: sem("ln_" + n) for n in totals}
        ln = [Phase(sems, totals, n) for n in range(4)]
        mq = {n: sem("mla_" + n) for n in (
            "a_ps", "sd", "c_ready", "kr_rot", "ct_ps", "c_hi", "ct_sb", "w_hi", "w_lo", "qr_ps", "qr_raw", "qr_rot_dve",
            "qr_rot_pool", "b_ps", "b_act", "b_dve", "qt_ps", "qt_sb", "krt_ps", "krt_sb")}
        totals = {"lgt_ps": 1, "lgt_sb": 1, "lg_ps": 1, "score": 1, "m_ready": 1, "cnt_ps": 1, "cnt_sb": 1,
                  "rank_ps": 1, "offs_ready": 1,
                  "iota_ready": 1, "hi_ready": 3, "lo_ready": 3, "hot_ready": TT, "pad_zero": 1, "key_ready": 1, "sort_ps": KD, "sort_act": KD // 2,
                  "sort_dve": KD // 2, "diag_ready": 4 * TT, "row_ps": 1, "row_sb_a": TT, "row_sb_d": TT,
                  "xg0_ready": 2, "gate0_ps": 1, "xg_ready": 2 * PAIRS - 2, "gu_ps": PAIRS, "s_ready": PAIRS, "h_ready": PAIRS, "ht_ps": PAIRS,
                  "ht_sb": PAIRS, "y0_ps": PAIRS, "y_ps": PAIRS, "y_act": PAIRS, "y_dve": PAIRS, "g_part": 2 * PAIRS,
                  "g_ready": PAIRS, "c_ps": PAIRS, "sum_ps": TT}
        sems = {n: sem("moe_" + n) for n in totals}
        mo = [Phase(sems, totals, l) for l in range(2)]
        uses = [len(range(s, PAIRS, SLOTS)) for s in range(SLOTS)]
        sems = [{n: sem(f"ring_{n}{s}") for n in ("gate", "up", "dn")} for s in range(SLOTS)]
        rings = [[Phase(sems[s], {"gate": 32 * uses[s], "up": 32 * uses[s], "dn": 32 * uses[s]}, l) for s in range(SLOTS)]
                 for l in range(2)]
        names = ("w", "xg", "gu", "s", "h", "ht_ps", "ht_sb", "y_ps", "y_act", "y_dve", "g_part", "g", "free")
        ov = [{n: sem(f"ov_{n}{l}") for n in names} for l in range(2)]
        out_done = sem("out_done")
        dve_chain, act_chain, pool_chain = sem("dve_chain"), sem("act_chain"), sem("pool_chain")

        def for_pairs_4_up(eng, body):
            with eng.Fori(0, (PAIRS - 4) // SLOTS) as it:
                for j in range(SLOTS):
                    body(it * SLOTS + (4 + j), (4 + j) % SLOTS)

        def for_pairs_1_up(eng, body):
            with eng.Fori(0, (PAIRS - 1) // SLOTS) as it:
                for j in range(SLOTS):
                    body(it * SLOTS + (1 + j), (1 + j) % SLOTS)

        def overflow_steps(eng, body):
            with eng.Fori(1, ROUNDS) as r:
                with eng.Fori(0, PAIRS) as i:
                    body(i, r, (r - 1) * PAIRS + i)

        def overflows(eng, l):
            eng.wait_ge(*mo[l]("offs_ready", 1))
            n = eng.value_load(offs[0:1, ROUNDS * EXPERTS:ROUNDS * EXPERTS + 1], min_val=0, max_val=SEQ)
            return n > WIN

        def routing():
            c, at_ = {}, 0
            for name, n in (("score", 64), ("sel", 64), ("mx2", 32), ("sm2", 32), ("t1", 16), ("t2", 16),
                            ("gs", 16), ("gmax", 2), ("gkey", 16), ("gmask", 16), ("masked", 64), ("m1", 2),
                            ("e1", 64), ("k1", 2), ("oh", 128), ("prod", 128), ("cnt", 32), ("pre", 64),
                            ("rank", 64), ("chosen", 32), ("cnt_col", 64)):
                c[name] = top[:, at_:at_ + n]
                at_ += n
            c["cnt_col"] = c["cnt_col"].bitcast(BF16)[0:EXPERTS, :]
            c["chosen"] = c["chosen"].bitcast(BF16).rearrange("p (t e) -> p t e", t=TT)
            return c

        def rotate(eng, link, dst, src, t, tmp, heads):
            shape = [P, heads, 32]
            c = cos[:, t, :].unsqueeze(1).broadcast_to(shape)
            s = sin[:, t, :].unsqueeze(1).broadcast_to(shape)
            lo, hi = slice(0, 32), slice(32, 64)
            link(eng.tensor_tensor(dst[:, :, lo], src[:, :, lo], c, ALU.mult))
            link(eng.tensor_tensor(tmp, src[:, :, hi], s, ALU.mult))
            link(eng.tensor_tensor(dst[:, :, lo], dst[:, :, lo], tmp, ALU.subtract))
            link(eng.tensor_tensor(dst[:, :, hi], src[:, :, hi], c, ALU.mult))
            link(eng.tensor_tensor(tmp, src[:, :, lo], s, ALU.mult))
            return eng.tensor_tensor(dst[:, :, hi], dst[:, :, hi], tmp, ALU.add)

        block = ctx.enter_context(nc.Block())

        @block.sync
        def _(sp):
            sp.dma_start(ident, consts[:, 0:P]).then_inc(ld_ident, 16)
            for t in range(TT):
                sp.dma_start(xs[:, t, :], x[0, t * P:(t + 1) * P, :]).then_inc(ld_x, 16)
            wq = diff_w_qkv[0].rearrange("(p k) n -> p k n", k=KD)
            for half, ld in enumerate((ld_qkv[0], ld_qkv0b)):
                cols = slice(half * 256, (half + 1) * 256)
                sp.dma_start(qkv_chunk(ring, 0)[:, :, cols], wq[:, :, cols]).then_inc(ld, 16)
            for c in range(1, 6):
                sp.dma_start(qkv_chunk(ring, c), wq[:, :, c * 512:(c + 1) * 512]).then_inc(ld_qkv[c], 16)
                if c == 1:
                    sp.dma_start(cst[:, P:], consts[:, P:CONSTS]).then_inc(ld_cst, 16)

            def load_wo(w, at_):
                sp.dma_start(ring[2][:, at_:at_ + HEADS * D].rearrange("p (h n) -> p h n", h=HEADS),
                             w[0].rearrange("(h p) n -> p h n", p=P)).then_inc(ld_wo, 16)

            sp.wait_ge(qkv_ps, 4)
            load_wo(diff_w_o, wo_a)

            def load_gate_up(l, i, s, which=(0, 1)):
                for u in which:
                    for j in range(2):
                        sp.dma_start(slot_gu(s, j)[:, u, :, :], (moe_w_gate, moe_w_up)[u][l, i * 2 + j]
                                     .rearrange("(p k) f -> p k f", k=KD)).then_inc(rings[l][s][("gate", "up")[u]], 16)

            def load_down(l, i, s):
                for j in range(2):
                    sp.dma_start(slot_dn(s, j), moe_w_down[l, i * 2 + j].rearrange("(k p) n -> p k n", p=P))\
                      .then_inc(rings[l][s]["dn"], 16)

            def load_pair(l, i, s):
                load_gate_up(l, i, s)
                load_down(l, i, s)

            def load_ln(n):
                sp.dma_start(gb[n][:, 0, :], ln_g[n // 2, n % 2].partition_broadcast(P)).then_inc(ld_gb[n]["gb"], 16)
                sp.dma_start(gb[n][:, 1, :], ln_b[n // 2, n % 2].partition_broadcast(P)).then_inc(ld_gb[n]["gb"], 16)

            def load_router(l):
                sp.wait_ge(*at[l]("o_ps", HEADS))
                sp.dma_start(rw, router_w.rearrange("(p k) n -> p k n", k=KD)).then_inc(ld_rw, 16)

            def moe(l):
                def reload(i, s):
                    sp.wait_ge(*mo[l]("gu_ps", i - 2))
                    load_gate_up(l, i, s)
                    sp.wait_ge(*mo[l]("y_ps", i - 2))
                    load_down(l, i, s)

                sp.wait_ge(*mo[l]("gate0_ps", 1))
                load_gate_up(l, 3, 0, (0,))
                sp.wait_ge(*mo[l]("gu_ps", 1))
                load_gate_up(l, 3, 0, (1,))
                sp.wait_ge(*mo[l]("y_ps", 1))
                load_down(l, 3, 0)
                for_pairs_4_up(sp, reload)

            def overflow(l):
                with sp.If(overflows(sp, l)):
                    sp.wait_ge(*mo[l]("y_ps", PAIRS))

                    def step(i, r, n):
                        sp.wait_ge(ov[l]["free"], n + 1)
                        for j in range(2):
                            for u, w in enumerate((moe_w_gate, moe_w_up)):
                                sp.dma_start(slot_gu(0, j)[:, u, :, :],
                                             w[l, i * 2 + j].rearrange("(p k) f -> p k f", k=KD))\
                                  .then_inc(ov[l]["w"], 16)
                            sp.dma_start(slot_dn(0, j), moe_w_down[l, i * 2 + j].rearrange("(k p) n -> p k n", p=P))\
                              .then_inc(ov[l]["w"], 16)

                    overflow_steps(sp, step)
                    sp.wait_ge(ov[l]["y_ps"], PAIRS * (ROUNDS - 1))

            sp.wait_ge(qkv_ps, 12)
            load_pair(0, 0, 0)
            load_gate_up(0, 1, 1)
            sp.wait_ge(*at[0]("sc_ps", 2 * HEADS))
            load_ln(0)
            load_router(0)
            sp.wait_ge(wo_ps, 4)
            load_down(0, 1, 1)
            load_pair(0, 2, 2)
            moe(0)
            sp.wait_ge(*mo[0]("gu_ps", 14))
            sp.dma_start(qa, mla_w_q_a[0].rearrange("(p k) n -> p k n", k=KD)).then_inc(ld_qa, 16)
            sp.dma_start(kva, mla_w_kv_a.rearrange("(p k) n -> p k n", k=KD)).then_inc(ld_kva, 16)
            sp.wait_ge(*mo[0]("y_ps", 14))
            load_ln(1)
            sp.dma_start(qb, mla_w_q_b[0].rearrange("(k p) n -> p k n", p=P)).then_inc(ld_qb, 16)
            sp.wait_ge(*mo[0]("y_ps", 15))
            sp.dma_start(kvb, mla_w_kv_b.rearrange("(k p) n -> p k n", p=P)).then_inc(ld_kvb, 16)
            load_wo(mla_w_o, wo_b)
            overflow(0)
            sp.wait_ge(mq["b_ps"], 12)
            sp.wait_ge(*ln[1]("x_dve", 1))
            sp.wait_ge(*ln[1]("x_pool", 1))
            load_pair(1, 0, 0)
            load_gate_up(1, 1, 1)
            sp.wait_ge(*at[1]("sc_ps", HEADS))
            load_ln(2)
            load_router(1)
            sp.wait_ge(wo_ps, 8)
            load_down(1, 1, 1)
            load_pair(1, 2, 2)
            moe(1)
            overflow(1)
            sp.wait_ge(*mo[1]("xg_ready", 2 * PAIRS - 2))
            load_ln(3)
            sp.wait_ge(*ln[3]("x_pool", 1))
            for t in range(TT):
                sp.wait_ge(*ln[3]("x_dve", t + 1))
                sp.dma_start(out[0, t * P:(t + 1) * P, :], xs[:, t, :]).then_inc(out_done, 16)
            sp.wait_ge(out_done, 16 * TT)

        @block.tensor
        def _(pe):
            def mm(dst, lhsT, rhs, start, stop):
                return pe.matmul(dst, lhsT, rhs, start=start, stop=stop, skip_group_check=True)

            def keep_clock(n, bank=4):
                for _ in range(n):
                    mm(psum[:, bank, :], zeros_b[:, 0:P], zeros_b[:, :], True, True)

            def transpose_x(n):
                for t in range(TT):
                    if n:
                        keep_clock(NORM_WAIT[t], (4, 0)[t])
                        pe.wait_ge(*ln[n - 1]("norm", (1, 3)[t]))
                    for k in range(KD):
                        at_ = (k % 2) * SEQ + t * P
                        last = pe.transpose(psum[:, 4 + k // 2, at_:at_ + P], xs[:, t, k::KD], ident)
                        if t and k % 2:
                            last.then_inc(xt[n]["ps"], 1)
                pe.wait_ge(*xt[n]("sb", KD))

            def products(dst, lhsT, rhs, first, last):
                (a_hi, a_lo), (b_hi, b_lo) = lhsT, rhs
                mm(dst, a_hi, b_hi, first, False)
                mm(dst, a_hi, b_lo, False, False)
                return mm(dst, a_lo, b_hi, False, last)

            def out_projection(l, w, o_lo):
                for t in range(TT):
                    tok = slice(t * P, (t + 1) * P)
                    for c in range(2):
                        cols = slice(c * 512, (c + 1) * 512)
                        for h in range(HEADS):
                            if t == 0 and c == 0 and h < 4:
                                pe.wait_ge(w_pool_ready, 4 * l + h + 1)
                            if t == 0 and c == 0 and h >= 4:
                                pe.wait_ge(w_lo_ready, 24 + 4 * l + h - 3)
                            last = products(psum[:, 2 * t + c, :], (oT[:, h, tok], o_lo[:, h, tok]),
                                            (wo_hi(w, h)[:, cols], wo(ring_r, w, h)[:, cols]), h == 0, h == HEADS - 1)
                        last.then_inc(wo_ps, 1)

            def diff_attention():
                pe.wait_ge(cast_ready, 1)
                keep_clock(START_WAIT)
                pe.wait_ge(ld_ident, 16)
                pe.wait_ge(ld_x, 16 * TT)
                transpose_x(0)
                g = 0
                for c in range(4):
                    for m in range(4):
                        pe.wait_ge(w_lo_ready, 4 * c + m + 1)
                        cols = slice(m * P, (m + 1) * P)
                        for k in range(KD):
                            last = products(psum[:, g % 8, (m % 2) * SEQ:(m % 2 + 1) * SEQ],
                                            (w_hi[:, c % 2, k, cols], qkv_chunk(ring_r, c)[:, k, cols]),
                                            (xT_r[:, k, :], x_lo[:, k, :]), k == 0, k == KD - 1)
                        if m % 2:
                            last.then_inc(qkv_ps, 1)
                            g += 1
                s = at[0]

                def scores(h):
                    if h >= 2:
                        pe.wait_ge(*s("sc_read", 2 * (h - 1)))
                    for c in range(2):
                        bank = psum[:, 2 * (h % 2) + c, :]
                        mm(bank[:, 0:P], qz[:, h, c, 0:P], kT[:, h, 0:P], True, True)
                        mm(bank[:, P:3 * P], qz[:, h, c, P:SEQ], kT[:, h, :], True, True).then_inc(s["sc_ps"], 1)

                for c in range(4, 6):
                    pe.wait_ge(w_lo_ready, 4 * c + 4)
                    for t in range(TT):
                        pe.wait_ge((qkv_act, qkv_dve)[g % 2], 4 + (g - 8) // 2 + 1)
                        tok = slice(t * P, (t + 1) * P)
                        for k in range(KD):
                            last = products(psum[:, g - 4, :], (xT_r[:, k, tok], x_lo[:, k, tok]),
                                            (w_hi[:, c % 2, k, :], qkv_chunk(ring_r, c)[:, k, :]), k == 0, k == KD - 1)
                        last.then_inc(qkv_ps, 1)
                        g += 1
                    if c == 4:
                        pe.wait_ge(qkv_act, 6)
                        pe.wait_ge(qkv_dve, 6)
                        pe.wait_ge(zeroed, 2)
                        scores(0)
                        scores(1)
                scores(2)
                pe.wait_ge(qkv_act, 8)
                pe.wait_ge(qkv_dve, 8)

                def transposes(h):
                    pe.wait_ge(*s("p_ready", 2 * (h + 1)))
                    if h >= 2:
                        pe.wait_ge(*s("pt_sb", h - 1))
                    for b in range(3):
                        last = pe.transpose(psum[:, 4 + h % 2, b * P:(b + 1) * P], lg[h % 4][:, 0, b * P:(b + 1) * P],
                                            ident)
                    last.then_inc(s["pt_ps"], 1)

                def values(h):
                    pe.wait_ge(*s("pt_sb", h + 1))
                    if h >= 2:
                        pe.wait_ge(*s("o_sb", h - 1))
                    bank = psum[:, 6 + h % 2, :]
                    hv = slice(h * P, (h + 1) * P)
                    a = aT[h % 2]
                    mm(bank[:, 0:P], a[:, 0:P], v[:, 0, hv], True, True)
                    mm(bank[:, P:SEQ], a[:, P:2 * P], v[:, 0, hv], True, False)
                    mm(bank[:, P:SEQ], a[:, 2 * P:3 * P], v[:, 1, hv], False, True).then_inc(s["o_ps"], 1)

                for h in range(HEADS):
                    if 1 <= h < HEADS - 3:
                        scores(h + 3)
                    transposes(h)
                    if h == 0:
                        scores(3)
                    if h >= 1:
                        values(h - 1)
                values(HEADS - 1)
                keep_clock(NORM_WAIT[0], 0)
                for b in range(4):
                    pe.wait_ge(on_dve, min(b + 1, 2))
                    if b >= 2:
                        pe.wait_ge(on_pool, 1)
                    for h in (2 * b, 2 * b + 1):
                        for t in range(TT):
                            a = (h % 2) * SEQ + t * P
                            last = pe.transpose(psum[:, 4 + b, a:a + P], o_sb[:, h, t * P:(t + 1) * P], ident)
                    last.then_inc(ot_ps, 1)
                keep_clock(NORM_WAIT[1], 0)
                pe.wait_ge(ot_sb, 4)
                out_projection(0, wo_a, o_lo_a)

            def mla_attention():
                transpose_x(2)
                pe.wait_ge(ld_qa, 16)
                for t in range(TT):
                    for k in range(KD):
                        last = mm(psum[:, 2 + t, 0:QR], xT[:, k, t * P:(t + 1) * P], qa[:, k, :], k == 0, k == KD - 1)
                    last.then_inc(mq["a_ps"], 1)
                pe.wait_ge(ld_kva, 16)
                for t in range(TT):
                    for k in range(KD):
                        last = mm(psum[:, t, 0:KVR + ROPE], xT[:, k, t * P:(t + 1) * P], kva[:, k, :],
                                  k == 0, k == KD - 1)
                    last.then_inc(mq["a_ps"], 1)
                pe.wait_ge(mq["c_ready"], 2)
                for k in range(QR // P):
                    for t in range(TT):
                        a = (k % 2) * SEQ + t * P
                        last = pe.transpose(psum[:, 4 + k // 2, a:a + P], c_q[:, t, k * P:(k + 1) * P], ident)
                last.then_inc(mq["ct_ps"], 1)
                pe.wait_ge(mq["c_ready"], 4)
                for k in range(KVR // P):
                    for t in range(TT):
                        a = k * SEQ + t * P
                        last = pe.transpose(psum[:, 6, a:a + P], c_kv[:, t, k * P:(k + 1) * P], ident)
                last.then_inc(mq["ct_ps"], 1)
                pe.wait_ge(mq["w_lo"], 3)
                pe.wait_ge(mq["ct_sb"], 3)
                q_w = [w.rearrange("p k (h n) -> p k h n", h=HEADS) for w in (qb_hi, qb_lo)]
                kv_w = [w.rearrange("p k (h n) -> p k h n", h=HEADS) for w in (kvb_hi, kvb_lo)]
                for t in range(TT):
                    tok = slice(t * P, (t + 1) * P)
                    for k in range(QR // P):
                        last = products(psum[:, 2 + t, :], (cqT[:, k, tok], cq_lo[:, k, tok]),
                                        [w[:, k, :, NOPE:] for w in q_w], k == 0, k == QR // P - 1)
                    last.then_inc(mq["qr_ps"], 1)
                def group(g):
                    if g in (6, 7):
                        pe.wait_ge((mq["b_act"], mq["b_dve"])[g % 2], 1)
                    if g == 4:
                        pe.wait_ge(mq["w_lo"], 5)
                        pe.wait_ge(mq["ct_sb"], 5)
                    if g == 8:
                        pe.wait_ge(mq["qr_raw"], 2)
                    if g == 10:
                        pe.wait_ge(mq["b_dve"], 4)
                    if g == 11:
                        pe.wait_ge(mq["krt_sb"], 1)
                    if g < 8:
                        w, src, n = (q_w, (cqT, cq_lo), QR // P) if g < 4 else (kv_w, (ckvT, ckv_lo), KVR // P)
                        for h in (2 * (g % 4), 2 * (g % 4) + 1):
                            for k in range(n):
                                last = products(psum[:, B_BANKS[g], (h % 2) * SEQ:(h % 2 + 1) * SEQ],
                                                [a[:, k, h, 0:NOPE] for a in w], [a[:, k, :] for a in src],
                                                k == 0, k == n - 1)
                    else:
                        t, half = (g - 8) // 2, (g - 8) % 2
                        tok = slice(t * P, (t + 1) * P)
                        for k in range(KVR // P):
                            last = products(psum[:, B_BANKS[g], :], (ckvT[:, k, tok], ckv_lo[:, k, tok]),
                                            [w[:, k, 4 * half:4 * half + 4, NOPE:] for w in kv_w],
                                            k == 0, k == KVR // P - 1)
                    last.then_inc(mq["b_ps"], 1)

                for g in range(9):
                    group(g)
                pe.wait_ge(mq["kr_rot"], 1)
                pe.wait_ge(mq["b_act"], 4)
                pe.wait_ge(mq["b_dve"], 4)
                for t in range(TT):
                    last = pe.transpose(psum[:, 6, t * P:(t + 1) * P], kr2[:, t, :], ident)
                last.then_inc(mq["krt_ps"], 1)
                pe.wait_ge(mq["qr_rot_dve"], 1)
                pe.wait_ge(mq["qr_rot_pool"], 1)
                for b in range(2):
                    for hp in (2 * b, 2 * b + 1):
                        for t in range(TT):
                            a = (hp % 2) * SEQ + t * P
                            last = pe.transpose(psum[:, (7, 4)[b], a:a + P],
                                                qr_rot[:, t, 2 * hp:2 * hp + 2, :].rearrange("p h d -> p (h d)"), ident)
                    last.then_inc(mq["qt_ps"], 1)
                group(9)
                s = at[1]
                pe.wait_ge(mq["krt_sb"], 1)
                pe.wait_ge(zeroed, 4)
                pe.wait_ge(mq["qt_sb"], 4)

                def scores(h):
                    if h >= 2:
                        pe.wait_ge(*s("sc_read", h - 1))
                    bank = psum[:, h % 2, :]
                    mm(bank[:, 0:P], qnT[:, h, 0:P], knT[:, h, 0:P], True, False)
                    mm(bank[:, 0:P], qrz[:, h, 0:P], krT2[:, 0:P], False, True)
                    mm(bank[:, P:3 * P], qnT[:, h, P:SEQ], knT[:, h, :], True, False)
                    mm(bank[:, P:3 * P], qrz[:, h, P:SEQ], krT2, False, True).then_inc(s["sc_ps"], 1)

                scores(0)
                scores(1)
                group(10)
                group(11)
                scores(2)
                pe.wait_ge(mq["b_act"], 6)
                pe.wait_ge(mq["b_dve"], 6)

                def transposes(h):
                    pe.wait_ge(*s("p_ready", 2 * (h + 1)))
                    if h >= 2:
                        pe.wait_ge(*s("pt_sb", h - 1))
                    for b in range(3):
                        last = pe.transpose(psum[:, 2 + h % 2, b * P:(b + 1) * P], mlg[h % 3][:, b * P:(b + 1) * P],
                                            ident)
                    last.then_inc(s["pt_ps"], 1)

                def values(h):
                    pe.wait_ge(*s("pt_sb", h + 1))
                    if h >= 2:
                        pe.wait_ge(o_lo_ready, h - 1)
                    bank = psum[:, 4 + h % 2, :]
                    hv = slice(h * P, (h + 1) * P)
                    mm(bank[:, 0:SEQ], v[:, 0, hv], pT[h % 2][:, 0:SEQ], True, False)
                    mm(bank[:, P:SEQ], v[:, 1, hv], pT[h % 2][:, SEQ:3 * P], False, True).then_inc(s["o_ps"], 1)

                for h in range(HEADS):
                    if 1 <= h < HEADS - 3:
                        scores(h + 3)
                    transposes(h)
                    if h == 0:
                        scores(3)
                    if h >= 1:
                        values(h - 1)
                values(HEADS - 1)
                pe.wait_ge(o_lo_ready, HEADS)
                out_projection(1, wo_b, o_lo_b)

            def moe(l):
                m = mo[l]
                transpose_x(2 * l + 1)
                pe.wait_ge(ld_rw, 16 * (l + 1))
                for k in range(KD):
                    rows = slice((k % 4) * EXPERTS, (k % 4 + 1) * EXPERTS)
                    last = mm(psum[rows, 0, 0:SEQ], rw[:, k, :], xT[:, k, :], k < 4, k >= 4)
                last.then_inc(m["lgt_ps"], 1)
                pe.wait_ge(*m("lgt_sb", 1))
                for t in range(TT):
                    last = mm(psum[:, 1, t * EXPERTS:(t + 1) * EXPERTS], logit_T[:, t * P:(t + 1) * P], fold, True, True)
                last.then_inc(m["lg_ps"], 1)
                pe.wait_ge(cast_ready, 3)
                keep_clock(TOP_WAIT)
                pe.wait_ge(*m("m_ready", 1))
                chosen = routing()["chosen"]
                count = psum[0:EXPERTS, 3, 0:P]
                for t in range(TT):
                    last = mm(count, chosen[:, t, :], ones_b[:, :], t == 0, t == TT - 1)
                last.then_inc(m["cnt_ps"], 1)
                rank = psum[:, 2, :]
                mm(rank[:, 0:32], tri_b[:, :], chosen[:, 0, :], True, True)
                mm(rank[:, 32:64], tri_b[:, :], chosen[:, 1, :], True, False)
                mm(rank[:, 32:64], ones_b[:, :], chosen[:, 0, :], False, True)
                mm(rank[:, 128:160], ones_b[:, :], chosen[:, 0, :], True, False)
                mm(rank[:, 128:160], ones_b[:, :], chosen[:, 1, :], False, True)
                pe.wait_ge(*m("cnt_sb", 1))
                count, before = routing()["cnt_col"], tri_b[0:EXPERTS, 0:EXPERTS]
                mm(rank[:, 160:192], count, before, True, True)
                mm(rank[:, 64:96], count, before, True, False)
                mm(rank[:, 64:96], tri_b[:, :], chosen[:, 0, :], False, True)
                mm(rank[:, 96:128], count, before, True, False)
                mm(rank[:, 96:128], tri_b[:, :], chosen[:, 1, :], False, False)
                mm(rank[:, 96:128], ones_b[:, :], chosen[:, 0, :], False, True).then_inc(m["rank_ps"], 1)
                keep_clock(SORT_WAIT)
                pe.wait_ge(*m("hi_ready", 3))
                pe.wait_ge(*m("lo_ready", 3))
                for t in range(TT):
                    pe.wait_ge(*m("hot_ready", t + 1))
                    for k in range(KD):
                        if t == 0 and k == KD - 1:
                            pe.wait_ge(*m("offs_ready", 1))
                        for half, part in enumerate((xs_hi(t, k), xs_lo[:, t, k, :])):
                            last = mm(psum[:, SORT_BANKS[k], :], part, onehot_r[:, t, :],
                                      t == 0 and half == 0, t == TT - 1 and half == 1)
                        if t == TT - 1:
                            last.then_inc(m["sort_ps"], 1)
                def rows():
                    pe.wait_ge(*m("diag_ready", 8))
                    for t in range(TT):
                        last = mm(psum[:, t, :], ones, diag[:, t, :, :].rearrange("p q n -> p (q n)"), True, True)
                    last.then_inc(m["row_ps"], 1)

                def start_sums():
                    pe.wait_ge(*m("row_sb_a", TT))
                    pe.wait_ge(*m("row_sb_d", TT))
                    for b in range(4):
                        mm(psum[:, b, :], zeros_b[:, 0:P], zeros_b[:, :], True, False)

                def gate_or_up(u, s, buf):
                    for k in range(KD):
                        for j in range(2):
                            last = mm(psum[j * WIN:(j + 1) * WIN, 6, u * FF:(u + 1) * FF],
                                      xg[:, buf, k, j * WIN:(j + 1) * WIN], slot_gu(s, j)[:, u, k, :],
                                      k == 0, k == KD - 1)
                    return last

                def gate_and_up(s, buf):
                    for k in range(KD):
                        for j in range(2):
                            last = mm(psum[j * WIN:(j + 1) * WIN, 6, :], xg[:, buf, k, j * WIN:(j + 1) * WIN],
                                      slot_gu(s, j)[:, :, k, :], k == 0, k == KD - 1)
                    return last

                def transpose_h():
                    for k in range(FF // P):
                        last = pe.transpose(psum[:, 7, k * P:(k + 1) * P], h_sb[:, k * P:(k + 1) * P], ident)
                    return last

                def down(s, ready):
                    for c in range(2):
                        for k in range(FF // P):
                            for j in range(2):
                                last = mm(psum[j * WIN:(j + 1) * WIN, 4 + c, :], hT[:, k, j * WIN:(j + 1) * WIN],
                                          slot_dn(s, j)[:, k, c * 512:(c + 1) * 512], k == 0, k == FF // P - 1)
                        if ready[c] is not None:
                            last.then_inc(ready[c], 1)

                def combine(buf, t, halves=(0, 1)):
                    for c in halves:
                        last = mm(psum[:, 2 * t + c, :], comb[:, buf, t * P:(t + 1) * P],
                                  y_sb[:, c * 512:(c + 1) * 512], False, False)
                    return last

                def pair(i, s, first=False, waits_for_up=True):
                    prev = (s + SLOTS - 1) % SLOTS
                    if first:
                        pe.wait_ge(*m("xg0_ready", 2))
                    else:
                        pe.wait_ge(*m("xg_ready", i * 2))
                    pe.wait_ge(*rings[l][s]("gate", turn(i, s) * 32))
                    if not first:
                        pe.wait_ge(*m("h_ready", i))

                    def combine_previous(t):
                        if not first:
                            if t == 0:
                                pe.wait_ge(*m("y_act", i))
                                pe.wait_ge(*m("y_dve", i))
                                pe.wait_ge(*m("g_ready", i))
                            last = combine(prev, t)
                            if t:
                                last.then_inc(m["c_ps"], 1)

                    def transpose():
                        pe.wait_ge(*m("h_ready", i + 1))
                        if not first:
                            pe.wait_ge(*m("ht_sb", i))
                        transpose_h().then_inc(m["ht_ps"], 1)

                    if waits_for_up:
                        last = gate_or_up(0, s, s)
                        if first:
                            last.then_inc(m["gate0_ps"], 1)
                            rows()
                        combine_previous(0)
                        pe.wait_ge(*rings[l][s]("up", turn(i, s) * 32))
                        gate_or_up(1, s, s).then_inc(m["gu_ps"], 1)
                        if first:
                            start_sums()
                        combine_previous(1)
                        transpose()
                    else:
                        pe.wait_ge(*rings[l][s]("up", turn(i, s) * 32))
                        gate_and_up(s, s).then_inc(m["gu_ps"], 1)
                        combine_previous(0)
                        transpose()
                        combine_previous(1)
                    pe.wait_ge(*m("ht_sb", i + 1))
                    pe.wait_ge(*rings[l][s]("dn", turn(i, s) * 32))
                    down(s, (m["y0_ps"], m["y_ps"]))

                def turn(i, s):
                    return (i - s) // SLOTS + 1 if isinstance(i, int) else turns[s]

                more_windows = overflows(pe, l)
                pair(0, 0, True)
                turns = [None] * SLOTS
                for lo, hi in ((0, LOADED_TURNS), (LOADED_TURNS, (PAIRS - 1) // SLOTS)):
                    with pe.Fori(lo, hi) as it:
                        for j in range(SLOTS):
                            i, s = it * SLOTS + (1 + j), (1 + j) % SLOTS
                            turns[s] = it + (1 + (1 + j) // SLOTS)
                            pair(i, s, waits_for_up=lo > 0)
                s = (PAIRS - 1) % SLOTS
                pe.wait_ge(*m("g_ready", PAIRS))
                pe.wait_ge(*m("y_act", PAIRS))

                def close(t):
                    for c in range(2):
                        last = mm(psum[:, 2 * t + c, :], zeros_b[:, 0:P], zeros_b[:, :], False, True)
                    last.then_inc(m["sum_ps"], 1)

                with pe.If(more_windows):
                    o = ov[l]
                    pe.wait_ge(*m("y_dve", PAIRS))
                    combine(s, 0)
                    combine(s, 1).then_inc(m["c_ps"], 1)
                    pe.sem_inc(o["free"], 1)

                    def step(i, r, n):
                        pe.wait_ge(o["w"], n * 96 + 96)
                        pe.wait_ge(o["xg"], n * 2 + 2)
                        gate_or_up(0, 0, 0)
                        gate_or_up(1, 0, 0).then_inc(o["gu"], 1)
                        pe.wait_ge(o["h"], n + 1)
                        transpose_h().then_inc(o["ht_ps"], 1)
                        pe.wait_ge(o["ht_sb"], n + 1)
                        down(0, (None, o["y_ps"]))
                        pe.wait_ge(o["y_act"], n + 1)
                        pe.wait_ge(o["y_dve"], n + 1)
                        pe.wait_ge(o["g"], n + 1)
                        combine(0, 0)
                        combine(0, 1).then_inc(o["free"], 1)

                    overflow_steps(pe, step)
                    close(0)
                    close(1)
                with pe.Else():
                    combine(s, 0, (0,))
                    pe.wait_ge(*m("y_dve", PAIRS))
                    combine(s, 0, (1,))
                    close(0)
                    combine(s, 1).then_inc(m["c_ps"], 1)
                    close(1)

            diff_attention()
            moe(0)
            mla_attention()
            moe(1)

        @block.scalar
        def _(act):
            chain = Chain(act, act_chain)

            def act_xt(n):
                for b in (0, 2):
                    act.wait_ge(*xt[n]("ps", b + 1))
                    for k in (2 * b, 2 * b + 1):
                        act.activation(xT[:, k, :], psum[:, 4 + b, (k % 2) * SEQ:(k % 2 + 1) * SEQ], ACT.Identity,
                                       scale=gcol[:, n - 1, k:k + 1], bias=bcol[:, n - 1, k:k + 1])\
                           .then_inc(xt[n]["sb"], 1)

            def wo_upper(w, heads):
                for h in heads:
                    act.copy(wo_hi(w, h), wo(ring, w, h)).then_inc(w_hi_ready, 1)

            def root(n, t):
                act.wait_ge(*ln[n]("var", t + 1))
                act.activation(ln_sd[:, t:t + 1], ln_mv[:, t, 1:2], ACT.Sqrt, bias=eps[:, :]).then_inc(ln[n]["sd"], 1)

            def normalise(n, t, cols):
                act.wait_ge(*ln[n]("rstd", t + 1))
                act.activation(xs[:, t, cols], xs[:, t, cols], ACT.Identity, scale=ln_rstd[:, t:t + 1],
                               bias=ln_nb[:, t:t + 1]).then_inc(ln[n]["norm"], 1)

            def layer_norm(n):
                for t in range(TT):
                    root(n, t)
                    normalise(n, t, (slice(0, D), slice(0, D // 2))[t])

            def diff_attention():
                for b in range(4):
                    act.wait_ge(*xt[0]("ps", b + 1))
                    act.copy(xT_r[:, 2 * b:2 * b + 2, :], psum[:, 4 + b, :].rearrange("p (k t) -> p k t", k=2))\
                       .then_inc(x_hi_ready, 1)

                def move(g):
                    act.wait_ge(qkv_ps, g + 1)
                    src = psum[:, g if g < 8 else g - 4, :]
                    if g < 4:
                        for c in range(2):
                            rows = slice(c * DH, (c + 1) * DH)
                            act.mul(qz[rows, 2 * g:2 * g + 2, c, :], src[rows, :].rearrange("p (h t) -> p h t", h=2),
                                    DH ** -0.5).then_inc(qkv_act, 1)
                    elif g < 8:
                        act.copy(kT[:, 2 * (g - 4):2 * (g - 4) + 2, :], src.rearrange("p (h t) -> p h t", h=2))\
                           .then_inc(qkv_act, 1)
                    else:
                        c = (g - 8) // 2
                        act.copy(v[:, 0, c * 512:(c + 1) * 512], src).then_inc(qkv_act, 1)

                for c in range(6):
                    for m in range(4):
                        if m % 2 == 0 or c == 1:
                            act.wait_ge(ld_qkv0b if c == 0 and m else ld_qkv[c], 16)
                        if c >= 2:
                            act.wait_ge(qkv_ps, 2 * (c - 2) + m // 2 + 1)
                        cols = slice(m * P, (m + 1) * P)
                        act.copy(w_hi[:, c % 2, :, cols], qkv_chunk(ring, c)[:, :, cols]).then_inc(w_hi_ready, 1)
                    if c >= 1:
                        move(2 * (c - 1))
                    if c == 3:
                        act.wait_ge(lam_ready, 2)
                        act.activation(lam_dot, lam_dot, ACT.Exp).then_inc(lam_exp, 1)
                s = at[0]
                nmx = small[:, 0:8].rearrange("p (b q c) -> p b q c", b=2, q=2)
                sums = small[:, 8:16].rearrange("p (b q c) -> p b q c", b=2, q=2)
                nlr = small[:, 24:28].rearrange("p (b q) -> p b q", b=2)
                part = (slice(0, P), slice(P, 3 * P))

                def exps(h):
                    act.wait_ge(*s("mx_ready", 2 * (h + 1)))
                    for c in range(2):
                        for q in range(2):
                            e = lg[h % 4][:, c, part[q]]
                            act.activation(e, e, ACT.Exp, bias=nmx[:, h % 2, q, c:c + 1],
                                           accum_out=sums[:, h % 2, q, c:c + 1]).then_inc(s["e_ready"], 1)

                def scale_second(h):
                    act.wait_ge(*s("r_ready", h + 1))
                    for q in range(2):
                        e = lg[h % 4][:, 1, part[q]]
                        act.activation(e, e, ACT.Copy, scale=nlr[:, h % 2, q:q + 1]).then_inc(s["e1_scaled"], 1)

                def out(h):
                    act.wait_ge(*s("o_ps", h + 1))
                    act.copy(o_sb[:, h, :], psum[:, 6 + h % 2, 0:SEQ]).then_inc(s["o_sb"], 1)

                def transposed(h):
                    act.wait_ge(*s("pt_ps", h + 1))
                    if h >= 2:
                        act.wait_ge(*s("o_ps", h - 1))
                    act.copy(aT[h % 2], psum[:, 4 + h % 2, 0:3 * P]).then_inc(s["pt_sb"], 1)

                exps(0)
                exps(1)
                scale_second(0)
                move(10)
                for h in range(HEADS):
                    if h >= 1:
                        scale_second(h)
                    if h >= 1:
                        transposed(h - 1)
                    if h >= 2:
                        out(h - 2)
                    if h + 2 < HEADS:
                        exps(h + 2)
                transposed(HEADS - 1)
                out(HEADS - 2)
                out(HEADS - 1)
                ss, sd = small[:, 32:48], small[:, 48:64]
                act.wait_ge(ss_ready, 2)
                act.activation(sd, ss, ACT.Sqrt, scale=1.0 / P, bias=eps[:, :]).then_inc(sd_ready, 1)
                act.wait_ge(ld_wo, 16)
                wo_upper(wo_a, (4, 5, 6))
                for b in range(4):
                    act.wait_ge(ot_ps, b + 1)
                    act.activation(oT[:, 2 * b:2 * b + 2, :], psum[:, 4 + b, :].rearrange("p (h t) -> p h t", h=2),
                                   ACT.Copy, scale=subg[:, :]).then_inc(x_hi_ready, 1)
                wo_upper(wo_a, (7,))

            def mla_attention():
                act_xt(2)
                for n, (w, hi, lo) in enumerate(b_parts):
                    if n in (0, 3):
                        act.wait_ge((ld_qb, ld_kvb)[n // 3], 16)
                    act.copy(hi, w).then_inc(mq["w_hi"], 1)
                ss, sd = small[:, 0:4], small[:, 4:8]
                for i, (bank, n) in enumerate(((2, QR), (3, QR), (0, KVR), (1, KVR))):
                    act.wait_ge(mq["a_ps"], i + 1)
                    chain(act.activation(sq_junk[:, 0:n], psum[:, bank, 0:n], ACT.Square, accum_out=ss[:, i:i + 1]))
                    act.activation(sd[:, i:i + 1], ss[:, i:i + 1], ACT.Sqrt, scale=1.0 / n, bias=eps[:, :])\
                       .then_inc(mq["sd"], 1)
                for k in range(QR // P + KVR // P):
                    act.wait_ge(mq["ct_ps"], 1 + k // 3)
                    dst, bank, at_, g = ((cqT[:, k, :], 4 + k // 2, k % 2, qg[:, k:k + 1]) if k < 3 else
                                         (ckvT[:, k - 3, :], 6, k - 3, kvg[:, k - 3:k - 2]))
                    act.activation(dst, psum[:, bank, at_ * SEQ:(at_ + 1) * SEQ], ACT.Copy, scale=g)\
                       .then_inc(mq["c_hi"], 1)
                for t in range(TT):
                    act.wait_ge(mq["qr_ps"], t + 1)
                    act.mul(qr_raw[:, t, :, :], psum[:, 2 + t, :].rearrange("p (h d) -> p h d", h=HEADS), MLA_SCALE)\
                       .then_inc(mq["qr_raw"], 1)
                def move(g):
                    act.wait_ge(mq["b_ps"], g + 1)
                    src = psum[:, B_BANKS[g], :]
                    if g < 4:
                        act.mul(qnT[:, 2 * g:2 * g + 2, :], src.rearrange("p (h t) -> p h t", h=2), MLA_SCALE)\
                           .then_inc(mq["b_act"], 1)
                    elif g < 8:
                        act.copy(knT[:, 2 * (g - 4):2 * (g - 4) + 2, :], src.rearrange("p (h t) -> p h t", h=2))\
                           .then_inc(mq["b_act"], 1)
                    else:
                        act.wait_ge(mq["krt_ps"], 1)
                        act.copy(v[:, (g - 8) // 2, 0:512], src).then_inc(mq["b_act"], 1)

                for g in (0, 2, 4, 6):
                    move(g)
                for b in range(2):
                    act.wait_ge(mq["qt_ps"], b + 1)
                    src = psum[0:ROPE, (7, 4)[b], :].rearrange("p (h t) -> p h t", h=2)
                    act.copy(qrz[0:ROPE, 4 * b:4 * b + 4:2, :], src).then_inc(mq["qt_sb"], 1)
                move(8)
                s = at[1]
                nmx = small[:, 16:20].rearrange("p (b q) -> p b q", b=2)
                sums = small[:, 20:24].rearrange("p (b q) -> p b q", b=2)

                def exps(h):
                    act.wait_ge(*s("mx_ready", 2 * (h + 1)))
                    for q, part in enumerate((slice(0, P), slice(P, 3 * P))):
                        e = mlg[h % 3][:, part]
                        act.activation(e, e, ACT.Exp, bias=nmx[:, h % 2, q:q + 1],
                                       accum_out=sums[:, h % 2, q:q + 1]).then_inc(s["e_ready"], 1)

                def out(h):
                    act.wait_ge(*s("o_ps", h + 1))
                    act.copy(oT[:, h, :], psum[:, 4 + h % 2, 0:SEQ]).then_inc(s["o_sb"], 1)

                def transposed(h):
                    act.wait_ge(*s("pt_ps", h + 1))
                    if h >= 2:
                        act.wait_ge(*s("o_ps", h - 1))
                    act.copy(pT[h % 2], psum[:, 2 + h % 2, 0:3 * P]).then_inc(s["pt_sb"], 1)

                exps(0)
                exps(1)
                move(10)
                for h in range(HEADS):
                    if h >= 1:
                        transposed(h - 1)
                    if h >= 2:
                        out(h - 2)
                    if h + 2 < HEADS:
                        exps(h + 2)
                transposed(HEADS - 1)
                out(HEADS - 2)
                out(HEADS - 1)
                act.wait_ge(ld_wo, 32)
                wo_upper(wo_b, range(4, HEADS))

            def moe(l):
                m = mo[l]
                act_xt(2 * l + 1)
                act.activation(small[:, 60:61], eps[:, :], ACT.Sigmoid)
                act.wait_ge(*m("lgt_ps", 1))
                act.copy(logit_T, psum[:, 0, 0:SEQ]).then_inc(m["lgt_sb"], 1)
                act.wait_ge(*m("lg_ps", 1))
                act.activation(routing()["score"], psum[:, 1, 0:64], ACT.Sigmoid).then_inc(m["score"], 1)
                for part, (t, k0, k1) in zip(hi_parts, hi_of):
                    act.wait_ge(*ln[2 * l](("x_dve", "x_pool")[t], 1))
                    act.copy(part, xs_tiles(t, k0, k1)).then_inc(m["hi_ready"], 1)
                for k in range(0, KD, 2):
                    act.wait_ge(*m("sort_ps", k + 1))
                    act.copy(xsT[:, k, 0:NSLOT], psum[:, SORT_BANKS[k], :]).then_inc(m["sort_act"], 1)
                act.wait_ge(*m("row_ps", 1))
                for t in range(TT):
                    act.copy(gate_row[:, :, t * P:(t + 1) * P],
                             psum[:, t, 2 * P:4 * P].rearrange("p (j n) -> p j n", j=2)).then_inc(m["row_sb_a"], 1)

                def pair(i, s, first=False):
                    act.wait_ge(*m("gu_ps", i + 1))
                    if not first:
                        act.wait_ge(*m("h_ready", i))
                    act.activation(act_s, psum[:, 6, 0:FF], ACT.Silu).then_inc(m["s_ready"], 1)
                    act.wait_ge(*m("ht_ps", i + 1))
                    if not first:
                        act.wait_ge(*m("y_ps", i))
                    act.copy(hT, psum[:, 7, 0:FF].rearrange("p (k c) -> p k c", k=2)).then_inc(m["ht_sb"], 1)
                    act.wait_ge(*m("y0_ps", i + 1))
                    if not first:
                        act.wait_ge(*m("c_ps", i))
                    act.copy(y_sb[:, 0:512], psum[:, 4, :]).then_inc(m["y_act"], 1)

                pair(0, 0, True)
                for_pairs_1_up(act, pair)
                with act.If(overflows(act, l)):
                    o = ov[l]

                    def step(i, r, n):
                        act.wait_ge(o["gu"], n + 1)
                        act.activation(act_s, psum[:, 6, 0:FF], ACT.Silu).then_inc(o["s"], 1)
                        act.wait_ge(o["ht_ps"], n + 1)
                        act.copy(hT, psum[:, 7, 0:FF].rearrange("p (k c) -> p k c", k=2)).then_inc(o["ht_sb"], 1)
                        act.wait_ge(o["y_ps"], n + 1)
                        act.copy(y_sb[:, 0:512], psum[:, 4, :]).then_inc(o["y_act"], 1)

                    overflow_steps(act, step)

            act.wait_ge(lam_ready, 1)
            act.copy(ln_sd[:, 0:1], eps[:, :])
            act.dma_start(tri_f, consts[:, CONSTS:CONSTS + P]).then_inc(ld_misc, 16)
            act.dma_start(lam_in, diff_lambda[0].partition_broadcast(P)).then_inc(ld_lam, 16)
            act.dma_start(rb[:, :], router_b.partition_broadcast(P)).then_inc(ld_misc, 16)
            with nc.allow_non_contiguous_dma(reason="norm scales as columns, once"):
                act.dma_start(subg[:, :], diff_subln_g[0].rearrange("(p a) -> p a", a=1)).then_inc(ld_misc, 16)
                act.dma_start(qg[:, :], mla_q_norm_g[0].rearrange("(k p) -> p k", p=P)).then_inc(ld_misc, 16)
                act.dma_start(kvg[:, :], mla_kv_norm_g.rearrange("(k p) -> p k", p=P)).then_inc(ld_misc, 16)
                for col, w in ((gcol, ln_g), (bcol, ln_b)):
                    act.dma_start(col[:, :, :], w.rearrange("l j (p k) -> p (l j) k", k=KD)[:, 0:3, :])\
                       .then_inc(ld_misc, 16)
            diff_attention()
            layer_norm(0)
            act.wait_ge(ld_misc, 16 * MISC)
            moe(0)
            layer_norm(1)
            mla_attention()
            layer_norm(2)
            moe(1)
            root(3, 0)
            normalise(3, 0, slice(0, D))
            root(3, 1)

        @block.vector
        def _(dve):
            chain = Chain(dve, dve_chain)

            def dve_xt(n):
                for b in (1, 3):
                    dve.wait_ge(*xt[n]("ps", b + 1))
                    for k in (2 * b, 2 * b + 1):
                        dve.tensor_scalar(xT[:, k, :], psum[:, 4 + b, (k % 2) * SEQ:(k % 2 + 1) * SEQ],
                                          gcol[:, n - 1, k:k + 1], bcol[:, n - 1, k:k + 1], ALU.mult, ALU.add)\
                           .then_inc(xt[n]["sb"], 1)

            def wo_lower(l, w):
                for h in range(4, HEADS):
                    dve.wait_ge(w_hi_ready, 24 + 4 * l + h - 3)
                    dve.tensor_tensor(wo(ring_r, w, h), wo(ring, w, h), wo_hi(w, h), ALU.subtract)\
                       .then_inc(w_lo_ready, 1)

            def add(n, t, c, ready):
                ready(t, c)
                cols = slice(c * 512, (c + 1) * 512)
                chain(dve.scalar_tensor_tensor(out=xs[:, t, cols], in0=xs[:, t, cols], scalar=ALPHA,
                                               in1=psum[:, 2 * t + c, :], op0=ALU.mult, op1=ALU.add))
                chain(dve.bn_stats(ln_stats[:, t, c, :], xs[:, t, cols]))

            def statistics(n, t):
                dve.bn_aggr(ln_mv[:, t, :], ln_stats[:, t, :, :].rearrange("p c s -> p (c s)"))\
                   .then_inc(ln[n]["var"], 1)

            def scales(n, t):
                dve.wait_ge(*ln[n]("sd", t + 1))
                chain(dve.reciprocal(ln_rstd[:, t:t + 1], ln_sd[:, t:t + 1]))
                dve.tensor_scalar(ln_nb[:, t:t + 1], ln_mv[:, t, 0:1], ln_rstd[:, t:t + 1], -1.0, ALU.mult,
                                  ALU.mult).then_inc(ln[n]["rstd"], 1)

            def layer_norm(n, ready):
                add(n, 0, 0, ready)
                add(n, 0, 1, ready)
                statistics(n, 0)
                add(n, 1, 0, ready)
                scales(n, 0)
                add(n, 1, 1, ready)
                statistics(n, 1)
                scales(n, 1)
                dve.wait_ge(*ln[n]("rstd", 2))
                dve.tensor_scalar(xs[:, 1, D // 2:], xs[:, 1, D // 2:], ln_rstd[:, 1:2], ln_nb[:, 1:2], ALU.mult,
                                  ALU.add).then_inc(ln[n]["norm"], 1)

            def last_layer_norm(ready):
                add(3, 0, 0, ready)
                add(3, 0, 1, ready)
                statistics(3, 0)
                add(3, 1, 0, ready)
                scales(3, 0)
                add(3, 1, 1, ready)
                statistics(3, 1)
                dve.wait_ge(*ln[3]("var", 2))
                dve.wait_ge(*ld_gb[3]("gb", 32))
                chain(dve.scalar_tensor_tensor(out=xs[:, 1, :], in0=xs[:, 1, :], scalar=ln_mv[:, 1, 0:1],
                                               in1=gb[3][:, 0, :], op0=ALU.subtract, op1=ALU.mult))
                scales(3, 1)
                dve.wait_ge(*ln[3]("norm", 1))
                cols = slice(LAST_SPLIT, D)
                chain(dve.tensor_tensor(xs[:, 0, cols], xs[:, 0, cols], gb[3][:, 0, cols], ALU.mult))
                dve.tensor_tensor(xs[:, 0, cols], xs[:, 0, cols], gb[3][:, 1, cols], ALU.add).then_inc(ln[3]["x_dve"], 1)
                dve.wait_ge(*ln[3]("rstd", 2))
                dve.scalar_tensor_tensor(out=xs[:, 1, :], in0=xs[:, 1, :], scalar=ln_rstd[:, 1:2],
                                         in1=gb[3][:, 1, :], op0=ALU.mult, op1=ALU.add).then_inc(ln[3]["x_dve"], 1)

            def scale_shift(n):
                dve.wait_ge(*ln[n]("norm", 3))
                dve.wait_ge(*ld_gb[n]("gb", 32))
                chain(dve.tensor_tensor(xs[:, 0, :], xs[:, 0, :], gb[n][:, 0, :], ALU.mult))
                dve.tensor_tensor(xs[:, 0, :], xs[:, 0, :], gb[n][:, 1, :], ALU.add).then_inc(ln[n]["x_dve"], 1)

            def prepare():
                dve.memset(zeros_b[:, :], 0.0).then_inc(cast_ready, 1)
                dve.memset(eps[:, :], EPS).then_inc(lam_ready, 1)
            def constants():
                dve.wait_ge(ld_cst, 16)
                dve.tensor_copy(ones_b[:, :], ones).then_inc(cast_ready, 1)
                dve.wait_ge(ld_misc, 16 * MISC)
                dve.tensor_copy(tri_b[:, :], tri_f).then_inc(cast_ready, 1)
                dve.wait_ge(ld_lam, 16)
                chain(dve.tensor_tensor(lam_prod, lam_in[:, 0::2, :], lam_in[:, 1::2, :], ALU.mult))
                dve.tensor_reduce(lam_dot, lam_prod, AX.X, ALU.add).then_inc(lam_ready, 1)

            def diff_attention():
                for b in range(4):
                    dve.wait_ge(x_hi_ready, b + 1)
                    dve.tensor_tensor(x_lo[:, 2 * b:2 * b + 2, :], psum[:, 4 + b, :].rearrange("p (k t) -> p k t", k=2),
                                      xT_r[:, 2 * b:2 * b + 2, :], ALU.subtract).then_inc(xt[0]["sb"], 2)

                def move(g):
                    dve.wait_ge(qkv_ps, g + 1)
                    src = psum[:, g if g < 8 else g - 4, :]
                    if g < 4:
                        for c in range(2):
                            rows = slice(c * DH, (c + 1) * DH)
                            dve.tensor_scalar(qz[rows, 2 * g:2 * g + 2, c, :],
                                              src[rows, :].rearrange("p (h t) -> p h t", h=2), DH ** -0.5, None,
                                              ALU.mult).then_inc(qkv_dve, 1)
                    elif g < 8:
                        dve.tensor_copy(kT[:, 2 * (g - 4):2 * (g - 4) + 2, :],
                                        src.rearrange("p (h t) -> p h t", h=2)).then_inc(qkv_dve, 1)
                    else:
                        dve.wait_ge(cast_ready, 3)
                        c = (g - 8) // 2
                        dve.tensor_copy(v[:, 1, c * 512:(c + 1) * 512], src).then_inc(qkv_dve, 1)

                for c in range(6):
                    for m in range(4):
                        dve.wait_ge(w_hi_ready, 4 * c + m + 1)
                        cols = slice(m * P, (m + 1) * P)
                        dve.tensor_tensor(qkv_chunk(ring_r, c)[:, :, cols], qkv_chunk(ring, c)[:, :, cols],
                                          w_hi[:, c % 2, :, cols], ALU.subtract).then_inc(w_lo_ready, 1)
                    if c >= 1:
                        move(2 * (c - 1) + 1)
                    if c == 2:
                        constants()
                dve.wait_ge(lam_exp, 1)
                chain(dve.tensor_tensor(nlam[:, :], lam_dot[:, 1:2], lam_dot[:, 0:1], ALU.subtract))
                chain(dve.tensor_scalar(nlam[:, :], nlam[:, :], LAMBDA_INIT, None, ALU.subtract))
                chain(dve.tensor_scalar(subg[:, :], subg[:, :], 1.0 - LAMBDA_INIT, None, ALU.mult))
                s = at[0]
                nmx = small[:, 0:8].rearrange("p (b q c) -> p b q c", b=2, q=2)
                sums = small[:, 8:16].rearrange("p (b q c) -> p b q c", b=2, q=2)
                rec = small[:, 16:24].rearrange("p (b q c) -> p b q c", b=2, q=2)
                nlr = small[:, 24:28].rearrange("p (b q) -> p b q", b=2)

                def logits(h):
                    if h >= 4:
                        dve.wait_ge(*s("pt_ps", h - 3))
                    b = lg[h % 4]
                    for c in range(2):
                        dve.wait_ge(*s("sc_ps", 2 * h + c + 1))
                        dve.scalar_tensor_tensor(out=b[:, c, :], in0=dist, scalar=-(2.0 ** -(h + 1)),
                                                 in1=psum[:, 2 * (h % 2) + c, 0:3 * P], op0=ALU.mult, op1=ALU.add)\
                           .then_inc(s["sc_read"], 1)
                    dve.wait_ge(*s("sc_read", 2 * (h + 1)))
                    dve.tensor_reduce(nmx[:, h % 2, 0, :], b[:, :, 0:P], AX.X, ALU.max, negate=True)\
                       .then_inc(s["mx_ready"], 1)
                    dve.tensor_reduce(nmx[:, h % 2, 1, :], b[:, :, P:3 * P], AX.X, ALU.max, negate=True)\
                       .then_inc(s["mx_ready"], 1)

                def reciprocals(h):
                    dve.wait_ge(*s("e_ready", 4 * (h + 1)))
                    chain(dve.reciprocal(rec[:, h % 2, :, :], sums[:, h % 2, :, :]))
                    dve.tensor_scalar(nlr[:, h % 2, :], rec[:, h % 2, :, 1], nlam[:, :], None, ALU.mult)\
                       .then_inc(s["r_ready"], 1)

                def probabilities(h):
                    dve.wait_ge(*s("e1_scaled", 2 * (h + 1)))
                    e = lg[h % 4]
                    for q, part in enumerate((slice(0, P), slice(P, 3 * P))):
                        dve.scalar_tensor_tensor(out=e[:, 0, part], in0=e[:, 0, part], scalar=rec[:, h % 2, q, 0:1],
                                                 in1=e[:, 1, part], op0=ALU.mult, op1=ALU.add)\
                           .then_inc(s["p_ready"], 1)

                logits(0)
                logits(1)
                reciprocals(0)
                probabilities(0)
                move(11)
                for h in range(HEADS):
                    if h >= 1:
                        reciprocals(h)
                    if h + 2 < HEADS:
                        logits(h + 2)
                    if h >= 1:
                        probabilities(h)
                ss, sd = small[:, 32:48], small[:, 48:64]
                for heads, n in (((0, 6), 6), ((6, 8), 8)):
                    dve.wait_ge(sq_ready, n)
                    dve.tensor_reduce(ss[:, 2 * heads[0]:2 * heads[1]],
                                      o_sq[:, heads[0]:heads[1], :].rearrange("p h (q d) -> p h q d", q=2), AX.X, ALU.add)\
                       .then_inc(ss_ready, 1)
                dve.wait_ge(sd_ready, 1)
                rs = small[:, 32:48].rearrange("p (h q) -> p h q", h=HEADS)
                dve.reciprocal(small[:, 32:48], sd).then_inc(rs_ready, 1)
                dve.wait_ge(rs_ready, 1)
                for lo, hi in ((0, 2), (2, 5)):
                    o4 = o_sb[:, lo:hi, :].rearrange("p h (q d) -> p h q d", q=2)
                    dve.tensor_tensor(o4, o4, rs[:, lo:hi, :].unsqueeze(3).broadcast_to([P, hi - lo, 2, P]), ALU.mult)\
                       .then_inc(on_dve, 1)
                for b in range(4):
                    dve.wait_ge(x_hi_ready, 4 + b + 1)
                    dve.scalar_tensor_tensor(out=o_lo_a[:, 2 * b:2 * b + 2, :], in0=psum[:, 4 + b, :]
                                             .rearrange("p (h t) -> p h t", h=2), scalar=subg[:, :],
                                             in1=oT[:, 2 * b:2 * b + 2, :], op0=ALU.mult, op1=ALU.subtract)\
                       .then_inc(ot_sb, 1)
                wo_lower(0, wo_a)

            def mla_attention():
                dve_xt(2)
                dve.wait_ge(*xt[2]("ps", 4))
                scale_shift(1)
                sd, rstd = small[:, 4:8], small[:, 8:12]
                for i, (bank, n) in enumerate(((2, QR), (3, QR), (0, KVR), (1, KVR))):
                    dve.wait_ge(mq["sd"], i + 1)
                    chain(dve.reciprocal(rstd[:, i:i + 1], sd[:, i:i + 1]))
                    dst = c_q[:, i, :] if i < 2 else c_kv[:, i - 2, :]
                    dve.tensor_scalar(dst, psum[:, bank, 0:n], rstd[:, i:i + 1], None, ALU.mult)\
                       .then_inc(mq["c_ready"], 1)
                    if i >= 2:
                        chain(dve.tensor_copy(kr_raw[:, i - 2, :], psum[:, bank, KVR:KVR + ROPE]))
                for k in range(QR // P + KVR // P):
                    dve.wait_ge(mq["c_hi"], (2, 2, 3, 5, 5)[k])
                    hi, lo, bank, at_, g = ((cqT[:, k, :], cq_lo[:, k, :], 4 + k // 2, k % 2, qg[:, k:k + 1]) if k < 3 else
                                            (ckvT[:, k - 3, :], ckv_lo[:, k - 3, :], 6, k - 3, kvg[:, k - 3:k - 2]))
                    dve.scalar_tensor_tensor(out=lo, in0=psum[:, bank, at_ * SEQ:(at_ + 1) * SEQ], scalar=g, in1=hi,
                                             op0=ALU.mult, op1=ALU.subtract).then_inc(mq["ct_sb"], 1)
                for t in range(TT):
                    dst = kr2[:, t, 0:ROPE].unsqueeze(1)
                    chain(rotate(dve, chain, dst, kr_raw[:, t, :].unsqueeze(1), t, rope_tmp[:, 0:1, :], 1))
                dve.tensor_copy(kr2[:, :, ROPE:2 * ROPE], kr2[:, :, 0:ROPE]).then_inc(mq["kr_rot"], 1)
                def move(g):
                    dve.wait_ge(mq["b_ps"], g + 1)
                    src = psum[:, B_BANKS[g], :]
                    if g < 4:
                        dve.tensor_scalar(qnT[:, 2 * g:2 * g + 2, :], src.rearrange("p (h t) -> p h t", h=2), MLA_SCALE,
                                          None, ALU.mult).then_inc(mq["b_dve"], 1)
                    elif g < 8:
                        dve.tensor_copy(knT[:, 2 * (g - 4):2 * (g - 4) + 2, :],
                                        src.rearrange("p (h t) -> p h t", h=2)).then_inc(mq["b_dve"], 1)
                    else:
                        dve.wait_ge(mq["krt_ps"], 1)
                        dve.wait_ge(mq["qr_rot_pool"], 1)
                        dve.tensor_copy(v[:, (g - 8) // 2, 512:1024], src).then_inc(mq["b_dve"], 1)

                move(1)
                dve.wait_ge(mq["qr_raw"], 1)
                rotate(dve, chain, qr_rot[:, 0, :, :], qr_raw[:, 0, :, :], 0, rope_tmp, HEADS)\
                    .then_inc(mq["qr_rot_dve"], 1)
                for g in (3, 5, 7):
                    move(g)
                dve.wait_ge(mq["krt_ps"], 1)
                dve.tensor_copy(krT2, psum[:, 6, 0:SEQ]).then_inc(mq["krt_sb"], 1)
                for b in range(2):
                    dve.wait_ge(mq["qt_ps"], b + 1)
                    src = psum[ROPE:P, (7, 4)[b], :].rearrange("p (h t) -> p h t", h=2)
                    dve.tensor_copy(qrz[ROPE:P, 4 * b + 1:4 * b + 4:2, :], src).then_inc(mq["qt_sb"], 1)
                move(9)
                s = at[1]
                nmx = small[:, 16:20].rearrange("p (b q) -> p b q", b=2)
                sums = small[:, 20:24].rearrange("p (b q) -> p b q", b=2)
                rec = small[:, 24:28].rearrange("p (b q) -> p b q", b=2)

                def logits(h):
                    if h >= 3:
                        dve.wait_ge(*s("pt_ps", h - 2))
                    dve.wait_ge(*s("sc_ps", h + 1))
                    dve.tensor_tensor(mlg[h % 3], psum[:, h % 2, 0:3 * P], mask, ALU.add).then_inc(s["sc_read"], 1)
                    dve.wait_ge(*s("sc_read", h + 1))
                    for q, part in enumerate((slice(0, P), slice(P, 3 * P))):
                        dve.tensor_reduce(nmx[:, h % 2, q:q + 1], mlg[h % 3][:, part], AX.X, ALU.max, negate=True)\
                           .then_inc(s["mx_ready"], 1)

                def reciprocals(h):
                    dve.wait_ge(*s("e_ready", 2 * (h + 1)))
                    dve.reciprocal(rec[:, h % 2, :], sums[:, h % 2, :]).then_inc(s["r_ready"], 1)

                def probabilities(h):
                    dve.wait_ge(*s("r_ready", h + 1))
                    for q, part in enumerate((slice(0, P), slice(P, 3 * P))):
                        dve.tensor_scalar(mlg[h % 3][:, part], mlg[h % 3][:, part], rec[:, h % 2, q:q + 1], None,
                                          ALU.mult).then_inc(s["p_ready"], 1)

                def o_lower(h):
                    dve.wait_ge(*s("o_sb", h + 1))
                    dve.tensor_tensor(o_lo_b[:, h, :], psum[:, 4 + h % 2, 0:SEQ], oT[:, h, :], ALU.subtract)\
                       .then_inc(o_lo_ready, 1)

                logits(0)
                logits(1)
                reciprocals(0)
                probabilities(0)
                move(11)
                for h in range(HEADS):
                    if h >= 1:
                        reciprocals(h)
                    if h >= 3:
                        o_lower(h - 3)
                    if h + 2 < HEADS:
                        logits(h + 2)
                    if h >= 1:
                        probabilities(h)
                o_lower(HEADS - 3)
                o_lower(HEADS - 2)
                o_lower(HEADS - 1)
                wo_lower(1, wo_b)

            def moe(l):
                m = mo[l]
                dve_xt(2 * l + 1)
                dve.wait_ge(*xt[2 * l + 1]("ps", 4))
                scale_shift(2 * l)
                c = routing()
                both = TT * EXPERTS

                def tt(dst, a, b, op):
                    chain(dve.tensor_tensor(dst, a, b, op))

                def te(a):
                    return a.rearrange("p (t e) -> p t e", t=TT)

                def spread(a, n):
                    return a.unsqueeze(2).broadcast_to([P, TT, n])

                def per_tile(a, n):
                    return a.unsqueeze(1).broadcast_to([P, TT, n])

                dve.wait_ge(*m("score", 1))
                tt(te(c["sel"]), te(c["score"]), per_tile(rb[:, :], EXPERTS), ALU.add)
                quad = c["sel"].rearrange("p (g e) -> p g e", e=PER_GROUP)
                mx2, sm2 = (c[n].rearrange("p (g e) -> p g e", e=2) for n in ("mx2", "sm2"))
                tt(mx2, quad[:, :, 0::2], quad[:, :, 1::2], ALU.max)
                tt(sm2, quad[:, :, 0::2], quad[:, :, 1::2], ALU.add)
                tt(c["t1"], mx2[:, :, 0], mx2[:, :, 1], ALU.add)
                tt(c["t2"], sm2[:, :, 0], sm2[:, :, 1], ALU.max)
                tt(c["gs"], c["t1"], c["t2"], ALU.max)
                chain(dve.tensor_reduce(c["gmax"], te(c["gs"]), AX.X, ALU.max))
                tt(te(c["gkey"]), te(c["gs"]), spread(c["gmax"], GROUPS), ALU.is_equal)
                tt(te(c["gkey"]), te(c["gkey"]), per_tile(w8, GROUPS), ALU.mult)
                chain(dve.tensor_reduce(c["gmax"], te(c["gkey"]), AX.X, ALU.max))
                tt(te(c["gmask"]), te(c["gkey"]), spread(c["gmax"], GROUPS), ALU.is_equal)
                masked = c["masked"].rearrange("p (g e) -> p g e", e=PER_GROUP)
                wide = [P, TT * GROUPS, PER_GROUP]
                chain(dve.tensor_scalar(c["gmask"], c["gmask"], 1.0, BIG, ALU.subtract, ALU.mult))
                tt(masked, quad, c["gmask"].unsqueeze(2).broadcast_to(wide), ALU.add)
                oh = c["oh"].rearrange("p (j t e) -> p j t e", j=2, t=TT)
                for j in range(2):
                    chain(dve.tensor_reduce(c["m1"], te(c["masked"]), AX.X, ALU.max))
                    tt(te(c["e1"]), te(c["masked"]), spread(c["m1"], EXPERTS), ALU.is_equal)
                    tt(te(c["e1"]), te(c["e1"]), per_tile(w32, EXPERTS), ALU.mult)
                    chain(dve.tensor_reduce(c["k1"], te(c["e1"]), AX.X, ALU.max))
                    tt(oh[:, j], te(c["e1"]), spread(c["k1"], EXPERTS), ALU.is_equal)
                    if j == 0:
                        chain(dve.scalar_tensor_tensor(out=c["masked"], in0=c["oh"][:, 0:both], scalar=-3 * BIG,
                                                       in1=c["masked"], op0=ALU.mult, op1=ALU.add))
                dve.tensor_tensor(c["chosen"], oh[:, 0], oh[:, 1], ALU.add).then_inc(m["m_ready"], 1)
                kg = small[:, 0:8].rearrange("p (q t) -> p q t", q=4)
                slot = small[:, 8:12].rearrange("p (j t) -> p j t", j=2)
                total = small[:, 12:14]
                prod = c["prod"].rearrange("p (j n) -> p j n", j=2)
                oh2 = c["oh"].rearrange("p (j n) -> p j n", j=2)

                def pick(dst, src):
                    tt(prod, oh2, src.unsqueeze(1).broadcast_to([P, 2, both]), ALU.mult)
                    chain(dve.tensor_reduce(dst, c["prod"].rearrange("p (j t e) -> p j t e", j=2, t=TT), AX.X, ALU.add))

                pick(kg[:, 2:4, :], c["score"])
                dve.wait_ge(*m("cnt_ps", 1))
                dve.tensor_copy(c["cnt_col"], psum[0:EXPERTS, 3, 0:P]).then_inc(m["cnt_sb"], 1)
                tt(total, kg[:, 2, :], kg[:, 3, :], ALU.add)
                chain(dve.reciprocal(total, total))
                tt(kg[:, 2:4, :], kg[:, 2:4, :], total.unsqueeze(1).broadcast_to([P, 2, TT]), ALU.mult)
                dve.wait_ge(*m("rank_ps", 1))
                pick(slot, psum[:, 2, both:2 * both])
                dve.wait_ge(*m("iota_ready", 1))
                for t in range(TT):
                    chain(dve.tensor_scalar(onehot_r[:, t, :], iota, slot[:, 0, t:t + 1], None, ALU.is_equal))
                    dve.scalar_tensor_tensor(out=onehot_r[:, t, :], in0=iota, scalar=slot[:, 1, t:t + 1],
                                             in1=onehot_r[:, t, :], op0=ALU.is_equal, op1=ALU.add)\
                       .then_inc(m["hot_ready"], 1)
                tt(te(c["rank"]), te(psum[:, 2, 0:both]), per_tile(ekey, EXPERTS), ALU.add)
                tt(prod, oh2, c["rank"].unsqueeze(1).broadcast_to([P, 2, both]), ALU.mult)
                dve.tensor_reduce(kg[:, 0:2, :], c["prod"].rearrange("p (j t e) -> p j t e", j=2, t=TT), AX.X, ALU.add)\
                   .then_inc(m["key_ready"], 1)
                for r in range(ROUNDS):
                    chain(dve.tensor_scalar(offs[:, r * EXPERTS:(r + 1) * EXPERTS], psum[:, 2, 160:192], float(WIN * r),
                                            float(NSLOT), ALU.add, ALU.min))
                chain(dve.tensor_reduce(c["cnt"][:, 0:1], psum[:, 2, 128:160], AX.X, ALU.max))
                dve.tensor_copy(offs[:, ROUNDS * EXPERTS:ROUNDS * EXPERTS + 1], c["cnt"][:, 0:1])\
                   .then_inc(m["offs_ready"], 1)
                dve.wait_ge(*m("offs_ready", 1))
                first_starts = [dve.value_load(offs[0:1, j:j + 1], min_val=0, max_val=NSLOT) for j in range(2)]
                for k in range(1, KD, 2):
                    dve.wait_ge(*m("sort_ps", k + 1))
                    dve.tensor_copy(xsT[:, k, 0:NSLOT], psum[:, SORT_BANKS[k], :]).then_inc(m["sort_dve"], 1)
                dve.wait_ge(*m("sort_act", 4))
                dve.wait_ge(*m("sort_dve", 4))
                dve.wait_ge(*m("pad_zero", 1))
                for j, a in enumerate(first_starts):
                    dve.tensor_copy(xg[:, 0, :, j * WIN:(j + 1) * WIN], xsT[:, :, bass.ds(a, WIN)])\
                       .then_inc(m["xg0_ready"], 1)
                dve.wait_ge(*m("row_ps", 1))
                dve.wait_ge(*m("row_sb_a", TT))
                for t in range(TT):
                    dve.tensor_scalar(key_row[:, :, t * P:(t + 1) * P],
                                      psum[:, t, 0:2 * P].rearrange("p (j n) -> p j n", j=2), rowc, None,
                                      ALU.subtract).then_inc(m["row_sb_d"], 1)
                dve.wait_ge(*m("row_sb_d", TT))

                def weights(i, r, buf, part, ready, n):
                    at_ = ecol[:, bass.ds(i + r * PAIRS, 1)]
                    dve.scalar_tensor_tensor(out=comb[:, buf, :], in0=key_row[:, 0, :], scalar=at_,
                                             in1=gate_row[:, 0, :], op0=ALU.is_equal, op1=ALU.mult).then_inc(part, 1)
                    dve.scalar_tensor_tensor(out=g_tmp, in0=key_row[:, 1, :], scalar=at_,
                                             in1=gate_row[:, 1, :], op0=ALU.is_equal, op1=ALU.mult).then_inc(part, 1)
                    dve.wait_ge(part, n * 2 + 2)
                    dve.tensor_tensor(comb[:, buf, :], comb[:, buf, :], g_tmp, ALU.add).then_inc(ready, 1)

                def pair(i, s, first=False):
                    dve.wait_ge(*m("s_ready", i + 1))
                    if not first:
                        dve.wait_ge(*m("ht_ps", i))
                    dve.tensor_tensor(h_sb, psum[:, 6, FF:2 * FF], act_s, ALU.mult).then_inc(m["h_ready"], 1)
                    if not first:
                        dve.wait_ge(*m("g_ready", i))
                    weights(i, 0, s, m["g_part"], m["g_ready"], i + l * PAIRS)
                    dve.wait_ge(*m("y_ps", i + 1))
                    if not first:
                        dve.wait_ge(*m("c_ps", i))
                    dve.tensor_copy(y_sb[:, 512:1024], psum[:, 5, :]).then_inc(m["y_dve"], 1)

                pair(0, 0, True)
                for_pairs_1_up(dve, pair)
                with dve.If(overflows(dve, l)):
                    o = ov[l]
                    dve.wait_ge(*m("c_ps", PAIRS))

                    def step(i, r, n):
                        dve.wait_ge(o["free"], n + 1)
                        dve.wait_ge(o["s"], n + 1)
                        dve.tensor_tensor(h_sb, psum[:, 6, FF:2 * FF], act_s, ALU.mult).then_inc(o["h"], 1)
                        weights(i, r, 0, o["g_part"], o["g"], n)
                        dve.wait_ge(o["y_ps"], n + 1)
                        dve.tensor_copy(y_sb[:, 512:1024], psum[:, 5, :]).then_inc(o["y_dve"], 1)

                    overflow_steps(dve, step)

            prepare()
            diff_attention()
            layer_norm(0, lambda t, c: dve.wait_ge(wo_ps, 2 * t + c + 1))
            moe(0)
            layer_norm(1, lambda t, c: dve.wait_ge(*mo[0]("sum_ps", t + 1)))
            mla_attention()
            layer_norm(2, lambda t, c: dve.wait_ge(wo_ps, 4 + 2 * t + c + 1))
            moe(1)
            last_layer_norm(lambda t, c: dve.wait_ge(*mo[1]("sum_ps", t + 1)))

        @block.gpsimd
        def _(pool):
            chain = Chain(pool, pool_chain)

            def layer_norm(n):
                pool.wait_ge(*ln[n]("norm", 3))
                pool.wait_ge(*xt[n + 1]("ps", 4))
                pool.wait_ge(*ld_gb[n]("gb", 32))
                chain(pool.tensor_tensor(xs[:, 1, :], xs[:, 1, :], gb[n][:, 0, :], ALU.mult))
                pool.tensor_tensor(xs[:, 1, :], xs[:, 1, :], gb[n][:, 1, :], ALU.add).then_inc(ln[n]["x_pool"], 1)

            def split_wo(l, w, heads):
                pool.wait_ge(ld_wo, 16 * (l + 1))
                for h in heads:
                    chain(pool.tensor_copy(wo_hi(w, h), wo(ring, w, h)))
                    pool.tensor_tensor(wo(ring_r, w, h), wo(ring, w, h), wo_hi(w, h), ALU.subtract)\
                        .then_inc(w_pool_ready, 1)

            def windows(i, r, buf, ready):
                for j in range(2):
                    a = pool.value_load(offs[0:1, bass.ds(r * EXPERTS + i * 2 + j, 1)], min_val=0, max_val=NSLOT)
                    last = pool.tensor_copy(xg[:, buf, :, j * WIN:(j + 1) * WIN], xsT[:, :, bass.ds(a, WIN)])
                    last.then_inc(ready, 1)

            def moe(l):
                m = mo[l]
                pool.wait_ge(*ln[2 * l]("x_dve", 1))
                pool.iota(iota, pattern=[[1, NSLOT]], base=0, channel_multiplier=0,
                          allow_small_or_imprecise_dtypes=True).then_inc(m["iota_ready"], 1)
                pool.memset(xsT[:, :, NSLOT:], 0.0).then_inc(m["pad_zero"], 1)
                pool.wait_ge(*ln[2 * l]("x_pool", 1))
                for n, (part, (t, k0, k1)) in enumerate(zip(hi_parts, hi_of)):
                    pool.wait_ge(*m("hi_ready", n + 1))
                    pool.tensor_tensor(xs_lo[:, t, k0:k1, :], xs_tiles(t, k0, k1), part, ALU.subtract)\
                        .then_inc(m["lo_ready"], 1)
                pool.wait_ge(*m("key_ready", 1))
                kg = small[:, 0:8].rearrange("p (q t) -> p q t", q=4)
                for t in range(TT):
                    for q in range(4):
                        pool.tensor_scalar(diag[:, t, q, :], ident, kg[:, q, t:t + 1], None, ALU.mult)\
                            .then_inc(m["diag_ready"], 1)
                pool.wait_ge(*m("offs_ready", 1))
                pool.wait_ge(*m("sort_act", 4))
                pool.wait_ge(*m("sort_dve", 4))
                pool.wait_ge(*m("pad_zero", 1))

                def pair(i, s):
                    pool.wait_ge(*m("gu_ps", i - 2))
                    windows(i, 0, s, m["xg_ready"])

                for i in (1, 2):
                    windows(i, 0, i, m["xg_ready"])
                pair(3, 0)
                for_pairs_4_up(pool, pair)
                with pool.If(overflows(pool, l)):
                    pool.wait_ge(*m("gu_ps", PAIRS))

                    def step(i, r, n):
                        pool.wait_ge(ov[l]["free"], n + 1)
                        windows(i, r, 0, ov[l]["xg"])

                    overflow_steps(pool, step)
                    pool.wait_ge(ov[l]["xg"], 2 * PAIRS * (ROUNDS - 1))

            pool.memset(qz[DH:P, :, 0, :], 0.0).then_inc(zeroed, 1)
            pool.memset(qz[0:DH, :, 1, :], 0.0).then_inc(zeroed, 1)
            pool.wait_ge(zeroed, 2)
            pool.wait_ge(qkv_ps, 12)
            split_wo(0, wo_a, range(3))
            for h in range(HEADS):
                pool.wait_ge(*at[0]("o_sb", h + 1))
                pool.tensor_tensor(o_sq[:, h, :], o_sb[:, h, :], o_sb[:, h, :], ALU.mult).then_inc(sq_ready, 1)
            pool.wait_ge(rs_ready, 1)
            rs = small[:, 32:48].rearrange("p (h q) -> p h q", h=HEADS)
            o4 = o_sb[:, 5:8, :].rearrange("p h (q d) -> p h q d", q=2)
            pool.tensor_tensor(o4, o4, rs[:, 5:8, :].unsqueeze(3).broadcast_to([P, 3, 2, P]), ALU.mult)\
                .then_inc(on_pool, 1)
            split_wo(0, wo_a, (3,))
            layer_norm(0)
            moe(0)
            pool.wait_ge(*mo[0]("xg_ready", 2 * PAIRS - 2))
            pool.memset(qrz[ROPE:P, 0::2, :], 0.0).then_inc(zeroed, 1)
            pool.wait_ge(zeroed, 3)
            pool.memset(qrz[0:ROPE, 1::2, :], 0.0).then_inc(zeroed, 1)
            pool.wait_ge(zeroed, 4)
            layer_norm(1)
            for n, (w, hi, lo) in enumerate(b_parts):
                pool.wait_ge(mq["w_hi"], n + 1)
                pool.tensor_tensor(lo, w, hi, ALU.subtract).then_inc(mq["w_lo"], 1)
            pool.wait_ge(mq["qr_raw"], 2)
            rotate(pool, chain, qr_rot[:, 1, :, :], qr_raw[:, 1, :, :], 1, rope_tmp2, HEADS)\
                .then_inc(mq["qr_rot_pool"], 1)
            pool.wait_ge(mq["b_ps"], 4)
            pool.wait_ge(*ln[1]("x_dve", 1))
            split_wo(1, wo_b, range(4))
            layer_norm(2)
            moe(1)
            cols = slice(0, LAST_SPLIT)
            pool.wait_ge(*ln[3]("norm", 1))
            pool.wait_ge(*ld_gb[3]("gb", 32))
            chain(pool.tensor_tensor(xs[:, 0, cols], xs[:, 0, cols], gb[3][:, 0, cols], ALU.mult))
            pool.tensor_tensor(xs[:, 0, cols], xs[:, 0, cols], gb[3][:, 1, cols], ALU.add).then_inc(ln[3]["x_pool"], 1)


INPUTS = ["x", "diff_w_qkv", "diff_lambda", "diff_subln_g", "diff_w_o", "mla_w_kv_a", "mla_kv_norm_g", "mla_w_kv_b",
          "mla_w_q_a", "mla_q_norm_g", "mla_w_q_b", "mla_w_o", "router_w", "router_b", "moe_w_gate", "moe_w_up",
          "moe_w_down", "ln_g", "ln_b"]


def kernel(**inputs):
    import concourse.bacc as bacc
    from concourse.bass_utils import run_bass_kernel_spmd

    nc = bacc.Bacc("TRN2", target_bir_lowering=False, num_devices=1)
    arrays = {"in_shape_constants": shape_constants()}
    for name in INPUTS:
        arrays[f"in_{name}"] = np.ascontiguousarray(inputs[name])
    args = [nc.dram_tensor(n, a.shape, mybir.dt.from_np(a.dtype), kind="ExternalInput").ap()
            for n, a in arrays.items()]
    args.append(nc.dram_tensor("out_x", (1, SEQ, D), F32, kind="ExternalOutput").ap())
    build(nc, *args)
    r = run_bass_kernel_spmd(nc, [arrays], core_ids=[0])
    return r.results[0]["out_x"]
```
